# Optimizing a Trainium2 kernel written in Bass

```python
import math
import jax, jax.numpy as jnp
from jax import lax
import numpy as np

D_MODEL = 2048
BATCH = 1
SEQ = 512
DEPTH = 1

SB_HEAD_DIM = 128
SB_HEADS = (D_MODEL // 2) // SB_HEAD_DIM
SB_WIDTH = SB_HEADS * SB_HEAD_DIM
SB_BLOCK = 128
GDN_HEAD_DIM = 128
GDN_HEADS = (D_MODEL // 2) // GDN_HEAD_DIM
GDN_WIDTH = GDN_HEADS * GDN_HEAD_DIM
GDN_CONV = 4
GDN_CHUNK = 64
MIX_WIDTH = SB_WIDTH + GDN_WIDTH
OFF_SB_Q = 0
OFF_SB_K = OFF_SB_Q + SB_WIDTH
OFF_SB_V = OFF_SB_K + SB_WIDTH
OFF_GDN_QKV = OFF_SB_V + SB_WIDTH
OFF_GDN_Z = OFF_GDN_QKV + 3 * GDN_WIDTH
OFF_GDN_A = OFF_GDN_Z + GDN_WIDTH
OFF_GDN_B = OFF_GDN_A + GDN_HEADS
IN_COLS = OFF_GDN_B + GDN_HEADS
N_GROUPS = 4
EXPERTS_PER_GROUP = 8
N_EXPERTS = N_GROUPS * EXPERTS_PER_GROUP
TOP_K = 2
D_EXPERT = D_MODEL // 4
MOE_BLOCK = 128
RMS_EPS = 1e-6

kernel_name = "hybrid_stickbreak_gdn_hmoe"

def rms_norm(x, w):
    xf = x.astype(jnp.float32)
    y = xf * lax.rsqrt(jnp.mean(xf * xf, axis=-1, keepdims=True) + RMS_EPS)
    return (y * w.astype(jnp.float32)).astype(x.dtype)

def l2_normalize(x):
    xf = x.astype(jnp.float32)
    return xf * lax.rsqrt(jnp.sum(xf * xf, axis=-1, keepdims=True) + RMS_EPS)

def stick_breaking_attention(q, k, v):
    b_, h_, s_, d = q.shape
    nq = s_ // SB_BLOCK
    qf, kf, vf = (t.astype(jnp.float32) for t in (q, k, v))
    q_blocks = qf.reshape(b_, h_, nq, SB_BLOCK, d).transpose(2, 0, 1, 3, 4)
    key_pos = jnp.arange(s_)
    scale = 1.0 / math.sqrt(d)

    def one_block(args):
        qb, i = args
        z = jnp.einsum('bhqd,bhkd->bhqk', qb, kf) * scale
        q_pos = i * SB_BLOCK + jnp.arange(SB_BLOCK)
        causal = key_pos[None, :] < q_pos[:, None]
        log_1mb = jnp.where(causal, jax.nn.log_sigmoid(-z), 0.0)
        after = lax.cumsum(log_1mb, axis=3, reverse=True) - log_1mb
        weights = jnp.where(causal, jnp.exp(jax.nn.log_sigmoid(z) + after), 0.0)
        return jnp.einsum('bhqk,bhkd->bhqd', weights, vf)

    out = lax.map(one_block, (q_blocks, jnp.arange(nq)))
    return out.transpose(1, 2, 0, 3, 4).reshape(b_, h_, s_, d).astype(q.dtype)

def causal_depthwise_conv(x, w):
    kw = w.shape[0]
    return lax.conv_general_dilated(
        x, w[:, None, :], window_strides=(1,), padding=((kw - 1, 0),),
        dimension_numbers=('NWC', 'WIO', 'NWC'), feature_group_count=x.shape[-1])

def chunk_gated_delta_rule(q, k, v, g, beta):
    b_, h_, s_, dk = q.shape
    dv = v.shape[-1]
    c = GDN_CHUNK
    nc = s_ // c
    q = q * (1.0 / math.sqrt(dk))
    q, k, v = (t.reshape(b_, h_, nc, c, t.shape[-1]) for t in (q, k, v))
    g = g.reshape(b_, h_, nc, c)
    beta = beta.reshape(b_, h_, nc, c)
    gc = jnp.cumsum(g, axis=-1)
    incl = jnp.tril(jnp.ones((c, c), dtype=bool))
    strict = jnp.tril(jnp.ones((c, c), dtype=bool), -1)
    diff = gc[..., :, None] - gc[..., None, :]
    decay = jnp.where(incl, jnp.exp(jnp.where(incl, diff, 0.0)), 0.0)
    k_beta = k * beta[..., None]
    v_beta = v * beta[..., None]
    lmat = jnp.where(strict, jnp.einsum('bhncd,bhnkd->bhnck', k_beta, k) * decay, 0.0)
    eye = jnp.eye(c, dtype=q.dtype)
    t_inv = lax.linalg.triangular_solve(lmat + eye, jnp.broadcast_to(eye, lmat.shape),
                                        left_side=True, lower=True)
    u = t_inv @ v_beta
    w = t_inv @ (k_beta * jnp.exp(gc)[..., None])
    attn_intra = jnp.einsum('bhncd,bhnkd->bhnck', q, k) * decay

    def step(state, xs):
        q_i, k_i, u_i, w_i, gc_i, attn_i = xs
        v_new = u_i - w_i @ state
        o = (q_i * jnp.exp(gc_i)[..., None]) @ state + attn_i @ v_new
        g_last = gc_i[..., -1]
        k_dec = k_i * jnp.exp(g_last[..., None] - gc_i)[..., None]
        state = state * jnp.exp(g_last)[..., None, None] + jnp.einsum('bhck,bhcv->bhkv', k_dec, v_new)
        return state, o

    xs = tuple(jnp.moveaxis(t, 2, 0) for t in (q, k, u, w, gc, attn_intra))
    state0 = jnp.zeros((b_, h_, dk, dv), q.dtype)
    _, o = lax.scan(step, state0, xs)
    return jnp.moveaxis(o, 0, 2).reshape(b_, h_, s_, dv)

def hybrid_mixer(h, w_in, q_norm_w, k_norm_w, conv_w, a_log, dt_bias, out_norm_w, w_o):
    b_, s_, _ = h.shape
    proj = h @ w_in

    def heads(t, n):
        return t.reshape(b_, s_, n, -1).transpose(0, 2, 1, 3)

    sb_q = rms_norm(heads(proj[..., OFF_SB_Q:OFF_SB_K], SB_HEADS), q_norm_w)
    sb_k = rms_norm(heads(proj[..., OFF_SB_K:OFF_SB_V], SB_HEADS), k_norm_w)
    sb_v = heads(proj[..., OFF_SB_V:OFF_GDN_QKV], SB_HEADS)
    o_sb = stick_breaking_attention(sb_q, sb_k, sb_v)
    o_sb = o_sb.transpose(0, 2, 1, 3).reshape(b_, s_, SB_WIDTH)

    qkv = jax.nn.silu(causal_depthwise_conv(proj[..., OFF_GDN_QKV:OFF_GDN_Z], conv_w))
    gq = l2_normalize(heads(qkv[..., :GDN_WIDTH], GDN_HEADS))
    gk = l2_normalize(heads(qkv[..., GDN_WIDTH:2 * GDN_WIDTH], GDN_HEADS))
    gv = heads(qkv[..., 2 * GDN_WIDTH:], GDN_HEADS).astype(jnp.float32)
    gz = proj[..., OFF_GDN_Z:OFF_GDN_A].reshape(b_, s_, GDN_HEADS, GDN_HEAD_DIM)
    ga = proj[..., OFF_GDN_A:OFF_GDN_B].astype(jnp.float32)
    gb = proj[..., OFF_GDN_B:IN_COLS].astype(jnp.float32)
    beta = jax.nn.sigmoid(gb).transpose(0, 2, 1)
    log_decay = -(jnp.exp(a_log.astype(jnp.float32))
                  * jax.nn.softplus(ga + dt_bias.astype(jnp.float32))).transpose(0, 2, 1)
    o_gdn = chunk_gated_delta_rule(gq, gk, gv, log_decay, beta)
    o_gdn = o_gdn.transpose(0, 2, 1, 3)
    o_gdn = rms_norm(o_gdn, out_norm_w) * jax.nn.silu(gz.astype(jnp.float32))
    o_gdn = o_gdn.reshape(b_, s_, GDN_WIDTH).astype(h.dtype)

    return jnp.concatenate([o_sb, o_gdn], axis=-1) @ w_o

def hierarchical_moe(h, w_group, b_group, w_expert, b_expert, w1, w3, w2):
    b_, s_, d_ = h.shape
    xt = h.reshape(-1, d_)
    n_tok = xt.shape[0]
    group_logits = (xt @ w_group + b_group).astype(jnp.float32)
    group_prob = jax.nn.softmax(group_logits, axis=-1)
    top_group = jnp.argmax(group_logits, axis=-1)
    group_gate = jnp.take_along_axis(group_prob, top_group[:, None], axis=1)
    expert_logits = (xt @ w_expert + b_expert).astype(jnp.float32).reshape(n_tok, N_GROUPS, EXPERTS_PER_GROUP)
    in_group = jnp.take_along_axis(expert_logits, top_group[:, None, None], axis=1)[:, 0]
    top_p, top_local = lax.top_k(jax.nn.softmax(in_group, axis=-1), TOP_K)
    gate = group_gate * top_p / jnp.sum(top_p, axis=-1, keepdims=True)
    expert_id = top_group[:, None] * EXPERTS_PER_GROUP + top_local

    n_assign = n_tok * TOP_K
    flat_e = expert_id.reshape(-1)
    flat_tok = jnp.repeat(jnp.arange(n_tok, dtype=jnp.int32), TOP_K)
    order = jnp.argsort(flat_e)
    sorted_e = flat_e[order]
    sorted_tok = flat_tok[order]
    sorted_gate = gate.reshape(-1)[order]
    counts = jnp.bincount(flat_e, length=N_EXPERTS)
    padded = ((counts + MOE_BLOCK - 1) // MOE_BLOCK) * MOE_BLOCK
    start = jnp.cumsum(counts) - counts
    padded_end = jnp.cumsum(padded)
    padded_start = padded_end - padded
    dest = padded_start[sorted_e] + jnp.arange(n_assign) - start[sorted_e]
    n_blocks = (n_assign + MOE_BLOCK - 1) // MOE_BLOCK + N_EXPERTS
    cap = n_blocks * MOE_BLOCK
    slot_tok = jnp.full((cap,), n_tok, dtype=jnp.int32).at[dest].set(sorted_tok)
    x_pad = jnp.concatenate([xt, jnp.zeros((1, d_), xt.dtype)], axis=0)
    x_slots = x_pad[slot_tok].reshape(n_blocks, MOE_BLOCK, d_)
    block_expert = jnp.minimum(
        jnp.searchsorted(padded_end, jnp.arange(n_blocks) * MOE_BLOCK, side='right'), N_EXPERTS - 1)

    def expert_block(args):
        xb, e = args
        hid = jax.nn.silu(xb @ w1[e]) * (xb @ w3[e])
        return hid @ w2[e]

    y_slots = lax.map(expert_block, (x_slots, block_expert)).reshape(cap, d_)
    y_assign = y_slots[dest] * sorted_gate[:, None].astype(y_slots.dtype)
    y = jnp.zeros((n_tok, d_), h.dtype).at[sorted_tok].add(y_assign.astype(h.dtype))
    return y.reshape(b_, s_, d_)

def setup_inputs(seed: int = 0) -> dict:
    key = jax.random.key(seed)
    ks = jax.random.split(key, 20)
    L = DEPTH
    f32 = jnp.float32

    def nrm(k, shape, fan_in):
        return jax.random.normal(k, shape, f32) * (fan_in ** -0.5)

    def gain(k, shape):
        return 1.0 + 0.02 * jax.random.normal(k, shape, f32)

    dt = jnp.exp(jax.random.uniform(ks[8], (L, GDN_HEADS), f32, math.log(1e-3), math.log(1e-1)))
    return {
        "x": jax.random.normal(ks[0], (BATCH, SEQ, D_MODEL), f32),
        "norm1_w": gain(ks[1], (L, D_MODEL)),
        "w_in": nrm(ks[2], (L, D_MODEL, IN_COLS), D_MODEL),
        "sb_q_norm_w": gain(ks[3], (L, SB_HEAD_DIM)),
        "sb_k_norm_w": gain(ks[4], (L, SB_HEAD_DIM)),
        "gdn_conv_w": nrm(ks[5], (L, GDN_CONV, 3 * GDN_WIDTH), GDN_CONV),
        "gdn_a_log": jnp.log(jax.random.uniform(ks[6], (L, GDN_HEADS), f32, 1.0, 16.0)),
        "gdn_dt_bias": dt + jnp.log(-jnp.expm1(-dt)),
        "gdn_out_norm_w": gain(ks[7], (L, GDN_HEAD_DIM)),
        "w_o": nrm(ks[9], (L, MIX_WIDTH, D_MODEL), MIX_WIDTH),
        "norm2_w": gain(ks[10], (L, D_MODEL)),
        "w_group": nrm(ks[11], (L, D_MODEL, N_GROUPS), D_MODEL),
        "b_group": 0.01 * jax.random.normal(ks[12], (L, N_GROUPS), f32),
        "w_expert": nrm(ks[13], (L, D_MODEL, N_EXPERTS), D_MODEL),
        "b_expert": 0.01 * jax.random.normal(ks[14], (L, N_EXPERTS), f32),
        "w1": nrm(ks[15], (L, N_EXPERTS, D_MODEL, D_EXPERT), D_MODEL),
        "w3": nrm(ks[16], (L, N_EXPERTS, D_MODEL, D_EXPERT), D_MODEL),
        "w2": nrm(ks[17], (L, N_EXPERTS, D_EXPERT, D_MODEL), D_EXPERT),
    }

def reference(x, norm1_w, w_in, sb_q_norm_w, sb_k_norm_w, gdn_conv_w, gdn_a_log, gdn_dt_bias,
              gdn_out_norm_w, w_o, norm2_w, w_group, b_group, w_expert, b_expert, w1, w3, w2):
    for l in range(DEPTH):
        h = rms_norm(x, norm1_w[l])
        x = x + hybrid_mixer(h, w_in[l], sb_q_norm_w[l], sb_k_norm_w[l], gdn_conv_w[l],
                             gdn_a_log[l], gdn_dt_bias[l], gdn_out_norm_w[l], w_o[l])
        h = rms_norm(x, norm2_w[l])
        x = x + hierarchical_moe(h, w_group[l], b_group[l], w_expert[l], b_expert[l],
                                 w1[l], w3[l], w2[l])
    return x


_drawn_inputs = setup_inputs


def setup_inputs(seed=0):
    import zlib

    import numpy as np

    out = dict(_drawn_inputs(seed))
    spreads = {}
    factors = {'sb_q_norm_w': 4.968,
     'sb_k_norm_w': 5.544,
     'gdn_out_norm_w': 3.202,
     'b_group': 7.047,
     'b_expert': 18.524,
     'norm2_w': 2.983}
    for name, (base, spread) in spreads.items():
        noise = np.random.default_rng([zlib.crc32(name.encode()), seed]).standard_normal(out[name].shape)
        drawn = base * np.exp(spread * noise) if base else spread * noise
        out[name] = __import__('jax').numpy.asarray(drawn.astype(out[name].dtype))
    for name, factor in factors.items():
        out[name] = (out[name] * factor).astype(out[name].dtype)
    return out
```

```python
from contextlib import ExitStack

import concourse.bass as bass
from concourse import mybir

F32 = mybir.dt.float32
F32R = mybir.dt.float32r
I32 = mybir.dt.int32
U32 = mybir.dt.uint32
ALU = mybir.AluOpType
ACT = mybir.ActivationFunctionType
AX = mybir.AxisListType

P = 128
T = 512
NT = T // P
D = 2048
KT = D // P
HEADS = 8
GRP = 512
N_GRP = 14
IN_COLS = N_GRP * GRP + 2 * HEADS
TILE_Q, TILE_K, TILE_V = 0, 8, 16
TILE_GQ, TILE_GK, TILE_GV, TILE_GZ = 24, 32, 40, 48
TAPS = 4
LEVELS = 7
KC = 4
RAW = 4
NG, NE = 4, 32
PER = NE // NG
FE = 512
BLKS = T // P
EXTRA = 2 * T // P - 1
N_ITEMS = NE + EXTRA + 1
PAD_CODE = BLKS * NE
EPS = 1e-6
AHEAD = 1
BIG = 4096.0
CH_PER_ITEM = 12
C_NORM1, C_NORM2, C_CONV = 0, KT, 2 * KT


class Core:
    pass


class Semaphores:

    def __init__(self, nc):
        self.nc, self.taken = nc, []

    def __enter__(self):
        return self

    def __call__(self, name):
        self.taken.append(self.nc.alloc_semaphore(name))
        return self.taken[-1]

    def __exit__(self, *error):
        if error[0] is None:
            self.nc.clear_and_free_semaphores(self.taken)
            self.nc.all_engine_barrier()


def shared(nc, ctx):
    s = Core()

    def sb(name, shape, dt=F32):
        return ctx.enter_context(nc.sbuf_tensor(name, shape, dt))

    s.ident = sb("ident", [P, P])
    s.ones = sb("ones", [P, P])
    s.slot = sb("slot", [P, P])
    s.tri = sb("tri", [P, P])
    s.tri_s = sb("tri_s", [P, P])
    s.ntri = sb("ntri", [P, P])
    s.nones = sb("nones", [P, P])
    s.unseen = sb("unseen", [P, P])
    s.par = sb("par", [P, P])
    s.wn = sb("wn", [P, 4])
    s.zeros = sb("zeros", [P, P])
    s.eps = sb("eps", [P, 1])
    s.one = sb("one", [P, 1])
    s.gates = sb("gates", [P, NT, 2 * HEADS])
    s.ps = ctx.enter_context(nc.psum_tensor("ps", [P, 8, 512], F32))
    return s


def setup_stage(nc, s, io, hT_hi, hT_lo):
    with ExitStack() as ctx:
        def sb(name, shape, dt=F32):
            return ctx.enter_context(nc.sbuf_tensor(name, shape, dt))

        sem = ctx.enter_context(Semaphores(nc))

        xs = sb("xs", [P, NT, D])
        sq = sb("sq", [P, D])
        ss = sb("ss", [P, NT])
        ms = sb("ms", [P, NT])
        rec = sb("rec", [P, NT])
        rstd = sb("rstd", [P, NT])
        prow = sb("prow", [P, P])
        wrow = sb("wrow", [3, P])
        x_in = [sem(f"x_in{t}") for t in range(NT)]
        par_in, memset_done, consts_done = sem("par_in"), sem("memset_done"), sem("consts_done")
        sumsq_done, ms_done, rec_done, rstd_done = sem("sumsq_done"), sem("ms_done"), sem("rec_done"), sem("rstd_done")
        xn_done, par_t, par_out = sem("xn_done"), sem("par_t"), sem("par_out")
        tp_done, hi_done, lo_done = sem("tp_done"), sem("hi_done"), sem("lo_done")
        block = ctx.enter_context(nc.Block())
        ps = s.ps

        @block.sync
        def _(sp):
            for t in range(NT):
                sp.dma_start(xs[:, t, :], io.x[t * P:(t + 1) * P, :]).then_inc(x_in[t], 16)
            sp.dma_start(prow[0:KT, :], io.norm1_w).then_inc(par_in, 16)
            sp.dma_start(prow[KT:2 * KT, :], io.norm2_w).then_inc(par_in, 16)
            sp.dma_start(prow[2 * KT:P, :], io.conv_w).then_inc(par_in, 16)
            sp.dma_start(wrow[0:1, :], io.q_norm_w).then_inc(par_in, 16)
            sp.dma_start(wrow[1:2, :], io.k_norm_w).then_inc(par_in, 16)
            sp.dma_start(wrow[2:3, :], io.out_norm_w).then_inc(par_in, 16)

        @block.gpsimd
        def _(pool):
            pool.memset(s.ones[:], 1.0).then_inc(memset_done, 1)
            pool.memset(s.nones[:], -1.0).then_inc(memset_done, 1)
            pool.memset(s.eps[:], EPS).then_inc(memset_done, 1)
            pool.memset(s.one[:], 1.0).then_inc(memset_done, 1)
            pool.memset(s.zeros[:], 0.0).then_inc(memset_done, 1)
            pool.wait_ge(memset_done, 5)
            for out, src, op, base, step, mult in (
                (s.tri, s.ones, ALU.is_ge, 0, 1, -1),
                (s.tri_s, s.ones, ALU.is_gt, 0, 1, -1),
                (s.ntri, s.nones, ALU.is_ge, 0, -1, 1),
                (s.ident, s.ones, ALU.is_equal, 0, 1, -1),
                (s.unseen, s.zeros, ALU.is_gt, 0, 1, -1),
            ):
                pool.affine_select(out=out[:], in_=src[:], compare_op=op, fill=-1e30 if src is s.zeros else 0.0,
                                   base=base,
                                   pattern=[[step, P]], channel_multiplier=mult).then_inc(consts_done, 1)

        @block.scalar
        def _(act):
            for t in range(NT):
                act.wait_ge(x_in[t], 16)
                if t:
                    act.wait_ge(sumsq_done, t)
                nc.scalar.activation(sq[:], xs[:, t, :], ACT.Square, accum_out=ss[:, t:t + 1]).then_inc(sumsq_done, 1)
            act.wait_ge(rec_done, 1)
            nc.scalar.activation(rstd[:], rec[:], ACT.Sqrt).then_inc(rstd_done, 1)
            act.wait_ge(par_out, 2)
            for k in range(KT):
                act.wait_ge(tp_done, k + 1)
                nc.scalar.activation(hT_hi[:, k, :], ps[:, 2 + k % 4, :], ACT.Copy,
                                     scale=s.par[:, C_NORM1 + k:C_NORM1 + k + 1]).then_inc(hi_done, 1)

        @block.vector
        def _(dve):
            dve.wait_ge(sumsq_done, NT)
            nc.vector.tensor_scalar(ms[:], ss[:], 1.0 / D, EPS, ALU.mult, ALU.add).then_inc(ms_done, 1)
            dve.wait_ge(ms_done, 1)
            nc.vector.reciprocal(rec[:], ms[:]).then_inc(rec_done, 1)
            dve.wait_ge(par_t, 2)
            nc.vector.tensor_copy(s.par[:], ps[:, 0, 0:P]).then_inc(par_out, 1)
            nc.vector.tensor_scalar(s.wn[:, 0:1], ps[:, 1, 0:1], P ** -0.5, None, ALU.mult)
            nc.vector.tensor_copy(s.wn[:, 1:3], ps[:, 1, 1:3]).then_inc(par_out, 1)
            dve.wait_ge(rstd_done, 1)
            for t in range(NT):
                nc.vector.tensor_scalar(xs[:, t, :], xs[:, t, :], rstd[:, t:t + 1], None,
                                        ALU.mult).then_inc(xn_done, 1)
            dve.wait_ge(par_out, 2)
            for k in range(KT):
                dve.wait_ge(hi_done, k + 1)
                nc.vector.scalar_tensor_tensor(
                    out=hT_lo[:, k, :], in0=ps[:, 2 + k % 4, :], scalar=s.par[:, C_NORM1 + k:C_NORM1 + k + 1],
                    in1=hT_hi[:, k, :].bitcast(F32), op0=ALU.mult, op1=ALU.subtract).then_inc(lo_done, 1)

        @block.tensor
        def _(pe):
            pe.wait_ge(par_in, 6 * 16)
            pe.wait_ge(consts_done, 4)
            nc.tensor.transpose(ps[:, 0, 0:P], prow[:], s.ident[:]).then_inc(par_t, 1)
            nc.tensor.transpose(ps[:, 1, 0:3], wrow[:], s.ident[0:3, 0:3]).then_inc(par_t, 1)
            pe.wait_ge(xn_done, NT)
            for k in range(KT):
                if k >= 4:
                    pe.wait_ge(lo_done, k - 3)
                for t in range(NT):
                    tp = nc.tensor.transpose(ps[:, 2 + k % 4, t * P:(t + 1) * P],
                                             xs[:, t, k * P:(k + 1) * P], s.ident[:])
                tp.then_inc(tp_done, 1)


def project_stage(nc, s, io, hT_hi, hT_lo):
    with ExitStack() as ctx:
        def sb(name, shape, dt=F32):
            return ctx.enter_context(nc.sbuf_tensor(name, shape, dt))

        sem = ctx.enter_context(Semaphores(nc))

        raw = sb("w_raw", [P, RAW, KC, GRP])
        hi = sb("w_hi", [P, 2, KC, GRP], F32R)
        lo = sb("w_lo", [P, 2, KC, GRP], F32R)
        stage = sb("p_stage", [P, 2, 4, T])
        ab_raw = sb("ab_raw", [P, KT, 2 * HEADS])
        ab_hi = sb("ab_hi", [P, KT, 2 * HEADS], F32R)
        ab_lo = sb("ab_lo", [P, KT, 2 * HEADS], F32R)
        raw_in = [sem(f"pw_in{n}") for n in range(RAW)]
        hi_done, lo_done, mm_done = sem("pw_hi"), sem("pw_lo"), sem("pw_mm")
        staged = sem("staged")
        stored = [sem(f"p_stored{n}") for n in range(2)]
        stage_free = [sem(f"stage_free{n}") for n in range(2)]
        ab_in, ab_split, ab_mm, ab_out = sem("ab_in"), sem("ab_split"), sem("ab_mm"), sem("ab_out")
        block = ctx.enter_context(nc.Block())
        ps = s.ps
        CH = KT // KC
        BODY = 2 * CH
        PAIRS = N_GRP // 2

        @block.sync
        def _(sp):
            def load(ch, pair, col):
                return sp.dma_start(raw[:, ch % RAW, :, :], io.w_in_v[:, ch % CH * KC:(ch % CH + 1) * KC,
                                                                      bass.ds(col, GRP)])
            for ch in range(BODY):
                if ch >= RAW:
                    sp.wait_ge(lo_done, ch - RAW + 1)
                load(ch, 0, ch // CH * GRP).then_inc(raw_in[ch % RAW], 16)
            sp.dma_start(ab_raw[:], io.w_in_v[:, :, N_GRP * GRP:IN_COLS]).then_inc(ab_in, 16)
            with sp.Fori(1, PAIRS) as pair:
                for ch in range(BODY):
                    sp.wait_ge(lo_done, pair * BODY + (ch - RAW + 1))
                    load(ch, pair, pair * (2 * GRP) + ch // CH * GRP).then_inc(raw_in[ch % RAW], 16)

        @block.scalar
        def _(act):
            def split(pair, first):
                for ch in range(BODY):
                    act.wait_ge(raw_in[ch % RAW], pair * 32 + 16 * (ch // RAW + 1))
                    if ch >= 2 or not first:
                        act.wait_ge(mm_done, pair * BODY + (ch - 1))
                    nc.scalar.activation(hi[:, ch % 2], raw[:, ch % RAW], ACT.Copy).then_inc(hi_done, 1)
                    if ch % CH == 1 and (ch // CH or not first):
                        copy_out(pair, ch // CH)

            def copy_out(pair, g):
                half = 1 - g
                act.wait_ge(mm_done, pair * BODY + CH * g)
                act.wait_ge(stage_free[half], pair - half + AHEAD)
                nc.scalar.copy(stage[:, half], ps[:, 4 * half:4 * half + 4, :]).then_inc(staged, 1)

            split(0, True)
            with act.Fori(1, PAIRS) as pair:
                split(pair, False)
            copy_out(PAIRS, 0)
            act.wait_ge(ab_in, 16)
            nc.scalar.activation(ab_hi[:], ab_raw[:], ACT.Copy).then_inc(ab_split, 1)

        @block.gpsimd
        def _(pool):
            for g in range(2):
                pool.sem_inc(stage_free[g], AHEAD)
            with pool.Fori(0, PAIRS) as pair:
                for g in range(2):
                    pool.wait_ge(staged, pair * 2 + (g + 1))
                    pool.dma_start(io.proj[bass.ds(pair * 8 + 4 * g, 4)].rearrange("f p t -> p f t"),
                                   stage[:, g]).then_inc(stored[g], 16)
                    pool.wait_ge(stored[g], pair * 16 + 16)
                    pool.sem_inc(stage_free[g], 1)

        @block.vector
        def _(dve):
            with dve.Fori(0, PAIRS) as pair:
                for ch in range(BODY):
                    dve.wait_ge(hi_done, pair * BODY + (ch + 1))
                    nc.vector.tensor_tensor(lo[:, ch % 2], raw[:, ch % RAW], hi[:, ch % 2].bitcast(F32),
                                            ALU.subtract).then_inc(lo_done, 1)
            dve.wait_ge(ab_split, 1)
            nc.vector.tensor_tensor(ab_lo[:], ab_raw[:], ab_hi[:].bitcast(F32), ALU.subtract).then_inc(ab_split, 1)
            dve.wait_ge(ab_mm, 1)
            nc.vector.tensor_copy(s.gates[:], ps[:, 0, 0:NT * 2 * HEADS].rearrange(
                "p (t c) -> p t c", t=NT)).then_inc(ab_out, 1)

        @block.tensor
        def _(pe):
            def products(pair, first):
                for ch in range(BODY):
                    g, c = ch // CH, ch % CH
                    if c == 0 and not first:
                        pe.wait_ge(staged, pair * 2 + (g - 1))
                    pe.wait_ge(lo_done, pair * BODY + (ch + 1))
                    for f in range(4):
                        out = ps[:, 4 * g + f, :]
                        for k in range(KC):
                            kt = c * KC + k
                            w = slice(f * P, (f + 1) * P)
                            nc.tensor.matmul(out, hi[:, ch % 2, k, w], hT_hi[:, kt, :], start=kt == 0, stop=False)
                            nc.tensor.matmul(out, hi[:, ch % 2, k, w], hT_lo[:, kt, :], start=False, stop=False)
                            mm = nc.tensor.matmul(out, lo[:, ch % 2, k, w], hT_hi[:, kt, :], start=False,
                                                  stop=kt == KT - 1)
                    mm.then_inc(mm_done, 1)

            products(0, True)
            with pe.Fori(1, PAIRS) as pair:
                products(pair, False)
            pe.wait_ge(ab_split, 2)
            pe.wait_ge(staged, N_GRP - 1)
            for t in range(NT):
                out = ps[:, 0, t * 2 * HEADS:(t + 1) * 2 * HEADS]
                for k in range(KT):
                    tok = slice(t * P, (t + 1) * P)
                    nc.tensor.matmul(out, hT_hi[:, k, tok], ab_hi[:, k, :], start=k == 0, stop=False)
                    nc.tensor.matmul(out, hT_lo[:, k, tok], ab_hi[:, k, :], start=False, stop=False)
                    mm = nc.tensor.matmul(out, hT_hi[:, k, tok], ab_lo[:, k, :], start=False, stop=k == KT - 1)
            mm.then_inc(ab_mm, 1)


def stick_stage(nc, s, io, mix_hi, mix_lo):
    with ExitStack() as ctx:
        def sb(name, shape, dt=F32):
            return [ctx.enter_context(nc.sbuf_tensor(f"{name}{u}", shape, dt)) for u in range(2)]

        sem1 = ctx.enter_context(Semaphores(nc))

        def sem(name):
            return [sem1(f"{name}{u}") for u in range(2)]

        qkv = sb("s_qkv", [P, 3, T])
        sq = sb("s_sq", [P, 2, T])
        lnr = sb("s_ln", [P, 2, T])
        rr = sb("s_r", [P, 2, T])
        qn, kn = sb("s_qn", [P, T]), sb("s_kn", [P, T])
        vtok = sb("s_vtok", [P, NT, P])
        lg = sb("s_lg", [P, NT, T])
        spl = sb("s_spl", [P, NT, T])
        wgt = sb("s_wgt", [P, NT, T])
        qkv_in, sq_done, ss_done, ln_done, r_done = (sem(n) for n in ("qkv_in", "sq_done", "ss_done", "sln_done", "sr_done"))
        vt_done, vtok_done, qk_done, z_done = (sem(n) for n in ("vt_done", "vtok_done", "qk_done", "z_done"))
        abs_done, e_done, l_done, sp_done = (sem(n) for n in ("abs_done", "e_done", "l_done", "sp_done"))
        cum_done, w_done, o_done = (sem(n) for n in ("cum_done", "w_done", "o_done"))
        mhi_done, mlo_done, relu_done = sem("mhi_done"), sem("mlo_done"), sem("relu_done")
        block = ctx.enter_context(nc.Block())
        ps = s.ps
        PAIRS = HEADS // 2
        DOWN = list(range(NT - 1, -1, -1))

        def live(kb):
            return slice(kb * P, T)

        @block.sync
        def _(sp):
            with sp.Fori(0, PAIRS) as i:
                for u in range(2):
                    sp.wait_ge(z_done[u], i * NT + AHEAD)
                    sp.dma_start(qkv[u][:], io.proj_qkv[:, :, bass.ds(i * 2 + u, 1), :].rearrange(
                        "p g e t -> p (g e) t")).then_inc(qkv_in[u], 16)

        @block.scalar
        def _(act):
            with act.Fori(0, PAIRS) as i:
                for u in range(2):
                    act.wait_ge(qkv_in[u], i * 16 + 16)
                    nc.scalar.activation(sq[u][:], qkv[u][:, 0:2, :], ACT.Square).then_inc(sq_done[u], 1)
                for u in range(2):
                    b = 4 * u
                    act.wait_ge(ss_done[u], i + 1)
                    nc.scalar.activation(lnr[u][:], ps[:, b + 1:b + 3, :], ACT.Ln, scale=1.0 / P,
                                         bias=s.eps[:]).then_inc(ln_done[u], 1)
                    act.wait_ge(ln_done[u], i + 1)
                    nc.scalar.activation(rr[u][:], lnr[u][:], ACT.Exp, scale=-0.5).then_inc(r_done[u], 1)
                for n, kb in enumerate(DOWN):
                    for u in range(2):
                        act.wait_ge(abs_done[u], i * NT + (n + 1))
                        nc.scalar.activation(lg[u][:, kb, live(kb)], lg[u][:, kb, live(kb)],
                                             ACT.Exp).then_inc(e_done[u], 1)
                    for u in range(2):
                        act.wait_ge(e_done[u], i * NT + (n + 1))
                        nc.scalar.activation(lg[u][:, kb, live(kb)], lg[u][:, kb, live(kb)], ACT.Ln,
                                             bias=s.one[:]).then_inc(l_done[u], 1)
                for n, kb in enumerate(DOWN):
                    for u in range(2):
                        act.wait_ge(cum_done[u], i * NT + (n + 1))
                        nc.scalar.activation(wgt[u][:, kb, live(kb)], ps[:, 4 * u + kb, live(kb)],
                                             ACT.Exp).then_inc(w_done[u], 1)
                for u in range(2):
                    act.wait_ge(o_done[u], i + 1)
                    nc.scalar.copy(mix_hi[:, bass.ds(i * 2 + u, 1), :].rearrange("p e t -> p (e t)"),
                                   ps[:, 4 * u + 3, :]).then_inc(mhi_done[u], 1)

        @block.vector
        def _(dve):
            for u in range(2):
                for ahead in (vtok_done[u], mlo_done[u]):
                    dve.sem_inc(ahead, AHEAD)
            with dve.Fori(0, PAIRS) as i:
                for u in range(2):
                    dve.wait_ge(vt_done[u], i + 1)
                    nc.vector.tensor_copy(vtok[u][:], ps[:, 4 * u, :].rearrange(
                        "p (b d) -> p b d", b=NT)).then_inc(vtok_done[u], 1)
                for u in range(2):
                    dve.wait_ge(r_done[u], i + 1)
                    for n, out in enumerate((qn[u], kn[u])):
                        nc.vector.scalar_tensor_tensor(out=out[:], in0=qkv[u][:, n, :], scalar=s.wn[:, n:n + 1],
                                                       in1=rr[u][:, n, :], op0=ALU.mult,
                                                       op1=ALU.mult).then_inc(qk_done[u], 1)
                for n, kb in enumerate(DOWN):
                    for u in range(2):
                        dve.wait_ge(z_done[u], i * NT + (n + 1 + AHEAD))
                        nc.vector.tensor_scalar(spl[u][:, kb, live(kb)], ps[:, 4 * u + kb, live(kb)], 0.0, None,
                                                ALU.max).then_inc(relu_done[u], 1)
                    for u in range(2):
                        dve.wait_ge(relu_done[u], i * NT + (n + 1))
                        nc.vector.scalar_tensor_tensor(out=lg[u][:, kb, live(kb)], in0=spl[u][:, kb, live(kb)],
                                                       scalar=-2.0, in1=ps[:, 4 * u + kb, live(kb)], op0=ALU.mult,
                                                       op1=ALU.add).then_inc(abs_done[u], 1)
                for n, kb in enumerate(DOWN):
                    for u in range(2):
                        dve.wait_ge(l_done[u], i * NT + (n + 1))
                        nc.vector.tensor_tensor(spl[u][:, kb, live(kb)], spl[u][:, kb, live(kb)],
                                                lg[u][:, kb, live(kb)], ALU.add).then_inc(sp_done[u], 1)
                for u in range(2):
                    dve.wait_ge(mhi_done[u], i + 1)
                    nc.vector.tensor_tensor(
                        mix_lo[:, bass.ds(i * 2 + u, 1), :].rearrange("p e t -> p (e t)"), ps[:, 4 * u + 3, :],
                        mix_hi[:, bass.ds(i * 2 + u, 1), :].rearrange("p e t -> p (e t)").bitcast(F32),
                        ALU.subtract).then_inc(mlo_done[u], 1)

        @block.tensor
        def _(pe):
            for u in range(2):
                pe.sem_inc(z_done[u], AHEAD)
            with pe.Fori(0, PAIRS) as i:
                for u in range(2):
                    b = 4 * u
                    pe.wait_ge(qkv_in[u], i * 16 + 16)
                    pe.wait_ge(vtok_done[u], i + AHEAD)
                    for n in range(NT):
                        tp = nc.tensor.transpose(ps[:, b, n * P:(n + 1) * P], qkv[u][:, 2, n * P:(n + 1) * P],
                                                 s.ident[:])
                    tp.then_inc(vt_done[u], 1)
                    pe.wait_ge(sq_done[u], i + 1)
                    for n in range(2):
                        mm = nc.tensor.matmul(ps[:, b + 1 + n, :], s.ones[:], sq[u][:, n, :], start=True, stop=True)
                    mm.then_inc(ss_done[u], 1)
                for u in range(2):
                    pe.wait_ge(mlo_done[u], i + AHEAD)
                    pe.wait_ge(vtok_done[u], i + 1 + AHEAD)
                    pe.wait_ge(qk_done[u], i * 2 + 2)
                    for kb in DOWN:
                        nc.tensor.matmul(ps[:, 4 * u + kb, live(kb)], kn[u][:, kb * P:(kb + 1) * P],
                                         qn[u][:, live(kb)], start=True, stop=False, skip_group_check=True)
                        nc.tensor.matmul(ps[:, 4 * u + kb, kb * P:(kb + 1) * P], s.ident[:], s.unseen[:], start=False,
                                         stop=False, skip_group_check=True).then_inc(z_done[u], 1)
                for n, kb in enumerate(DOWN):
                    for u in range(2):
                        pe.wait_ge(sp_done[u], i * NT + (n + 1))
                        out = ps[:, 4 * u + kb, :]
                        mm = nc.tensor.matmul(out[:, live(kb)], s.ntri[:], spl[u][:, kb, live(kb)], start=False,
                                              stop=kb == NT - 1, skip_group_check=True)
                        for later in range(kb + 1, NT):
                            mm = nc.tensor.matmul(out[:, live(later)], s.nones[:], spl[u][:, later, live(later)],
                                                  start=False, stop=later == NT - 1, skip_group_check=True)
                        mm.then_inc(cum_done[u], 1)
                for u in range(2):
                    pe.wait_ge(w_done[u], i * NT + NT)
                    out = ps[:, 4 * u + 3, :]
                    for kb in range(NT):
                        mm = nc.tensor.matmul(out[:, live(kb)], vtok[u][:, kb, :], wgt[u][:, kb, live(kb)],
                                              start=kb == 0, stop=kb == NT - 1, skip_group_check=True)
                    mm.then_inc(o_done[u], 1)


def delta_stage(nc, s, io, mix_hi, mix_lo, spare):
    with ExitStack() as ctx:
        def one(name, shape, dt=F32):
            return ctx.enter_context(nc.sbuf_tensor(name, shape, dt))

        def sb(name, shape, dt=F32):
            return [one(f"{name}{u}", shape, dt) for u in range(2)]

        sem1 = ctx.enter_context(Semaphores(nc))

        def sem(name):
            return [sem1(f"{name}{u}") for u in range(2)]

        g = one("g", [P, HEADS, NT])
        beta = one("beta", [P, HEADS, NT])
        gcc = one("gcc", [P, HEADS, NT])
        nbe = one("nbe", [P, HEADS, NT])
        kds = one("kds", [P, HEADS, NT])
        gt = [one(f"gt{n}", [P, HEADS, NT]) for n in range(4)]
        alog = one("alog", [P, HEADS])
        dtb = one("dtb", [P, HEADS])
        ea = one("ea", [P, HEADS])
        ji = one("ji", [P, 2, P], I32)
        jx = one("jx", [P, P], I32)
        jl = one("jl", [P, LEVELS, P], I32)
        lvl = one("lvl", [P, LEVELS, P])
        raw = sb("d_raw", [P, 3, TAPS - 1 + T])
        zin = sb("d_z", [P, T])
        cv = sb("d_cv", [P, 3, T])
        sq = sb("d_sq", [P, 2, T])
        qn, kn, qg = sb("d_qn", [P, T]), sb("d_kn", [P, T]), sb("d_qg", [P, T])
        row_g, row_b = sb("d_row_g", [P, NT, P]), sb("d_row_b", [P, NT, P])
        eg = sb("d_eg", [P, T])
        dt = sb("d_dt", [P, NT, P])
        at = sb("d_at", [P, NT, P])
        qk = sb("d_qk", [P, NT, P])
        X, Y = sb("d_X", [P, NT, P]), sb("d_Y", [P, NT, P])
        blk = [spare[:].rearrange("p t d -> p (t d)")[:, u * D * NT // 2:u * D * NT // 2 + LEVELS * NT * P].rearrange(
            "p (l c t) -> p l c t", l=LEVELS, c=NT) for u in range(2)]
        Pm = sb("d_P", [P, NT, P])
        kd, vb = sb("d_kd", [P, NT, P]), sb("d_vb", [P, NT, P])
        res, vnew, state = sb("d_res", [P, P]), sb("d_vnew", [P, P]), sb("d_state", [P, P])
        names = ("tiles_in", "conv1", "conv_done", "silu_done", "sq_done", "ss_done", "dln_done", "dr_done", "qkn_done",
                 "rows_done", "row_mm", "eg_done", "diff_done", "dt_done", "dtm_done", "dtb_done", "kk_done",
                 "at_done", "atm_done", "qk_done", "L_done", "X0", "Y0a", "Y0", "blk_done", "qg_done", "ktv_done",
                 "kd_done", "vb_done", "P_mm", "P_out", "XY_mm", "X_out", "Y_out", "ks_mm", "res_done", "vn_mm",
                 "vn_done", "su_mm", "state_done", "o_done", "osq_done", "oss_done", "oln_done", "or_done",
                 "on_done", "fin_done", "mh_done", "ml_done")
        m = {n: sem("d_" + n) for n in names}
        par_in, mset, gstep, gmm, lstep, zeroed = (sem1(n) for n in ("gpar_in", "gmset", "gstep", "gmm", "lstep", "zeroed"))
        block = ctx.enter_context(nc.Block())
        ps = s.ps
        PAIRS = HEADS // 2
        LV = range(1, LEVELS)
        QC, KD, VD = 0, 1, 2

        def chunks(ap):
            return ap.rearrange("p (c t) -> p c t", c=NT)

        def col(table, head, c):
            return table[:, bass.ds(head, 1), c:c + 1].rearrange("p h c -> p (h c)")

        @block.sync
        def _(sp):
            sp.dma_start(alog[:], io.a_log.broadcast_to([P, HEADS])).then_inc(par_in, 16)
            sp.dma_start(dtb[:], io.dt_bias.broadcast_to([P, HEADS])).then_inc(par_in, 16)
            sp.wait_ge(zeroed, 2)
            with sp.Fori(0, PAIRS) as i:
                for u in range(2):
                    sp.wait_ge(m["conv_done"][u], i * 3 + AHEAD)
                    sp.dma_start(raw[u][:, :, TAPS - 1:], io.proj_gdn[:, :, bass.ds(i * 2 + u, 1), :].rearrange(
                        "p g e t -> p (g e) t")).then_inc(m["tiles_in"][u], 16)
                    sp.wait_ge(m["ml_done"][u], i + AHEAD)
                    sp.dma_start(zin[u][:], io.proj_z[:, bass.ds(i * 2 + u, 1), :].rearrange(
                        "p e t -> p (e t)")).then_inc(m["tiles_in"][u], 16)

        @block.gpsimd
        def _(pool):
            pool.iota(ji[:, 0, :], [[1, P]], base=0, channel_multiplier=0).then_inc(mset, 1)
            pool.iota(ji[:, 1, :], [[0, P]], base=0, channel_multiplier=1).then_inc(mset, 1)
            for u in range(2):
                pool.memset(raw[u][:, :, 0:TAPS - 1], 0.0).then_inc(zeroed, 1)
            pool.wait_ge(gstep, 9)
            pool.wait_ge(lstep, 3)
            with pool.Fori(0, PAIRS) as i:
                for u in range(2):
                    head = i * 2 + u
                    pool.wait_ge(m["row_mm"][u], i + AHEAD)
                    for out, mat, tab in ((row_g[u], s.tri, g), (row_b[u], s.ident, beta)):
                        pool.tensor_tensor(out=out[:], in0=mat[:].unsqueeze(1).broadcast_to([P, NT, P]),
                                           in1=tab[:, bass.ds(head, 1), :].rearrange("p h c -> p (h c)").unsqueeze(
                                               2).broadcast_to([P, NT, P]), op=ALU.mult).then_inc(m["rows_done"][u], 1)
                for u in range(2):
                    pool.wait_ge(m["dt_done"][u], i + 1)
                    pool.tensor_tensor(out=dt[u][:], in0=dt[u][:], in1=s.tri[:].unsqueeze(1).broadcast_to([P, NT, P]),
                                       op=ALU.mult).then_inc(m["dtm_done"][u], 1)
                for u in range(2):
                    pool.wait_ge(m["at_done"][u], i + 1)
                    pool.tensor_tensor(out=at[u][:], in0=at[u][:], in1=s.tri_s[:].unsqueeze(1).broadcast_to([P, NT, P]),
                                       op=ALU.mult).then_inc(m["atm_done"][u], 1)
                for n, l in enumerate(range(LEVELS)):
                    for u in range(2):
                        pool.wait_ge(m["atm_done"][u], i + 1)
                        pool.tensor_tensor(out=blk[u][:, l], in0=at[u][:],
                                           in1=lvl[:, l, :].unsqueeze(1).broadcast_to([P, NT, P]),
                                           op=ALU.mult).then_inc(m["blk_done"][u], 1)
                        if l == 0:
                            pool.wait_ge(m["blk_done"][u], i * LEVELS + 1)
                            pool.tensor_tensor(out=Y[u][:], in0=s.ident[:].unsqueeze(1).broadcast_to([P, NT, P]),
                                               in1=blk[u][:, 0], op=ALU.subtract).then_inc(m["Y0"][u], 1)
                for u in range(2):
                    pool.wait_ge(m["eg_done"][u], i + 1)
                    pool.wait_ge(m["qkn_done"][u], i * 2 + 2)
                    pool.tensor_tensor(out=qg[u][:], in0=qn[u][:], in1=eg[u][:],
                                       op=ALU.mult).then_inc(m["qg_done"][u], 1)

        @block.scalar
        def _(act):
            act.wait_ge(par_in, 32)
            nc.scalar.activation(ea[:], alog[:], ACT.Exp).then_inc(gstep, 1)
            act.wait_ge(mset, 4)
            nc.scalar.activation(gt[2][:], gt[2][:], ACT.Exp).then_inc(gstep, 1)
            act.wait_ge(gstep, 2)
            nc.scalar.activation(gt[2][:], gt[2][:], ACT.Ln, bias=s.one[:]).then_inc(gstep, 1)
            act.wait_ge(gstep, 3)
            nc.scalar.activation(gt[3][:], s.gates[:, :, HEADS:].rearrange("p t h -> p h t"), ACT.Exp,
                                 scale=-1.0).then_inc(gstep, 1)
            act.wait_ge(gmm, 1)
            nc.scalar.activation(nbe[:], ps[:, 0, 0:HEADS * NT].rearrange("p (h c) -> p h c", h=HEADS),
                                 ACT.Exp).then_inc(gstep, 1)
            act.wait_ge(gstep, 8)
            nc.scalar.activation(kds[:], kds[:], ACT.Exp).then_inc(gstep, 1)
            with act.Fori(0, PAIRS) as i:
                for u in range(2):
                    for n in range(3):
                        act.wait_ge(m["conv_done"][u], i * 3 + (n + 1 + AHEAD))
                        nc.scalar.activation(cv[u][:, n, :], cv[u][:, n, :], ACT.Silu).then_inc(m["silu_done"][u], 1)
                for u in range(2):
                    act.wait_ge(m["tiles_in"][u], i * 32 + 32)
                    nc.scalar.activation(zin[u][:], zin[u][:], ACT.Silu).then_inc(m["silu_done"][u], 1)
                for u in range(2):
                    act.wait_ge(m["silu_done"][u], i * 4 + 2)
                    nc.scalar.activation(sq[u][:], cv[u][:, 0:2, :], ACT.Square).then_inc(m["sq_done"][u], 1)
                for u in range(2):
                    b = 4 * u
                    act.wait_ge(m["row_mm"][u], i + 1 + AHEAD)
                    nc.scalar.activation(eg[u][:], ps[:, b, :], ACT.Exp).then_inc(m["eg_done"][u], 1)
                    act.wait_ge(m["ss_done"][u], i + 1)
                    nc.scalar.activation(sq[u][:], ps[:, b + 2:b + 4, :], ACT.Ln, bias=s.eps[:]).then_inc(m["dln_done"][u], 1)
                    act.wait_ge(m["dln_done"][u], i + 1)
                    nc.scalar.activation(sq[u][:], sq[u][:], ACT.Exp, scale=-0.5).then_inc(m["dr_done"][u], 1)
                for u in range(2):
                    act.wait_ge(m["diff_done"][u], i * NT + NT)
                    nc.scalar.activation(dt[u][:], dt[u][:], ACT.Exp).then_inc(m["dt_done"][u], 1)
                for u in range(2):
                    head = i * 2 + u
                    act.wait_ge(m["ktv_done"][u], i + 1)
                    for c in range(NT):
                        nc.scalar.activation(kd[u][:, c, :], chunks(ps[:, 4 * u, :])[:, c, :], ACT.Copy,
                                             scale=col(kds, head, c)).then_inc(m["kd_done"][u], 1)
                    for c in range(NT):
                        nc.scalar.activation(vb[u][:, c, :], chunks(ps[:, 4 * u + 1, :])[:, c, :], ACT.Copy,
                                             scale=col(beta, head, c)).then_inc(m["vb_done"][u], 1)
                for n, l in enumerate(LV):
                    for u in range(2):
                        act.wait_ge(m["P_mm"][u], i * len(LV) + (n + 1))
                        nc.scalar.copy(Pm[u][:], chunks(ps[:, 4 * u + 2, :])).then_inc(m["P_out"][u], 1)
                for c in range(NT):
                    for u in range(2):
                        act.wait_ge(m["vn_mm"][u], i * NT + (c + 1))
                        nc.scalar.copy(vnew[u][:], ps[:, 4 * u + 1, 0:P]).then_inc(m["vn_done"][u], 1)
                for u in range(2):
                    act.wait_ge(m["o_done"][u], i * NT + NT)
                    nc.scalar.activation(sq[u][:, 0, :], ps[:, 4 * u + 3, :], ACT.Square).then_inc(m["osq_done"][u], 1)
                for u in range(2):
                    act.wait_ge(m["oss_done"][u], i + 1)
                    nc.scalar.activation(sq[u][:, 1, :], ps[:, 4 * u, :], ACT.Ln, scale=1.0 / P,
                                         bias=s.eps[:]).then_inc(m["oln_done"][u], 1)
                    act.wait_ge(m["oln_done"][u], i + 1)
                    nc.scalar.activation(sq[u][:, 1, :], sq[u][:, 1, :], ACT.Exp, scale=-0.5).then_inc(m["or_done"][u], 1)
                for u in range(2):
                    act.wait_ge(m["fin_done"][u], i + 1 + AHEAD)
                    nc.scalar.copy(mix_hi[:, bass.ds(i * 2 + (HEADS + u), 1), :].rearrange("p e t -> p (e t)"),
                                   zin[u][:]).then_inc(m["mh_done"][u], 1)

        @block.vector
        def _(dve):
            a_in = s.gates[:, :, 0:HEADS].rearrange("p t h -> p h t")
            dve.wait_ge(par_in, 32)
            nc.vector.tensor_tensor(gt[1][:], a_in, dtb[:].unsqueeze(2).broadcast_to([P, HEADS, NT]),
                                    ALU.add).then_inc(lstep, 1)
            dve.wait_ge(lstep, 1)
            dve.wait_ge(mset, 2)
            nc.vector.tensor_scalar(gt[0][:], gt[1][:], 0.0, None, ALU.max).then_inc(mset, 1)
            dve.wait_ge(mset, 3)
            nc.vector.scalar_tensor_tensor(out=gt[2][:], in0=gt[0][:], scalar=-2.0, in1=gt[1][:], op0=ALU.mult,
                                           op1=ALU.add).then_inc(mset, 1)
            nc.vector.tensor_tensor(jx[:], ji[:, 0, :], ji[:, 1, :], ALU.bitwise_xor).then_inc(lstep, 1)
            dve.wait_ge(gstep, 4)
            nc.vector.tensor_tensor(gt[0][:], gt[0][:], gt[2][:], ALU.add).then_inc(mset, 1)
            nc.vector.tensor_scalar(gt[3][:], gt[3][:], 1.0, None, ALU.add).then_inc(mset, 1)
            dve.wait_ge(mset, 6)
            nc.vector.scalar_tensor_tensor(out=g[:], in0=gt[0][:], scalar=-1.0,
                                           in1=ea[:].unsqueeze(2).broadcast_to([P, HEADS, NT]), op0=ALU.mult,
                                           op1=ALU.mult).then_inc(gstep, 1)
            nc.vector.reciprocal(beta[:], gt[3][:]).then_inc(gstep, 1)
            dve.wait_ge(gmm, 1)
            dve.wait_ge(gstep, 7)
            nc.vector.tensor_copy(gcc[:], ps[:, 0, 0:HEADS * NT].rearrange("p (h c) -> p h c", h=HEADS)).then_inc(mset, 1)
            dve.wait_ge(mset, 7)
            nc.vector.tensor_tensor(kds[:], ps[:, 1, 0:HEADS * NT].rearrange("p (h c) -> p h c", h=HEADS), gcc[:],
                                    ALU.subtract)
            nc.vector.scalar_tensor_tensor(out=nbe[:], in0=nbe[:], scalar=-1.0, in1=beta[:], op0=ALU.mult,
                                           op1=ALU.mult).then_inc(gstep, 1)
            dve.wait_ge(lstep, 2)
            for l in range(LEVELS):
                nc.vector.tensor_single_scalar(jl[:, l, :], jx[:], l, ALU.logical_shift_right).then_inc(mset, 1)
            dve.wait_ge(mset, 7 + LEVELS)
            nc.vector.tensor_scalar(lvl[:], jl[:], 1.0, None, ALU.is_equal).then_inc(lstep, 1)
            dve.wait_ge(lstep, 3)
            for u in range(2):
                for ahead in ("conv_done", "fin_done", "ml_done"):
                    dve.sem_inc(m[ahead][u], AHEAD)
            with dve.Fori(0, PAIRS) as i:
                for u in range(2):
                    head = i * 2 + u
                    dve.wait_ge(m["tiles_in"][u], i * 32 + 32)
                    for k in range(TAPS):
                        for n in range(3):
                            tap = s.par[:, bass.ds(head + (C_CONV + 3 * HEADS * k + HEADS * n), 1)]
                            src = raw[u][:, n, k:k + T]
                            out = cv[u][:, n, :]
                            if k == 0:
                                nc.vector.tensor_scalar(out, src, tap, None, ALU.mult).then_inc(m["conv1"][u], 1)
                            else:
                                dve.wait_ge(m["conv1"][u], i * 9 + (3 * (k - 1) + n + 1))
                                nc.vector.scalar_tensor_tensor(
                                    out=out, in0=src, scalar=tap, in1=out, op0=ALU.mult, op1=ALU.add).then_inc(
                                        m["conv_done" if k == TAPS - 1 else "conv1"][u], 1)
                for u in range(2):
                    head = i * 2 + u
                    dve.wait_ge(m["row_mm"][u], i + 1 + AHEAD)
                    dve.wait_ge(m["eg_done"][u], i + 1)
                    for c in range(NT):
                        nc.vector.tensor_scalar(dt[u][:, c, :], chunks(ps[:, 4 * u, :])[:, c, :], col(gcc, head, c),
                                                0.0, ALU.subtract, ALU.min).then_inc(m["diff_done"][u], 1)
                for u in range(2):
                    dve.wait_ge(m["dr_done"][u], i + 1)
                    nc.vector.scalar_tensor_tensor(out=qn[u][:], in0=cv[u][:, 0, :], scalar=P ** -0.5,
                                                   in1=sq[u][:, 0, :], op0=ALU.mult,
                                                   op1=ALU.mult).then_inc(m["qkn_done"][u], 1)
                    nc.vector.tensor_tensor(kn[u][:], cv[u][:, 1, :], sq[u][:, 1, :],
                                            ALU.mult).then_inc(m["qkn_done"][u], 1)
                for u in range(2):
                    b = 4 * u
                    dve.wait_ge(m["dtm_done"][u], i + 1)
                    dve.wait_ge(m["row_mm"][u], i + 1 + AHEAD)
                    nc.vector.tensor_tensor(at[u][:], dt[u][:], chunks(ps[:, b + 1, :]), ALU.mult).then_inc(m["dtb_done"][u], 1)
                    dve.wait_ge(m["kk_done"][u], i + 1)
                    dve.wait_ge(m["dtb_done"][u], i + 1)
                    nc.vector.tensor_tensor(at[u][:], at[u][:], chunks(ps[:, b + 2, :]), ALU.mult).then_inc(m["at_done"][u], 1)
                    nc.vector.tensor_tensor(qk[u][:], dt[u][:], chunks(ps[:, b + 3, :]), ALU.mult).then_inc(m["qk_done"][u], 1)
                for u in range(2):
                    dve.wait_ge(m["L_done"][u], i + 1)
                    nc.vector.scalar_tensor_tensor(out=X[u][:], in0=chunks(ps[:, 4 * u + 2, :]), scalar=-1.0,
                                                   in1=lvl[:, 0, :].unsqueeze(1).broadcast_to([P, NT, P]),
                                                   op0=ALU.mult, op1=ALU.mult).then_inc(m["X0"][u], 1)
                for u in range(2):
                    dve.wait_ge(m["X0"][u], i * 2 + 1)
                    nc.vector.tensor_tensor(X[u][:], X[u][:], s.ident[:].unsqueeze(1).broadcast_to([P, NT, P]),
                                            ALU.add).then_inc(m["X0"][u], 1)
                for n, l in enumerate(LV):
                    for u in range(2):
                        b = 4 * u
                        dve.wait_ge(m["XY_mm"][u], i * len(LV) + (n + 1))
                        if l < LEVELS - 1:
                            nc.vector.tensor_tensor(X[u][:], X[u][:], chunks(ps[:, b + 3, :]),
                                                    ALU.subtract).then_inc(m["X_out"][u], 1)
                        nc.vector.tensor_tensor(Y[u][:], Y[u][:], chunks(ps[:, b + 2, :]),
                                                ALU.subtract).then_inc(m["Y_out"][u], 1)
                for c in range(NT):
                    for u in range(2):
                        head = i * 2 + u
                        if c:
                            dve.wait_ge(m["ks_mm"][u], i * (NT - 1) + c)
                            dve.wait_ge(m["vb_done"][u], i * NT + NT)
                            nc.vector.scalar_tensor_tensor(out=res[u][:], in0=ps[:, 4 * u, 0:P], scalar=col(nbe, head, c),
                                                           in1=vb[u][:, c, :], op0=ALU.mult,
                                                           op1=ALU.add).then_inc(m["res_done"][u], 1)
                    for u in range(2):
                        if c < NT - 1:
                            dve.wait_ge(m["su_mm"][u], i * (NT - 1) + (c + 1))
                            if c == 0:
                                nc.vector.tensor_copy(state[u][:], ps[:, 4 * u + 2, 0:P]).then_inc(m["state_done"][u], 1)
                            else:
                                dve.wait_ge(m["state_done"][u], i * (NT - 1) + c)
                                last = (c + 1) * P - 1
                                nc.vector.scalar_tensor_tensor(out=state[u][:], in0=state[u][:],
                                                               scalar=eg[u][:, last:last + 1],
                                                               in1=ps[:, 4 * u + 2, 0:P], op0=ALU.mult,
                                                               op1=ALU.add).then_inc(m["state_done"][u], 1)
                for u in range(2):
                    dve.wait_ge(m["or_done"][u], i + 1)
                    nc.vector.scalar_tensor_tensor(out=sq[u][:, 0, :], in0=ps[:, 4 * u + 3, :], scalar=s.wn[:, 2:3],
                                                   in1=sq[u][:, 1, :], op0=ALU.mult, op1=ALU.mult).then_inc(m["on_done"][u], 1)
                for u in range(2):
                    dve.wait_ge(m["on_done"][u], i + 1)
                    nc.vector.tensor_tensor(zin[u][:], sq[u][:, 0, :], zin[u][:], ALU.mult).then_inc(m["fin_done"][u], 1)
                for u in range(2):
                    at_ = bass.ds(i * 2 + (HEADS + u), 1)
                    dve.wait_ge(m["mh_done"][u], i + 1)
                    nc.vector.tensor_tensor(mix_lo[:, at_, :].rearrange("p e t -> p (e t)"), zin[u][:],
                                            mix_hi[:, at_, :].rearrange("p e t -> p (e t)").bitcast(F32),
                                            ALU.subtract).then_inc(m["ml_done"][u], 1)

        @block.tensor
        def _(pe):
            pe.wait_ge(gstep, 6)
            nc.tensor.matmul(ps[:, 0, 0:HEADS * NT], s.tri[:], g[:].rearrange("p h c -> p (h c)"), start=True, stop=True)
            nc.tensor.matmul(ps[:, 1, 0:HEADS * NT], s.ones[:], g[:].rearrange("p h c -> p (h c)"), start=True,
                             stop=True).then_inc(gmm, 1)
            pe.wait_ge(gstep, 8)

            def cols(c):
                return slice(c * P, (c + 1) * P)

            for u in range(2):
                pe.sem_inc(m["row_mm"][u], AHEAD)
            with pe.Fori(0, PAIRS) as i:
                for u in range(2):
                    b = 4 * u
                    pe.wait_ge(m["fin_done"][u], i + AHEAD)
                    pe.wait_ge(m["rows_done"][u], i * 2 + 2)
                    nc.tensor.matmul(ps[:, b, :], s.ones[:], row_g[u][:].rearrange("p c t -> p (c t)"), start=True, stop=True)
                    nc.tensor.matmul(ps[:, b + 1, :], s.ones[:], row_b[u][:].rearrange("p c t -> p (c t)"), start=True,
                                     stop=True).then_inc(m["row_mm"][u], 1)
                for u in range(2):
                    pe.wait_ge(m["sq_done"][u], i + 1)
                    for n in range(2):
                        mm = nc.tensor.matmul(ps[:, 4 * u + 2 + n, :], s.ones[:], sq[u][:, n, :], start=True, stop=True)
                    mm.then_inc(m["ss_done"][u], 1)
                for u in range(2):
                    b = 4 * u
                    pe.wait_ge(m["qkn_done"][u], i * 2 + 2)
                    for c in range(NT):
                        nc.tensor.matmul(ps[:, b + 2, cols(c)], kn[u][:, cols(c)], kn[u][:, cols(c)], start=True, stop=True)
                        mm = nc.tensor.matmul(ps[:, b + 3, cols(c)], kn[u][:, cols(c)], qn[u][:, cols(c)], start=True, stop=True)
                    mm.then_inc(m["kk_done"][u], 1)
                for u in range(2):
                    b = 4 * u
                    pe.wait_ge(m["diff_done"][u], i * NT + NT)
                    for c in range(NT):
                        nc.tensor.transpose(ps[:, b, cols(c)], kn[u][:, cols(c)], s.ident[:])
                    pe.wait_ge(m["dtb_done"][u], i + 1)
                    pe.wait_ge(m["silu_done"][u], i * 4 + 4)
                    for c in range(NT):
                        tp = nc.tensor.transpose(ps[:, b + 1, cols(c)], cv[u][:, 2, cols(c)], s.ident[:])
                    tp.then_inc(m["ktv_done"][u], 1)
                for u in range(2):
                    pe.wait_ge(m["atm_done"][u], i + 1)
                    for c in range(NT):
                        tp = nc.tensor.transpose(ps[:, 4 * u + 2, cols(c)], at[u][:, c, :], s.ident[:])
                    tp.then_inc(m["L_done"][u], 1)
                for n, l in enumerate(LV):
                    for u in range(2):
                        if n == 0:
                            pe.wait_ge(m["X0"][u], i * 2 + 2)
                            pe.wait_ge(m["Y0"][u], i + 1)
                            pe.wait_ge(m["qk_done"][u], i + 1)
                        else:
                            pe.wait_ge(m["X_out"][u], i * (len(LV) - 1) + n)
                            pe.wait_ge(m["Y_out"][u], i * len(LV) + n)
                        pe.wait_ge(m["blk_done"][u], i * LEVELS + (l + 1))
                        for c in range(NT):
                            mm = nc.tensor.matmul(ps[:, 4 * u + 2, cols(c)], blk[u][:, l, c, :], X[u][:, c, :], start=True, stop=True)
                        mm.then_inc(m["P_mm"][u], 1)
                    for u in range(2):
                        pe.wait_ge(m["P_out"][u], i * len(LV) + (n + 1))
                        for c in range(NT):
                            if l < LEVELS - 1:
                                nc.tensor.matmul(ps[:, 4 * u + 3, cols(c)], Y[u][:, c, :], Pm[u][:, c, :], start=True, stop=True)
                            mm = nc.tensor.matmul(ps[:, 4 * u + 2, cols(c)], Pm[u][:, c, :], Y[u][:, c, :], start=True, stop=True)
                        mm.then_inc(m["XY_mm"][u], 1)
                for c in range(NT):
                    if c:
                        for u in range(2):
                            pe.wait_ge(m["state_done"][u], i * (NT - 1) + c)
                            pe.wait_ge(m["kd_done"][u], i * NT + NT)
                            nc.tensor.matmul(ps[:, 4 * u, 0:P], kn[u][:, cols(c)], state[u][:], start=True,
                                             stop=True).then_inc(m["ks_mm"][u], 1)
                    for u in range(2):
                        if c == 0:
                            pe.wait_ge(m["Y_out"][u], i * len(LV) + len(LV))
                            pe.wait_ge(m["vb_done"][u], i * NT + NT)
                            right = vb[u][:, 0, :]
                        else:
                            pe.wait_ge(m["res_done"][u], i * (NT - 1) + c)
                            right = res[u][:]
                        nc.tensor.matmul(ps[:, 4 * u + 1, 0:P], Y[u][:, c, :], right, start=True, stop=True).then_inc(m["vn_mm"][u], 1)
                    for u in range(2):
                        pe.wait_ge(m["vn_done"][u], i * NT + (c + 1))
                        out = ps[:, 4 * u + 3, cols(c)]
                        mm = nc.tensor.matmul(out, vnew[u][:], qk[u][:, c, :], start=True, stop=c == 0)
                        if c:
                            pe.wait_ge(m["qg_done"][u], i + 1)
                            mm = nc.tensor.matmul(out, state[u][:], qg[u][:, cols(c)], start=False, stop=True)
                        mm.then_inc(m["o_done"][u], 1)
                        if c < NT - 1:
                            pe.wait_ge(m["kd_done"][u], i * NT + NT)
                            nc.tensor.matmul(ps[:, 4 * u + 2, 0:P], kd[u][:, c, :], vnew[u][:], start=True,
                                             stop=True).then_inc(m["su_mm"][u], 1)
                for u in range(2):
                    pe.wait_ge(m["osq_done"][u], i + 1)
                    nc.tensor.matmul(ps[:, 4 * u, :], s.ones[:], sq[u][:, 0, :], start=True, stop=True).then_inc(m["oss_done"][u], 1)


def out_proj_stage(nc, s, io, mix_hi, mix_lo, x2):
    with ExitStack() as ctx:
        def sb(name, shape, dt=F32):
            return ctx.enter_context(nc.sbuf_tensor(name, shape, dt))

        sem = ctx.enter_context(Semaphores(nc))
        raw = sb("o_raw", [P, RAW, KC, GRP])
        hi = sb("o_hi", [P, 2, KC, GRP], F32R)
        lo = sb("o_lo", [P, 2, KC, GRP], F32R)
        x_in = sem("ox_in")
        raw_in = [sem(f"ow_in{n}") for n in range(RAW)]
        hi_done = sem("ow_hi")
        lo_done = [sem(f"ow_lo{n}") for n in range(RAW)]
        mm_done = [sem(f"ow_mm{n}") for n in range(2)]
        added = [sem(f"o_added{n}") for n in range(2)]
        block = ctx.enter_context(nc.Block())
        ps = s.ps
        CH = KT // KC
        BODY = 2 * CH
        PAIRS = D // GRP // 2

        @block.sync
        def _(sp):
            sp.dma_start(x2[:], io.x.rearrange("(t p) d -> p t d", p=P)).then_inc(x_in, 16)
            with sp.Fori(0, PAIRS) as pair:
                for ch in range(BODY):
                    sp.wait_ge(lo_done[ch % RAW], pair * (BODY // RAW) + (ch // RAW + AHEAD))
                    sp.dma_start(raw[:, ch % RAW], io.w_o_v[:, ch % CH * KC:(ch % CH + 1) * KC, bass.ds(
                        pair * (2 * GRP) + ch // CH * GRP, GRP)]).then_inc(raw_in[ch % RAW], 16)

        @block.scalar
        def _(act):
            with act.Fori(0, PAIRS) as pair:
                for ch in range(BODY):
                    act.wait_ge(raw_in[ch % RAW], pair * (16 * BODY // RAW) + 16 * (ch // RAW + 1))
                    act.wait_ge(mm_done[ch % 2], pair * (BODY // 2) + (ch // 2 + AHEAD))
                    nc.scalar.copy(hi[:, ch % 2], raw[:, ch % RAW]).then_inc(hi_done, 1)

        @block.vector
        def _(dve):
            for ahead in (*lo_done, *added):
                dve.sem_inc(ahead, AHEAD)
            with dve.Fori(0, PAIRS) as pair:
                for ch in range(BODY):
                    dve.wait_ge(hi_done, pair * BODY + (ch + 1))
                    nc.vector.tensor_tensor(lo[:, ch % 2], raw[:, ch % RAW], hi[:, ch % 2].bitcast(F32),
                                            ALU.subtract).then_inc(lo_done[ch % RAW], 1)
                for g in range(2):
                    dve.wait_ge(mm_done[1], pair * (BODY // 2) + ((g + 1) * CH // 2 + AHEAD))
                    if g == 0:
                        dve.wait_ge(x_in, 16)
                    at = x2[:, :, bass.ds(pair * (2 * GRP) + g * GRP, GRP)]
                    nc.vector.tensor_tensor(at, ps[:, 4 * g:4 * g + 4, :], at, ALU.add).then_inc(added[g], 1)

        @block.tensor
        def _(pe):
            for ahead in mm_done:
                pe.sem_inc(ahead, AHEAD)
            with pe.Fori(0, PAIRS) as pair:
                for ch in range(BODY):
                    g, c = ch // CH, ch % CH
                    if c == 0:
                        pe.wait_ge(added[g], pair + AHEAD)
                    pe.wait_ge(lo_done[ch % RAW], pair * (BODY // RAW) + (ch // RAW + 1 + AHEAD))
                    for t in range(NT):
                        out, tok = ps[:, 4 * g + t, :], slice(t * P, (t + 1) * P)
                        for k in range(KC):
                            kt = c * KC + k
                            nc.tensor.matmul(out, mix_hi[:, kt, tok], hi[:, ch % 2, k], start=kt == 0, stop=False)
                            nc.tensor.matmul(out, mix_lo[:, kt, tok], hi[:, ch % 2, k], start=False, stop=False)
                            mm = nc.tensor.matmul(out, mix_hi[:, kt, tok], lo[:, ch % 2, k], start=False,
                                                  stop=kt == KT - 1)
                    mm.then_inc(mm_done[ch % 2], 1)


def route_stage(nc, s, io, x2, tab_pos, tab_val, items):
    NL = NG + NE
    with ExitStack() as ctx:
        def sb(name, shape, dt=F32):
            return ctx.enter_context(nc.sbuf_tensor(name, shape, dt))

        sem = ctx.enter_context(Semaphores(nc))
        xn = sb("xn", [P, NT, D])
        h2T = sb("h2T", [P, KT, T])
        wr = sb("wr", [P, KT, NL])
        bias = sb("bias", [P, NL])
        sq = sb("r_sq", [P, D])
        st = [sb(f"r_st{n}", [P, NT]) for n in range(4)]
        lg = sb("r_lg", [P, NT, NL])
        gmx, gsum, gg = sb("gmx", [P, NT]), sb("gsum", [P, NT]), sb("gg", [P, NT])
        gd, gsc, goh = sb("gd", [P, NT, NG]), sb("gsc", [P, NT, NG]), sb("goh", [P, NT, NG])
        picked = sb("picked", [P, NT, NG, PER])
        inl = sb("inl", [P, NT, PER])
        ex = [sb(f"r_ex{n}", [P, NT, PER]) for n in range(2)]
        esc = sb("esc", [P, NT, PER])
        eoh = [sb(f"eoh{n}", [P, NT, PER]) for n in range(2)]
        emx = [sb(f"emx{n}", [P, NT]) for n in range(2)]
        smx = sb("smx", [P, NT])
        gate = [sb(f"gate{n}", [P, NT]) for n in range(2)]
        den = sb("den", [P, NT])
        M = [sb(f"M{n}", [P, NT, NE]) for n in range(3)]
        gm = [sb(f"gm{n}", [P, NT, NE]) for n in range(2)]
        posm = sb("posm", [P, NT, NE])
        desc = sb("desc", [P, PER])
        tok = sb("tok", [P, NT])
        cnt = sb("cnt", [P, NE])
        NX = (BLKS - 1) * NE
        xcode, xexp = sb("xcode", [1, NX]), sb("xexp", [1, NX])
        kk, two = sb("kk", [1, EXTRA + 1]), sb("two", [1, NG])
        flag, rank, onesr = sb("flag", [1, NX]), sb("rank", [1, NX]), sb("onesr", [1, NX])
        fc = sb("fc", [1, 2, NX])
        hit = sb("hit", [1, EXTRA + 1, NX])
        hv = sb("hv", [1, EXTRA + 1, NX])
        xt = sb("xt", [1, 2, EXTRA + 1])
        np_ = sb("np_", [1, NG])
        npair = sb("npair", [1, 1])
        itf = sb("itf", [1, 2, N_ITEMS + 2])

        w_in, init = sem("rw_in"), sem("r_init")
        ssq, msd, recd, rstdd, xnd, stored = (sem(n) for n in ("r_ssq", "r_ms", "r_rec", "r_rstd", "r_xn", "r_stored"))
        tpd, h2d, lgm, act_exp, chain = (sem(n) for n in ("r_tp", "r_h2", "r_lgm", "r_exp", "r_chain"))
        m_done, pos_mm = sem("m_done"), sem("pos_mm")
        block = ctx.enter_context(nc.Block())
        ps = s.ps

        @block.sync
        def _(sp):
            sp.dma_start(wr[:, :, 0:NG], io.w_group.rearrange("(k p) n -> p k n", p=P)).then_inc(w_in, 16)
            sp.dma_start(wr[:, :, NG:NL], io.w_expert.rearrange("(k p) n -> p k n", p=P)).then_inc(w_in, 16)
            sp.dma_start(bias[:, 0:NG], io.b_group.broadcast_to([P, NG])).then_inc(w_in, 16)
            sp.dma_start(bias[:, NG:NL], io.b_expert.broadcast_to([P, NE])).then_inc(w_in, 16)
            for t in range(NT):
                sp.wait_ge(xnd, t + 1)
                sp.dma_start(io.xn[t * P:(t + 1) * P, :], xn[:, t, :]).then_inc(stored, 16)
            sp.wait_ge(stored, NT * 16)

        @block.gpsimd
        def _(pool):
            fl = dict(allow_small_or_imprecise_dtypes=True)
            pool.iota(desc[:], [[-1, PER]], base=PER, channel_multiplier=0, **fl).then_inc(init, 1)
            pool.iota(tok[:], [[P, NT]], base=-int(BIG), channel_multiplier=1, **fl).then_inc(init, 1)
            pool.iota(xcode[:], [[1, NX]], base=NE - PAD_CODE, channel_multiplier=0, **fl).then_inc(init, 1)
            pool.iota(xexp[:], [[0, BLKS - 1], [1, NE]], base=0, channel_multiplier=0, **fl).then_inc(init, 1)
            pool.iota(kk[:], [[1, EXTRA + 1]], base=1, channel_multiplier=0, **fl).then_inc(init, 1)
            pool.iota(two[:], [[2, NG]], base=0, channel_multiplier=0, **fl).then_inc(init, 1)
            pool.iota(itf[:], [[0, 2], [1, N_ITEMS + 2]], base=0, channel_multiplier=0, **fl).then_inc(init, 1)
            pool.iota(s.slot[:], [[1, P]], base=0, channel_multiplier=0, **fl).then_inc(init, 1)
            pool.memset(onesr[:], 1.0).then_inc(init, 1)
            pool.memset(tab_pos[:, PAD_CODE, :], -1.0).then_inc(init, 1)
            pool.memset(tab_val[:, PAD_CODE], 0.0).then_inc(init, 1)

        @block.scalar
        def _(act):
            for t in range(NT):
                if t:
                    act.wait_ge(ssq, t)
                nc.scalar.activation(sq[:], x2[:, t, :], ACT.Square, accum_out=st[0][:, t:t + 1]).then_inc(ssq, 1)
            act.wait_ge(recd, 1)
            nc.scalar.activation(st[3][:], st[2][:], ACT.Sqrt).then_inc(rstdd, 1)
            for k in range(KT):
                act.wait_ge(tpd, k + 1)
                nc.scalar.activation(h2T[:, k, :], ps[:, 2 + k % 4, :], ACT.Copy,
                                     scale=s.par[:, C_NORM2 + k:C_NORM2 + k + 1]).then_inc(h2d, 1)
            act.wait_ge(chain, 3)
            nc.scalar.activation(gsc[:], gd[:], ACT.Exp).then_inc(act_exp, 1)
            act.wait_ge(chain, 11)
            nc.scalar.activation(ex[0][:], inl[:], ACT.Exp).then_inc(act_exp, 1)

        @block.vector
        def _(dve):
            count = [0]

            def step(ins):
                count[0] += 1
                ins.then_inc(chain, 1)
                dve.wait_ge(chain, count[0])

            def wide(ap, n):
                return ap.unsqueeze(2).broadcast_to([P, NT, n])

            def first_max(values, peak, score, onehot, n):
                step(nc.vector.tensor_reduce(peak[:], values[:], AX.X, ALU.max))
                step(nc.vector.tensor_tensor(score[:], values[:], wide(peak[:], n), ALU.is_equal))
                step(nc.vector.tensor_tensor(score[:], score[:], desc[:, PER - n:].unsqueeze(1).broadcast_to([P, NT, n]),
                                             ALU.mult))
                step(nc.vector.tensor_reduce(smx[:], score[:], AX.X, ALU.max))
                step(nc.vector.tensor_tensor(onehot[:], score[:], wide(smx[:], n), ALU.is_equal))

            dve.wait_ge(ssq, NT)
            nc.vector.tensor_scalar(st[1][:], st[0][:], 1.0 / D, EPS, ALU.mult, ALU.add).then_inc(msd, 1)
            dve.wait_ge(msd, 1)
            nc.vector.reciprocal(st[2][:], st[1][:]).then_inc(recd, 1)
            dve.wait_ge(rstdd, 1)
            for t in range(NT):
                nc.vector.tensor_scalar(xn[:, t, :], x2[:, t, :], st[3][:, t:t + 1], None, ALU.mult).then_inc(xnd, 1)
            dve.wait_ge(init, 11)
            dve.wait_ge(lgm, 1)
            step(nc.vector.tensor_tensor(lg[:], ps[:, 0, 0:NT * NL].rearrange("p (t n) -> p t n", t=NT),
                                         bias[:].unsqueeze(1).broadcast_to([P, NT, NL]), ALU.add))
            step(nc.vector.tensor_reduce(gmx[:], lg[:, :, 0:NG], AX.X, ALU.max))
            step(nc.vector.tensor_tensor(gd[:], lg[:, :, 0:NG], wide(gmx[:], NG), ALU.subtract))
            dve.wait_ge(act_exp, 1)
            step(nc.vector.tensor_reduce(gsum[:], gsc[:], AX.X, ALU.add))
            step(nc.vector.reciprocal(gg[:], gsum[:]))
            step(nc.vector.tensor_scalar(gsc[:], gd[:], 0.0, None, ALU.is_equal))
            step(nc.vector.tensor_tensor(gsc[:], gsc[:], desc[:, PER - NG:].unsqueeze(1).broadcast_to([P, NT, NG]),
                                         ALU.mult))
            step(nc.vector.tensor_reduce(smx[:], gsc[:], AX.X, ALU.max))
            step(nc.vector.tensor_tensor(goh[:], gsc[:], wide(smx[:], NG), ALU.is_equal))
            for t in range(NT):
                ins = nc.vector.tensor_tensor(picked[:, t], lg[:, t, NG:NL].rearrange("p (g e) -> p g e", g=NG),
                                              goh[:, t].unsqueeze(2).broadcast_to([P, NG, PER]), ALU.mult)
            ins.then_inc(m_done, 1)
            dve.wait_ge(m_done, 1)
            step(nc.vector.tensor_reduce(inl[:], picked[:].rearrange("p t g e -> p t e g"), AX.X, ALU.add))
            ins = nc.vector.tensor_reduce(emx[0][:], inl[:], AX.X, ALU.max)
            ins.then_inc(m_done, 1)
            dve.wait_ge(m_done, 2)
            step(nc.vector.tensor_tensor(inl[:], inl[:], wide(emx[0][:], PER), ALU.subtract))
            dve.wait_ge(act_exp, 2)
            first_max(ex[0], emx[0], esc, eoh[0], PER)
            step(nc.vector.scalar_tensor_tensor(out=ex[1][:], in0=eoh[0][:], scalar=-2.0, in1=ex[0][:], op0=ALU.mult,
                                                op1=ALU.add))
            first_max(ex[1], emx[1], esc, eoh[1], PER)
            step(nc.vector.tensor_tensor(den[:], emx[0][:], emx[1][:], ALU.add))
            step(nc.vector.reciprocal(den[:], den[:]))
            step(nc.vector.tensor_tensor(den[:], den[:], gg[:], ALU.mult))
            for n in range(2):
                step(nc.vector.tensor_tensor(gate[n][:], den[:], emx[n][:], ALU.mult))
                for t in range(NT):
                    ins = nc.vector.tensor_tensor(M[n][:, t, :].rearrange("p (g e) -> p g e", g=NG),
                                                  goh[:, t].unsqueeze(2).broadcast_to([P, NG, PER]),
                                                  eoh[n][:, t].unsqueeze(1).broadcast_to([P, NG, PER]), ALU.mult)
                step(ins)
            nc.vector.tensor_tensor(M[2][:], M[0][:], M[1][:], ALU.add).then_inc(m_done, 1)
            val = tab_val[:, 0:NE].rearrange("p e t v -> p t e v")
            for n in range(2):
                step(nc.vector.tensor_tensor(gm[n][:], M[n][:], wide(gate[n][:], NE), ALU.mult))
            nc.vector.memset(val[:, :, :, 3], 0.0)
            step(nc.vector.tensor_tensor(val[:, :, :, 2], gm[0][:], gm[1][:], ALU.add))
            step(nc.vector.tensor_copy(val[:, :, :, 0], wide(tok[:], NE)))
            step(nc.vector.scalar_tensor_tensor(out=val[:, :, :, 1], in0=M[1][:], scalar=float(T), in1=wide(tok[:], NE),
                                                op0=ALU.mult, op1=ALU.add))
            for b in range(1, BLKS):
                ins = nc.vector.tensor_copy(tab_val[:, b * NE:(b + 1) * NE], tab_val[:, 0:NE])
            step(ins)
            dve.wait_ge(pos_mm, 1)
            step(nc.vector.scalar_tensor_tensor(out=posm[:], in0=ps[:, 0, 0:NT * NE].rearrange("p (t e) -> p t e", t=NT),
                                                scalar=1.0, in1=M[2][:], op0=ALU.add, op1=ALU.mult))
            for b in range(BLKS):
                ins = nc.vector.tensor_scalar(tab_pos[:, b * NE:(b + 1) * NE, :], posm[:].rearrange("p t e -> p e t"),
                                              -1.0 - P * b, None, ALU.add)
            step(ins)
            step(nc.vector.tensor_copy(cnt[:], ps[:, 1, 0:NE]))
            for b in range(1, BLKS):
                ins = nc.vector.tensor_scalar(flag[:, (b - 1) * NE:b * NE], cnt[0:1, :], float(P * b), None, ALU.is_gt)
            step(ins)
            step(nc.vector.tensor_tensor_scan(rank[:], onesr[:], flag[:], 0.0, ALU.mult, ALU.add))
            step(nc.vector.tensor_tensor(fc[:, 0], flag[:], xcode[:], ALU.mult))
            step(nc.vector.tensor_tensor(fc[:, 1], flag[:], xexp[:], ALU.mult))
            big = [1, EXTRA + 1, NX]
            step(nc.vector.tensor_tensor(hit[:], rank[:].unsqueeze(1).broadcast_to(big), kk[:].unsqueeze(2).broadcast_to(big),
                                         ALU.is_equal))
            for n in range(2):
                step(nc.vector.tensor_tensor(hv[:], hit[:], fc[:, n].unsqueeze(1).broadcast_to(big), ALU.mult))
                step(nc.vector.tensor_reduce(xt[:, n], hv[:], AX.X, ALU.add))
            step(nc.vector.tensor_scalar(itf[:, 0, NE:NE + EXTRA + 1], xt[:, 0], float(PAD_CODE), None, ALU.add))
            nc.vector.memset(itf[:, 0, N_ITEMS:], float(PAD_CODE))
            nc.vector.memset(itf[:, 1, N_ITEMS:], 0.0)
            step(nc.vector.tensor_copy(itf[:, 1, NE:NE + EXTRA + 1], xt[:, 1]))
            step(nc.vector.tensor_tensor(np_[:], rank[:, NX - 1:NX].broadcast_to([1, NG]), two[:], ALU.is_gt))
            step(nc.vector.tensor_reduce(npair[:], np_[:], AX.X, ALU.add))
            nc.vector.tensor_scalar(items[:, 2, 0:1], npair[:], float(NE // 2), None, ALU.add)
            step(nc.vector.tensor_copy(items[:, 0:2, :], itf[:]))

        @block.tensor
        def _(pe):
            pe.wait_ge(xnd, NT)
            for k in range(KT):
                if k >= 4:
                    pe.wait_ge(h2d, k - 3)
                for t in range(NT):
                    tp = nc.tensor.transpose(ps[:, 2 + k % 4, t * P:(t + 1) * P], xn[:, t, k * P:(k + 1) * P], s.ident[:])
                tp.then_inc(tpd, 1)
            pe.wait_ge(h2d, KT)
            pe.wait_ge(w_in, 64)
            for t in range(NT):
                for k in range(KT):
                    mm = nc.tensor.matmul(ps[:, 0, t * NL:(t + 1) * NL], h2T[:, k, t * P:(t + 1) * P], wr[:, k, :],
                                          start=k == 0, stop=k == KT - 1)
            mm.then_inc(lgm, 1)
            pe.wait_ge(m_done, 3)
            for t in range(NT):
                for t2 in range(t + 1):
                    nc.tensor.matmul(ps[:, 0, t * NE:(t + 1) * NE], (s.tri_s if t2 == t else s.ones)[:], M[2][:, t2, :],
                                     start=t2 == 0, stop=t2 == t)
            for t in range(NT):
                mm = nc.tensor.matmul(ps[:, 1, 0:NE], s.ones[:], M[2][:, t, :], start=t == 0, stop=t == NT - 1)
            mm.then_inc(pos_mm, 1)


def expert_stage(nc, s, io, tab_pos, tab_val, items):
    with ExitStack() as ctx:
        def sb(name, shape, dt=F32):
            return ctx.enter_context(nc.sbuf_tensor(name, shape, dt))

        sem = ctx.enter_context(Semaphores(nc))
        raw = sb("e_raw", [P, RAW, KC, FE])
        hi = sb("e_hi", [P, 2, KC, FE], F32R)
        lo = sb("e_lo", [P, 2, KC, FE], F32R)
        sel = sb("e_sel", [P, NT, P])
        slot_i = [sb(f"e_slot{u}", [P, 2], U32) for u in range(2)]
        gate = [sb(f"e_gate{u}", [P, 1]) for u in range(2)]
        xg = [sb(f"e_xg{u}", [P, D]) for u in range(2)]
        xT_hi = [sb(f"e_xh{u}", [P, KT, P], F32R) for u in range(2)]
        xT_lo = [sb(f"e_xl{u}", [P, KT, P], F32R) for u in range(2)]
        act_g = sb("e_act", [P, FE])
        hid = sb("e_hid", [P, FE])
        hT_hi = sb("e_hh", [P, KC, P], F32R)
        hT_lo = sb("e_hl", [P, KC, P], F32R)
        y = [sb(f"e_y{u}", [P, D]) for u in range(2)]
        raw_in = [sem(f"ew_in{n}") for n in range(RAW)]
        hi_done = sem("ew_hi")
        lo_done = [sem(f"ew_lo{n}") for n in range(RAW)]
        mm_done = [sem(f"ew_mm{n}") for n in range(2)]
        go, zero, sel_done, tab_mm, slot_done = sem("e_go"), sem("e_zero"), sem("e_sel_done"), sem("e_tab_mm"), sem("e_slot_done")
        rows_in = [sem(f"e_rows{u}") for u in range(2)]
        xt_mm = sem("e_xt_mm")
        xhi_done = sem("e_xhi")
        xlo_done = [sem(f"e_xlo{n}") for n in range(2)]
        silu_done, hid_done, ht_mm, hh_done, hl_done = (sem(n) for n in ("e_silu", "e_hid_done", "e_ht", "e_hh_done", "e_hl_done"))
        y_done = [sem(f"e_y_done{n}") for n in range(2)]
        scattered = [sem(f"e_scat{u}") for u in range(2)]
        y_free = [sem(f"e_y_free{u}") for u in range(2)]
        block = ctx.enter_context(nc.Block())
        ps = s.ps
        G, U, XB, HB, YB, TB = 0, 1, 2, 4, 5, 7
        CH = CH_PER_ITEM
        XR = KT // 4

        def n_pairs(eng):
            return eng.value_load(items[0:1, 2, 0:1], min_val=NE // 2, max_val=N_ITEMS // 2)

        def item(eng, row, k, top):
            return eng.value_load(items[0:1, row, bass.ds(k, 1)], min_val=0, max_val=top)

        @block.sync
        def _(sp):
            pairs = n_pairs(sp)
            with sp.Fori(0, pairs) as i:
                for u in range(2):
                    k = i * 2 + u
                    e = item(sp, 1, k, NE - 1)
                    for ch in range(CH):
                        c = ch % 4
                        sp.wait_ge(lo_done[ch % RAW], k * (CH // RAW) + (ch // RAW + AHEAD))
                        if ch < 8:
                            src = (io.w1_v, io.w3_v)[ch // 4][:, bass.ds(e, 1), c * KC:(c + 1) * KC, :]
                        else:
                            src = io.w2_v[:, bass.ds(e, 1), :, c * FE:(c + 1) * FE]
                        sp.dma_start(raw[:, ch % RAW], src.rearrange("p e k n -> p (e k) n")).then_inc(raw_in[ch % RAW], 16)

        @block.gpsimd
        def _(pool):
            for u in range(2):
                pool.memset(xg[u][:], 0.0).then_inc(zero, 1)
            pool.wait_ge(zero, 2)

            def gather(k, u):
                pool.wait_ge(slot_done, k + 1 + AHEAD)
                pool.sem_inc(go, 1)
                pool.indirect_dma_start(out=xg[u][:], out_offset=None, in_=io.xn,
                                        in_offset=bass.IndirectOffsetOnAxis(ap=slot_i[u][:, 0:1], axis=0),
                                        bounds_check=T - 1, oob_is_err=False).then_inc(rows_in[u], 16)

            for u in range(2):
                pool.sem_inc(y_free[u], AHEAD)
            gather(0, 0)
            pairs = n_pairs(pool)
            with pool.Fori(0, pairs) as i:
                for u in range(2):
                    k = i * 2 + u
                    pool.wait_ge(xt_mm, k * XR + AHEAD)
                    gather(k + 1, 1 - u)
                    for n in range(2):
                        pool.wait_ge(y_done[n], k * 2 + (2 + AHEAD))
                    pool.sem_inc(go, 1)
                    pool.indirect_dma_start(out=io.rows, out_offset=bass.IndirectOffsetOnAxis(
                        ap=slot_i[u][:, 1:2], axis=0), in_=y[u][:], in_offset=None,
                        bounds_check=2 * T - 1, oob_is_err=False).then_inc(scattered[u], 16)
                    pool.wait_ge(scattered[u], i * 16 + 16)
                    pool.sem_inc(y_free[u], 1)
            pool.wait_ge(rows_in[0], pairs * 16 + 16)
            pool.wait_ge(rows_in[1], pairs * 16)

        @block.scalar
        def _(act):
            def split(k, ch):
                act.wait_ge(raw_in[ch % RAW], k * (16 * CH // RAW) + 16 * (ch // RAW + 1))
                act.wait_ge(mm_done[ch % 2], k * (CH // 2) + (ch // 2 + AHEAD))
                nc.scalar.copy(hi[:, ch % 2], raw[:, ch % RAW]).then_inc(hi_done, 1)

            def x_hi(k, u, r):
                act.wait_ge(xt_mm, k * XR + (r + 1 + AHEAD))
                for j in range(4):
                    f = 4 * r + j
                    ins = nc.scalar.activation(xT_hi[u][:, f, :], ps[:, XB + r % 2, j * P:(j + 1) * P], ACT.Copy,
                                               scale=s.par[:, C_NORM2 + f:C_NORM2 + f + 1])
                ins.then_inc(xhi_done, 1)

            def y_out(k, u, c):
                act.wait_ge(mm_done[c % 2], k * (CH // 2) + (5 + c // 2 + AHEAD))
                nc.scalar.activation(y[u][:, c * FE:(c + 1) * FE], ps[:, YB + c % 2, :], ACT.Copy,
                                     scale=gate[u][:, 0:1]).then_inc(y_done[0], 1)

            act.sem_inc(y_done[0], AHEAD)
            for r in range(XR):
                x_hi(0, 0, r)
            pairs = n_pairs(act)
            with act.Fori(0, pairs) as i:
                for u in range(2):
                    k = i * 2 + u
                    for ch in range(6):
                        split(k, ch)
                    act.wait_ge(mm_done[1], k * (CH // 2) + (2 + AHEAD))
                    act.wait_ge(hid_done, k + AHEAD)
                    nc.scalar.activation(act_g[:], ps[:, G, :], ACT.Silu).then_inc(silu_done, 1)
                    for ch in range(6, 10):
                        split(k, ch)
                    x_hi(k + 1, 1 - u, 0)
                    x_hi(k + 1, 1 - u, 1)
                    act.wait_ge(ht_mm, k + 1 + AHEAD)
                    nc.scalar.copy(hT_hi[:], ps[:, HB, :].rearrange("p (f t) -> p f t", f=KC)).then_inc(hh_done, 1)
                    x_hi(k + 1, 1 - u, 2)
                    x_hi(k + 1, 1 - u, 3)
                    split(k, 10)
                    act.wait_ge(y_free[u], i + AHEAD)
                    y_out(k, u, 0)
                    split(k, 11)
                    y_out(k, u, 2)

        @block.vector
        def _(dve):
            def split(k, ch):
                dve.wait_ge(hi_done, k * CH + (ch + 1))
                nc.vector.tensor_tensor(lo[:, ch % 2], raw[:, ch % RAW], hi[:, ch % 2].bitcast(F32),
                                        ALU.subtract).then_inc(lo_done[ch % RAW], 1)

            def select(k, code):
                dve.wait_ge(tab_mm, k + AHEAD)
                for t in range(NT):
                    ins = nc.vector.tensor_scalar(sel[:, t, :], s.slot[:], tab_pos[:, bass.ds(code, 1), t:t + 1].rearrange(
                        "p c t -> p (c t)"), None, ALU.is_equal)
                ins.then_inc(sel_done, 1)

            def slots(k, u, n_scattered):
                dve.wait_ge(tab_mm, k + 1 + AHEAD)
                if n_scattered is not None:
                    dve.wait_ge(y_free[u], n_scattered + AHEAD)
                    dve.wait_ge(y_done[0], k * 2 - 2 + AHEAD)
                nc.vector.tensor_copy(gate[u][:], ps[:, TB, 2:3])
                nc.vector.tensor_scalar(slot_i[u][:], ps[:, TB, 0:2], BIG, None, ALU.add).then_inc(slot_done, 1)

            def x_lo(k, u, r):
                dve.wait_ge(xhi_done, k * XR + (r + 1))
                for j in range(4):
                    f = 4 * r + j
                    ins = nc.vector.scalar_tensor_tensor(
                        out=xT_lo[u][:, f, :], in0=ps[:, XB + r % 2, j * P:(j + 1) * P],
                        scalar=s.par[:, C_NORM2 + f:C_NORM2 + f + 1], in1=xT_hi[u][:, f, :].bitcast(F32),
                        op0=ALU.mult, op1=ALU.subtract)
                ins.then_inc(xlo_done[r % 2], 1)

            def y_out(k, u, c):
                dve.wait_ge(mm_done[c % 2], k * (CH // 2) + (5 + c // 2 + AHEAD))
                nc.vector.tensor_scalar(y[u][:, c * FE:(c + 1) * FE], ps[:, YB + c % 2, :], gate[u][:, 0:1], None,
                                        ALU.mult).then_inc(y_done[1], 1)

            for ahead in (*lo_done, *xlo_done, hid_done, slot_done, y_done[1]):
                dve.sem_inc(ahead, AHEAD)
            pairs = n_pairs(dve)
            select(0, item(dve, 0, 0, PAD_CODE))
            slots(0, 0, None)
            for r in range(XR):
                x_lo(0, 0, r)
            with dve.Fori(0, pairs) as i:
                for u in range(2):
                    k = i * 2 + u
                    select(k + 1, item(dve, 0, k + 1, PAD_CODE))
                    split(k, 0)
                    split(k, 1)
                    slots(k + 1, 1 - u, i + u)
                    for ch in range(2, 10):
                        split(k, ch)
                    dve.wait_ge(silu_done, k + 1)
                    dve.wait_ge(mm_done[1], k * (CH // 2) + (4 + AHEAD))
                    dve.wait_ge(ht_mm, k + AHEAD)
                    nc.vector.tensor_tensor(hid[:], act_g[:], ps[:, U, :], ALU.mult).then_inc(hid_done, 1)
                    x_lo(k + 1, 1 - u, 0)
                    x_lo(k + 1, 1 - u, 1)
                    dve.wait_ge(hh_done, k + 1)
                    nc.vector.tensor_tensor(hT_lo[:], ps[:, HB, :].rearrange("p (f t) -> p f t", f=KC),
                                            hT_hi[:].bitcast(F32), ALU.subtract).then_inc(hl_done, 1)
                    x_lo(k + 1, 1 - u, 2)
                    x_lo(k + 1, 1 - u, 3)
                    split(k, 10)
                    split(k, 11)
                    y_out(k, u, 1)
                    y_out(k, u, 3)

        @block.tensor
        def _(pe):
            def table(k, code):
                pe.wait_ge(sel_done, k + 1)
                pe.wait_ge(slot_done, k + AHEAD)
                for t in range(NT):
                    mm = nc.tensor.matmul(ps[:, TB, 0:4], sel[:, t, :], tab_val[:, bass.ds(code, 1), t, :].rearrange(
                        "p c v -> p (c v)"), start=t == 0, stop=t == NT - 1)
                mm.then_inc(tab_mm, 1)

            def transpose_x(k, u, r, n_rows):
                if r == 0:
                    pe.wait_ge(rows_in[u], n_rows)
                pe.wait_ge(xlo_done[r % 2], k * (XR // 2) + (r // 2 + AHEAD))
                for j in range(4):
                    f = 4 * r + j
                    tp = nc.tensor.transpose(ps[:, XB + r % 2, j * P:(j + 1) * P], xg[u][:, f * P:(f + 1) * P], s.ident[:])
                tp.then_inc(xt_mm, 1)

            def three(out, a_hi, a_lo, b_hi, b_lo, first, last):
                nc.tensor.matmul(out, a_hi, b_hi, start=first, stop=False)
                nc.tensor.matmul(out, a_lo, b_hi, start=False, stop=False)
                return nc.tensor.matmul(out, a_hi, b_lo, start=False, stop=last)

            for ahead in (*mm_done, tab_mm, xt_mm, ht_mm):
                pe.sem_inc(ahead, AHEAD)
            pairs = n_pairs(pe)
            table(0, item(pe, 0, 0, PAD_CODE))
            for r in range(XR):
                transpose_x(0, 0, r, 16)
            with pe.Fori(0, pairs) as i:
                for u in range(2):
                    k = i * 2 + u
                    for ch in range(8):
                        if ch == 0:
                            for n in range(2):
                                pe.wait_ge(xlo_done[n], k * (XR // 2) + (XR // 2 + AHEAD))
                        pe.wait_ge(lo_done[ch % RAW], k * (CH // RAW) + (ch // RAW + 1 + AHEAD))
                        for j in range(KC):
                            f = ch % 4 * KC + j
                            mm = three(ps[:, G if ch < 4 else U, :], xT_hi[u][:, f, :], xT_lo[u][:, f, :],
                                       hi[:, ch % 2, j], lo[:, ch % 2, j], f == 0, f == KT - 1)
                        mm.then_inc(mm_done[ch % 2], 1)
                        if ch == 0:
                            table(k + 1, item(pe, 0, k + 1, PAD_CODE))
                    n_rows = i * 16 + (32 if u else 16)
                    transpose_x(k + 1, 1 - u, 0, n_rows)
                    transpose_x(k + 1, 1 - u, 1, n_rows)
                    pe.wait_ge(hid_done, k + 1 + AHEAD)
                    for j in range(KC):
                        tp = nc.tensor.transpose(ps[:, HB, j * P:(j + 1) * P], hid[:, j * P:(j + 1) * P], s.ident[:])
                    tp.then_inc(ht_mm, 1)
                    transpose_x(k + 1, 1 - u, 2, n_rows)
                    transpose_x(k + 1, 1 - u, 3, n_rows)
                    pe.wait_ge(hl_done, k + 1)
                    for ch in range(8, CH):
                        c = ch - 8
                        pe.wait_ge(lo_done[ch % RAW], k * (CH // RAW) + (ch // RAW + 1 + AHEAD))
                        pe.wait_ge(y_done[c % 2], k * 2 + (c // 2 + AHEAD))
                        for j in range(KC):
                            mm = three(ps[:, YB + c % 2, :], hT_hi[:, j, :], hT_lo[:, j, :], hi[:, ch % 2, j],
                                       lo[:, ch % 2, j], j == 0, j == KC - 1)
                        mm.then_inc(mm_done[ch % 2], 1)


def combine_stage(nc, s, io, x2):
    with ExitStack() as ctx:
        sem = ctx.enter_context(Semaphores(nc))
        r = [ctx.enter_context(nc.sbuf_tensor(f"c_row{n}", [P, NT, D], F32)) for n in range(2)]
        row_in = [[sem(f"c_in{n}_{t}") for t in range(NT)] for n in range(2)]
        first, both, stored = sem("c_first"), sem("c_both"), sem("c_stored")
        block = ctx.enter_context(nc.Block())

        @block.sync
        def _(sp):
            for t in range(NT):
                for n in range(2):
                    at = n * T + t * P
                    sp.dma_start(r[n][:, t, :], io.rows[at:at + P, :]).then_inc(row_in[n][t], 16)

        @block.vector
        def _(dve):
            for t in range(NT):
                dve.wait_ge(row_in[0][t], 16)
                nc.vector.tensor_tensor(x2[:, t, :], x2[:, t, :], r[0][:, t, :], ALU.add).then_inc(first, 1)
                dve.wait_ge(row_in[1][t], 16)
                dve.wait_ge(first, t + 1)
                nc.vector.tensor_tensor(x2[:, t, :], x2[:, t, :], r[1][:, t, :], ALU.add).then_inc(both, 1)

        @block.scalar
        def _(act):
            for t in range(NT):
                act.wait_ge(both, t + 1)
                act.dma_start(io.out[t * P:(t + 1) * P, :], x2[:, t, :]).then_inc(stored, 16)
            act.wait_ge(stored, NT * 16)


def program(nc, io):
    with ExitStack() as ctx:
        s = shared(nc, ctx)
        with ExitStack() as front:
            hT_hi = front.enter_context(nc.sbuf_tensor("hT_hi", [P, KT, T], F32R))
            hT_lo = front.enter_context(nc.sbuf_tensor("hT_lo", [P, KT, T], F32R))
            setup_stage(nc, s, io, hT_hi, hT_lo)
            project_stage(nc, s, io, hT_hi, hT_lo)
        x2 = ctx.enter_context(nc.sbuf_tensor("x2", [P, NT, D], F32))
        with ExitStack() as mixed:
            mix_hi = mixed.enter_context(nc.sbuf_tensor("mix_hi", [P, KT, T], F32R))
            mix_lo = mixed.enter_context(nc.sbuf_tensor("mix_lo", [P, KT, T], F32R))
            stick_stage(nc, s, io, mix_hi, mix_lo)
            delta_stage(nc, s, io, mix_hi, mix_lo, x2)
            out_proj_stage(nc, s, io, mix_hi, mix_lo, x2)
        with ExitStack() as back:
            tab_pos = back.enter_context(nc.sbuf_tensor("tab_pos", [P, PAD_CODE + 1, NT], F32))
            tab_val = back.enter_context(nc.sbuf_tensor("tab_val", [P, PAD_CODE + 1, NT, 4], F32))
            items = back.enter_context(nc.sbuf_tensor("items", [1, 3, N_ITEMS + 2], I32))
            route_stage(nc, s, io, x2, tab_pos, tab_val, items)
            expert_stage(nc, s, io, tab_pos, tab_val, items)
        combine_stage(nc, s, io, x2)


def views(io, a):
    io.x = a["x"].rearrange("b t d -> (b t) d")
    io.norm1_w = a["norm1_w"].rearrange("l (k p) -> (l k) p", p=P)
    io.norm2_w = a["norm2_w"].rearrange("l (k p) -> (l k) p", p=P)
    io.conv_w = a["gdn_conv_w"].rearrange("l n (c p) -> (l n c) p", p=P)
    io.q_norm_w, io.k_norm_w, io.out_norm_w = a["sb_q_norm_w"], a["sb_k_norm_w"], a["gdn_out_norm_w"]
    io.a_log, io.dt_bias = a["gdn_a_log"], a["gdn_dt_bias"]
    io.w_in_v = a["w_in"].rearrange("l (k p) n -> p (l k) n", p=P)
    io.w_o_v = a["w_o"].rearrange("l (k p) n -> p (l k) n", p=P)
    io.w_group, io.w_expert = a["w_group"][0], a["w_expert"][0]
    io.b_group, io.b_expert = a["b_group"], a["b_expert"]
    io.w1_v = a["w1"][0].rearrange("e (k p) n -> p e k n", p=P)
    io.w3_v = a["w3"][0].rearrange("e (k p) n -> p e k n", p=P)
    io.w2_v = a["w2"][0].rearrange("e (k p) n -> p e k n", p=P)
    io.proj_qkv = io.proj[0:TILE_GQ].rearrange("(g e) p t -> p g e t", g=3)
    io.proj_gdn = io.proj[TILE_GQ:TILE_GZ].rearrange("(g e) p t -> p g e t", g=3)
    io.proj_z = io.proj[TILE_GZ:].rearrange("e p t -> p e t")


def build(nc, args, out):
    io = Core()
    io.proj = nc.dram_tensor("proj_scratch", (4 * N_GRP, P, T), F32, kind="Internal").ap()
    io.xn = nc.dram_tensor("xn_scratch", (T, D), F32, kind="Internal").ap()
    io.rows = nc.dram_tensor("rows_scratch", (2 * T, D), F32, kind="Internal").ap()
    io.out = out.rearrange("b t d -> (b t) d")
    views(io, args)
    program(nc, io)


INPUTS = ["x", "norm1_w", "w_in", "sb_q_norm_w", "sb_k_norm_w", "gdn_conv_w", "gdn_a_log", "gdn_dt_bias",
          "gdn_out_norm_w", "w_o", "norm2_w", "w_group", "b_group", "w_expert", "b_expert", "w1", "w3", "w2"]


def kernel(**inputs):
    import numpy as np
    from concourse import bacc
    from concourse.bass_utils import run_bass_kernel_spmd

    nc = bacc.Bacc("TRN2", target_bir_lowering=False, num_devices=1)
    arrays, args = {}, {}
    for name in INPUTS:
        a = np.ascontiguousarray(inputs[name])
        arrays[f"in_{name}"] = a
        args[name] = nc.dram_tensor(f"in_{name}", a.shape, mybir.dt.from_np(a.dtype), kind="ExternalInput").ap()
    out = nc.dram_tensor("out_0", (1, T, D), F32, kind="ExternalOutput").ap()
    build(nc, args, out)
    result = run_bass_kernel_spmd(nc, [arrays], core_ids=[0])
    return result.results[0]["out_0"]
```

```python
from contextlib import ExitStack

import concourse.bass as bass
from concourse import mybir

F32 = mybir.dt.float32
F32R = mybir.dt.float32r
I32 = mybir.dt.int32
U32 = mybir.dt.uint32
ALU = mybir.AluOpType
ACT = mybir.ActivationFunctionType
AX = mybir.AxisListType

P = 128
T = 512
NT = T // P
D = 2048
KT = D // P
HEADS = 8
GRP = 512
N_GRP = 14
IN_COLS = N_GRP * GRP + 2 * HEADS
TILE_Q, TILE_K, TILE_V = 0, 8, 16
TILE_GQ, TILE_GK, TILE_GV, TILE_GZ = 24, 32, 40, 48
TAPS = 4
LEVELS = 7
KC = 4
RAW = 4
NG, NE = 4, 32
PER = NE // NG
FE = 512
BLKS = T // P
EXTRA = 2 * T // P - 1
N_ITEMS = NE + EXTRA + 1
PAD_CODE = BLKS * NE
EPS = 1e-6
AHEAD = 1
BIG = 4096.0
EXP_LN = 6
CH_PER_ITEM = 12
C_NORM1, C_NORM2, C_CONV = 0, KT, 2 * KT


class Core:
    pass


class Semaphores:

    def __init__(self, nc):
        self.nc, self.taken = nc, []

    def __enter__(self):
        return self

    def __call__(self, name):
        self.taken.append(self.nc.alloc_semaphore(name))
        return self.taken[-1]

    def __exit__(self, *error):
        if error[0] is None:
            self.nc.clear_and_free_semaphores(self.taken)
            self.nc.all_engine_barrier()


def load_exp_and_ln(nc):
    nc.scalar.add_instruction(mybir.InstLoadActFuncSet(name=nc.get_next_instruction_name(), act_func_set_id=EXP_LN,
                                                       ins=[], outs=[]))


def shared(nc, ctx):
    s = Core()

    def sb(name, shape, dt=F32):
        return ctx.enter_context(nc.sbuf_tensor(name, shape, dt))

    s.ident = sb("ident", [P, P])
    s.ones = sb("ones", [P, P])
    s.slot = sb("slot", [P, P])
    s.tri = sb("tri", [P, P])
    s.tri_s = sb("tri_s", [P, P])
    s.ntri = sb("ntri", [P, P])
    s.nones = sb("nones", [P, P])
    s.unseen = sb("unseen", [P, P])
    s.par = sb("par", [P, P])
    s.wn = sb("wn", [P, 4])
    s.zeros = sb("zeros", [P, P])
    s.eps = sb("eps", [P, 1])
    s.one = sb("one", [P, 1])
    s.gates = sb("gates", [P, NT, 2 * HEADS])
    s.ps = ctx.enter_context(nc.psum_tensor("ps", [P, 8, 512], F32))
    return s


def setup_stage(nc, s, io, hT_hi, hT_lo):
    with ExitStack() as ctx:
        def sb(name, shape, dt=F32):
            return ctx.enter_context(nc.sbuf_tensor(name, shape, dt))

        sem = ctx.enter_context(Semaphores(nc))

        xs = sb("xs", [P, NT, D])
        sq = sb("sq", [P, D])
        ss = sb("ss", [P, NT])
        ms = sb("ms", [P, NT])
        rec = sb("rec", [P, NT])
        rstd = sb("rstd", [P, NT])
        prow = sb("prow", [P, P])
        wrow = sb("wrow", [3, P])
        x_in = [sem(f"x_in{t}") for t in range(NT)]
        par_in, memset_done, consts_done = sem("par_in"), sem("memset_done"), sem("consts_done")
        sumsq_done, ms_done, rec_done, rstd_done = sem("sumsq_done"), sem("ms_done"), sem("rec_done"), sem("rstd_done")
        xn_done, par_t, par_out = sem("xn_done"), sem("par_t"), sem("par_out")
        tp_done, hi_done, lo_done = sem("tp_done"), sem("hi_done"), sem("lo_done")
        block = ctx.enter_context(nc.Block())
        ps = s.ps

        @block.sync
        def _(sp):
            for t in range(NT):
                sp.dma_start(xs[:, t, :], io.x[t * P:(t + 1) * P, :]).then_inc(x_in[t], 16)
            sp.dma_start(prow[0:KT, :], io.norm1_w).then_inc(par_in, 16)
            sp.dma_start(prow[KT:2 * KT, :], io.norm2_w).then_inc(par_in, 16)
            sp.dma_start(prow[2 * KT:P, :], io.conv_w).then_inc(par_in, 16)
            sp.dma_start(wrow[0:1, :], io.q_norm_w).then_inc(par_in, 16)
            sp.dma_start(wrow[1:2, :], io.k_norm_w).then_inc(par_in, 16)
            sp.dma_start(wrow[2:3, :], io.out_norm_w).then_inc(par_in, 16)

        @block.gpsimd
        def _(pool):
            pool.memset(s.ones[:], 1.0).then_inc(memset_done, 1)
            pool.memset(s.nones[:], -1.0).then_inc(memset_done, 1)
            pool.memset(s.eps[:], EPS).then_inc(memset_done, 1)
            pool.memset(s.one[:], 1.0).then_inc(memset_done, 1)
            pool.memset(s.zeros[:], 0.0).then_inc(memset_done, 1)
            pool.wait_ge(memset_done, 5)
            for out, src, op, base, step, mult in (
                (s.tri, s.ones, ALU.is_ge, 0, 1, -1),
                (s.tri_s, s.ones, ALU.is_gt, 0, 1, -1),
                (s.ntri, s.nones, ALU.is_ge, 0, -1, 1),
                (s.ident, s.ones, ALU.is_equal, 0, 1, -1),
                (s.unseen, s.zeros, ALU.is_gt, 0, 1, -1),
            ):
                pool.affine_select(out=out[:], in_=src[:], compare_op=op, fill=-1e30 if src is s.zeros else 0.0,
                                   base=base,
                                   pattern=[[step, P]], channel_multiplier=mult).then_inc(consts_done, 1)

        @block.scalar
        def _(act):
            for t in range(NT):
                act.wait_ge(x_in[t], 16)
                if t:
                    act.wait_ge(sumsq_done, t)
                nc.scalar.activation(sq[:], xs[:, t, :], ACT.Square, accum_out=ss[:, t:t + 1]).then_inc(sumsq_done, 1)
            act.wait_ge(rec_done, 1)
            nc.scalar.activation(rstd[:], rec[:], ACT.Sqrt).then_inc(rstd_done, 1)
            act.wait_ge(par_out, 2)
            for k in range(KT):
                act.wait_ge(tp_done, k + 1)
                nc.scalar.activation(hT_hi[:, k, :], ps[:, 2 + k % 4, :], ACT.Copy,
                                     scale=s.par[:, C_NORM1 + k:C_NORM1 + k + 1]).then_inc(hi_done, 1)

        @block.vector
        def _(dve):
            dve.wait_ge(sumsq_done, NT)
            nc.vector.tensor_scalar(ms[:], ss[:], 1.0 / D, EPS, ALU.mult, ALU.add).then_inc(ms_done, 1)
            dve.wait_ge(ms_done, 1)
            nc.vector.reciprocal(rec[:], ms[:]).then_inc(rec_done, 1)
            dve.wait_ge(par_t, 2)
            nc.vector.tensor_copy(s.par[:], ps[:, 0, 0:P]).then_inc(par_out, 1)
            nc.vector.tensor_scalar(s.wn[:, 0:1], ps[:, 1, 0:1], P ** -0.5, None, ALU.mult)
            nc.vector.tensor_copy(s.wn[:, 1:3], ps[:, 1, 1:3]).then_inc(par_out, 1)
            dve.wait_ge(rstd_done, 1)
            for t in range(NT):
                nc.vector.tensor_scalar(xs[:, t, :], xs[:, t, :], rstd[:, t:t + 1], None,
                                        ALU.mult).then_inc(xn_done, 1)
            dve.wait_ge(par_out, 2)
            for k in range(KT):
                dve.wait_ge(hi_done, k + 1)
                nc.vector.scalar_tensor_tensor(
                    out=hT_lo[:, k, :], in0=ps[:, 2 + k % 4, :], scalar=s.par[:, C_NORM1 + k:C_NORM1 + k + 1],
                    in1=hT_hi[:, k, :].bitcast(F32), op0=ALU.mult, op1=ALU.subtract).then_inc(lo_done, 1)

        @block.tensor
        def _(pe):
            pe.wait_ge(par_in, 6 * 16)
            pe.wait_ge(consts_done, 4)
            nc.tensor.transpose(ps[:, 0, 0:P], prow[:], s.ident[:]).then_inc(par_t, 1)
            nc.tensor.transpose(ps[:, 1, 0:3], wrow[:], s.ident[0:3, 0:3]).then_inc(par_t, 1)
            pe.wait_ge(xn_done, NT)
            for k in range(KT):
                if k >= 4:
                    pe.wait_ge(lo_done, k - 3)
                for t in range(NT):
                    tp = nc.tensor.transpose(ps[:, 2 + k % 4, t * P:(t + 1) * P],
                                             xs[:, t, k * P:(k + 1) * P], s.ident[:])
                tp.then_inc(tp_done, 1)


def project_stage(nc, s, io, hT_hi, hT_lo):
    with ExitStack() as ctx:
        def sb(name, shape, dt=F32):
            return ctx.enter_context(nc.sbuf_tensor(name, shape, dt))

        sem = ctx.enter_context(Semaphores(nc))

        raw = sb("w_raw", [P, RAW, KC, GRP])
        hi = sb("w_hi", [P, 2, KC, GRP], F32R)
        lo = sb("w_lo", [P, 2, KC, GRP], F32R)
        stage = sb("p_stage", [P, 2, 4, T])
        ab_raw = sb("ab_raw", [P, KT, 2 * HEADS])
        ab_hi = sb("ab_hi", [P, KT, 2 * HEADS], F32R)
        ab_lo = sb("ab_lo", [P, KT, 2 * HEADS], F32R)
        raw_in = [sem(f"pw_in{n}") for n in range(RAW)]
        hi_done, lo_done, mm_done = sem("pw_hi"), sem("pw_lo"), sem("pw_mm")
        staged = sem("staged")
        stored = [sem(f"p_stored{n}") for n in range(2)]
        stage_free = [sem(f"stage_free{n}") for n in range(2)]
        ab_in, ab_split, ab_mm, ab_out = sem("ab_in"), sem("ab_split"), sem("ab_mm"), sem("ab_out")
        block = ctx.enter_context(nc.Block())
        ps = s.ps
        CH = KT // KC
        BODY = 2 * CH
        PAIRS = N_GRP // 2

        @block.sync
        def _(sp):
            def load(ch, pair, col):
                return sp.dma_start(raw[:, ch % RAW, :, :], io.w_in_v[:, ch % CH * KC:(ch % CH + 1) * KC,
                                                                      bass.ds(col, GRP)])
            for ch in range(BODY):
                if ch >= RAW:
                    sp.wait_ge(lo_done, ch - RAW + 1)
                load(ch, 0, ch // CH * GRP).then_inc(raw_in[ch % RAW], 16)
            sp.dma_start(ab_raw[:], io.w_in_v[:, :, N_GRP * GRP:IN_COLS]).then_inc(ab_in, 16)
            with sp.Fori(1, PAIRS) as pair:
                for ch in range(BODY):
                    sp.wait_ge(lo_done, pair * BODY + (ch - RAW + 1))
                    load(ch, pair, pair * (2 * GRP) + ch // CH * GRP).then_inc(raw_in[ch % RAW], 16)

        @block.scalar
        def _(act):
            def split(pair, first):
                for ch in range(BODY):
                    act.wait_ge(raw_in[ch % RAW], pair * 32 + 16 * (ch // RAW + 1))
                    if ch >= 2 or not first:
                        act.wait_ge(mm_done, pair * BODY + (ch - 1))
                    nc.scalar.activation(hi[:, ch % 2], raw[:, ch % RAW], ACT.Copy).then_inc(hi_done, 1)
                    if ch % CH == 1 and (ch // CH or not first):
                        copy_out(pair, ch // CH)

            def copy_out(pair, g):
                half = 1 - g
                act.wait_ge(mm_done, pair * BODY + CH * g)
                act.wait_ge(stage_free[half], pair - half + AHEAD)
                nc.scalar.copy(stage[:, half], ps[:, 4 * half:4 * half + 4, :]).then_inc(staged, 1)

            split(0, True)
            with act.Fori(1, PAIRS) as pair:
                split(pair, False)
            copy_out(PAIRS, 0)
            act.wait_ge(ab_in, 16)
            nc.scalar.activation(ab_hi[:], ab_raw[:], ACT.Copy).then_inc(ab_split, 1)

        @block.gpsimd
        def _(pool):
            for g in range(2):
                pool.sem_inc(stage_free[g], AHEAD)
            with pool.Fori(0, PAIRS) as pair:
                for g in range(2):
                    pool.wait_ge(staged, pair * 2 + (g + 1))
                    pool.dma_start(io.proj[bass.ds(pair * 8 + 4 * g, 4)].rearrange("f p t -> p f t"),
                                   stage[:, g]).then_inc(stored[g], 16)
                    pool.wait_ge(stored[g], pair * 16 + 16)
                    pool.sem_inc(stage_free[g], 1)

        @block.vector
        def _(dve):
            with dve.Fori(0, PAIRS) as pair:
                for ch in range(BODY):
                    dve.wait_ge(hi_done, pair * BODY + (ch + 1))
                    nc.vector.tensor_tensor(lo[:, ch % 2], raw[:, ch % RAW], hi[:, ch % 2].bitcast(F32),
                                            ALU.subtract).then_inc(lo_done, 1)
            dve.wait_ge(ab_split, 1)
            nc.vector.tensor_tensor(ab_lo[:], ab_raw[:], ab_hi[:].bitcast(F32), ALU.subtract).then_inc(ab_split, 1)
            dve.wait_ge(ab_mm, 1)
            nc.vector.tensor_copy(s.gates[:], ps[:, 0, 0:NT * 2 * HEADS].rearrange(
                "p (t c) -> p t c", t=NT)).then_inc(ab_out, 1)

        @block.tensor
        def _(pe):
            def products(pair, first):
                for ch in range(BODY):
                    g, c = ch // CH, ch % CH
                    if c == 0 and not first:
                        pe.wait_ge(staged, pair * 2 + (g - 1))
                    pe.wait_ge(lo_done, pair * BODY + (ch + 1))
                    for f in range(4):
                        out = ps[:, 4 * g + f, :]
                        for k in range(KC):
                            kt = c * KC + k
                            w = slice(f * P, (f + 1) * P)
                            nc.tensor.matmul(out, hi[:, ch % 2, k, w], hT_hi[:, kt, :], start=kt == 0, stop=False)
                            nc.tensor.matmul(out, hi[:, ch % 2, k, w], hT_lo[:, kt, :], start=False, stop=False)
                            mm = nc.tensor.matmul(out, lo[:, ch % 2, k, w], hT_hi[:, kt, :], start=False,
                                                  stop=kt == KT - 1)
                    mm.then_inc(mm_done, 1)

            products(0, True)
            with pe.Fori(1, PAIRS) as pair:
                products(pair, False)
            pe.wait_ge(ab_split, 2)
            pe.wait_ge(staged, N_GRP - 1)
            for t in range(NT):
                out = ps[:, 0, t * 2 * HEADS:(t + 1) * 2 * HEADS]
                for k in range(KT):
                    tok = slice(t * P, (t + 1) * P)
                    nc.tensor.matmul(out, hT_hi[:, k, tok], ab_hi[:, k, :], start=k == 0, stop=False)
                    nc.tensor.matmul(out, hT_lo[:, k, tok], ab_hi[:, k, :], start=False, stop=False)
                    mm = nc.tensor.matmul(out, hT_hi[:, k, tok], ab_lo[:, k, :], start=False, stop=k == KT - 1)
            mm.then_inc(ab_mm, 1)


def stick_stage(nc, s, io, mix_hi, mix_lo):
    with ExitStack() as ctx:
        def sb(name, shape, dt=F32):
            return [ctx.enter_context(nc.sbuf_tensor(f"{name}{u}", shape, dt)) for u in range(2)]

        sem1 = ctx.enter_context(Semaphores(nc))

        def sem(name):
            return [sem1(f"{name}{u}") for u in range(2)]

        qkv = sb("s_qkv", [P, 3, T])
        sq = sb("s_sq", [P, 2, T])
        lnr = sb("s_ln", [P, 2, T])
        rr = sb("s_r", [P, 2, T])
        qn, kn = sb("s_qn", [P, T]), sb("s_kn", [P, T])
        vtok = sb("s_vtok", [P, NT, P])
        lg = sb("s_lg", [P, NT, T])
        spl = sb("s_spl", [P, NT, T])
        wgt = sb("s_wgt", [P, NT, T])
        qkv_in, sq_done, ss_done, ln_done, r_done = (sem(n) for n in ("qkv_in", "sq_done", "ss_done", "sln_done", "sr_done"))
        vt_done, vtok_done, qk_done, z_done = (sem(n) for n in ("vt_done", "vtok_done", "qk_done", "z_done"))
        abs_done, e_done, l_done, sp_done = (sem(n) for n in ("abs_done", "e_done", "l_done", "sp_done"))
        cum_done, w_done, o_done = (sem(n) for n in ("cum_done", "w_done", "o_done"))
        mhi_done, mlo_done, relu_done = sem("mhi_done"), sem("mlo_done"), sem("relu_done")
        block = ctx.enter_context(nc.Block())
        ps = s.ps
        PAIRS = HEADS // 2
        DOWN = list(range(NT - 1, -1, -1))

        def live(kb):
            return slice(kb * P, T)

        @block.sync
        def _(sp):
            with sp.Fori(0, PAIRS) as i:
                for u in range(2):
                    sp.wait_ge(z_done[u], i * NT + AHEAD)
                    sp.dma_start(qkv[u][:], io.proj_qkv[:, :, bass.ds(i * 2 + u, 1), :].rearrange(
                        "p g e t -> p (g e) t")).then_inc(qkv_in[u], 16)

        @block.scalar
        def _(act):
            load_exp_and_ln(nc)
            with act.Fori(0, PAIRS) as i:
                for u in range(2):
                    act.wait_ge(qkv_in[u], i * 16 + 16)
                    nc.scalar.activation(sq[u][:], qkv[u][:, 0:2, :], ACT.Square).then_inc(sq_done[u], 1)
                for u in range(2):
                    b = 4 * u
                    act.wait_ge(ss_done[u], i + 1)
                    nc.scalar.activation(lnr[u][:], ps[:, b + 1:b + 3, :], ACT.Ln, scale=1.0 / P,
                                         bias=s.eps[:]).then_inc(ln_done[u], 1)
                    act.wait_ge(ln_done[u], i + 1)
                    nc.scalar.activation(rr[u][:], lnr[u][:], ACT.Exp, scale=-0.5).then_inc(r_done[u], 1)
                for n, kb in enumerate(DOWN):
                    for u in range(2):
                        act.wait_ge(abs_done[u], i * NT + (n + 1))
                        nc.scalar.activation(lg[u][:, kb, live(kb)], lg[u][:, kb, live(kb)],
                                             ACT.Exp).then_inc(e_done[u], 1)
                    for u in range(2):
                        act.wait_ge(e_done[u], i * NT + (n + 1))
                        nc.scalar.activation(lg[u][:, kb, live(kb)], lg[u][:, kb, live(kb)], ACT.Ln,
                                             bias=s.one[:]).then_inc(l_done[u], 1)
                for n, kb in enumerate(DOWN):
                    for u in range(2):
                        act.wait_ge(cum_done[u], i * NT + (n + 1))
                        nc.scalar.activation(wgt[u][:, kb, live(kb)], ps[:, 4 * u + kb, live(kb)],
                                             ACT.Exp).then_inc(w_done[u], 1)
                for u in range(2):
                    act.wait_ge(o_done[u], i + 1)
                    nc.scalar.copy(mix_hi[:, bass.ds(i * 2 + u, 1), :].rearrange("p e t -> p (e t)"),
                                   ps[:, 4 * u + 3, :]).then_inc(mhi_done[u], 1)

        @block.vector
        def _(dve):
            for u in range(2):
                for ahead in (vtok_done[u], mlo_done[u]):
                    dve.sem_inc(ahead, AHEAD)
            with dve.Fori(0, PAIRS) as i:
                for u in range(2):
                    dve.wait_ge(vt_done[u], i + 1)
                    nc.vector.tensor_copy(vtok[u][:], ps[:, 4 * u, :].rearrange(
                        "p (b d) -> p b d", b=NT)).then_inc(vtok_done[u], 1)
                for u in range(2):
                    dve.wait_ge(r_done[u], i + 1)
                    for n, out in enumerate((qn[u], kn[u])):
                        nc.vector.scalar_tensor_tensor(out=out[:], in0=qkv[u][:, n, :], scalar=s.wn[:, n:n + 1],
                                                       in1=rr[u][:, n, :], op0=ALU.mult,
                                                       op1=ALU.mult).then_inc(qk_done[u], 1)
                for n, kb in enumerate(DOWN):
                    for u in range(2):
                        dve.wait_ge(z_done[u], i * NT + (n + 1 + AHEAD))
                        nc.vector.tensor_scalar(spl[u][:, kb, live(kb)], ps[:, 4 * u + kb, live(kb)], 0.0, None,
                                                ALU.max).then_inc(relu_done[u], 1)
                    for u in range(2):
                        dve.wait_ge(relu_done[u], i * NT + (n + 1))
                        nc.vector.scalar_tensor_tensor(out=lg[u][:, kb, live(kb)], in0=spl[u][:, kb, live(kb)],
                                                       scalar=-2.0, in1=ps[:, 4 * u + kb, live(kb)], op0=ALU.mult,
                                                       op1=ALU.add).then_inc(abs_done[u], 1)
                for n, kb in enumerate(DOWN):
                    for u in range(2):
                        dve.wait_ge(l_done[u], i * NT + (n + 1))
                        nc.vector.tensor_tensor(spl[u][:, kb, live(kb)], spl[u][:, kb, live(kb)],
                                                lg[u][:, kb, live(kb)], ALU.add).then_inc(sp_done[u], 1)
                for u in range(2):
                    dve.wait_ge(mhi_done[u], i + 1)
                    nc.vector.tensor_tensor(
                        mix_lo[:, bass.ds(i * 2 + u, 1), :].rearrange("p e t -> p (e t)"), ps[:, 4 * u + 3, :],
                        mix_hi[:, bass.ds(i * 2 + u, 1), :].rearrange("p e t -> p (e t)").bitcast(F32),
                        ALU.subtract).then_inc(mlo_done[u], 1)

        @block.tensor
        def _(pe):
            for u in range(2):
                pe.sem_inc(z_done[u], AHEAD)
            with pe.Fori(0, PAIRS) as i:
                for u in range(2):
                    b = 4 * u
                    pe.wait_ge(qkv_in[u], i * 16 + 16)
                    pe.wait_ge(vtok_done[u], i + AHEAD)
                    for n in range(NT):
                        tp = nc.tensor.transpose(ps[:, b, n * P:(n + 1) * P], qkv[u][:, 2, n * P:(n + 1) * P],
                                                 s.ident[:])
                    tp.then_inc(vt_done[u], 1)
                    pe.wait_ge(sq_done[u], i + 1)
                    for n in range(2):
                        mm = nc.tensor.matmul(ps[:, b + 1 + n, :], s.ones[:], sq[u][:, n, :], start=True, stop=True)
                    mm.then_inc(ss_done[u], 1)
                for u in range(2):
                    pe.wait_ge(mlo_done[u], i + AHEAD)
                    pe.wait_ge(vtok_done[u], i + 1 + AHEAD)
                    pe.wait_ge(qk_done[u], i * 2 + 2)
                    for kb in DOWN:
                        nc.tensor.matmul(ps[:, 4 * u + kb, live(kb)], kn[u][:, kb * P:(kb + 1) * P],
                                         qn[u][:, live(kb)], start=True, stop=False, skip_group_check=True)
                        nc.tensor.matmul(ps[:, 4 * u + kb, kb * P:(kb + 1) * P], s.ident[:], s.unseen[:], start=False,
                                         stop=False, skip_group_check=True).then_inc(z_done[u], 1)
                for n, kb in enumerate(DOWN):
                    for u in range(2):
                        pe.wait_ge(sp_done[u], i * NT + (n + 1))
                        out = ps[:, 4 * u + kb, :]
                        mm = nc.tensor.matmul(out[:, live(kb)], s.ntri[:], spl[u][:, kb, live(kb)], start=False,
                                              stop=kb == NT - 1, skip_group_check=True)
                        for later in range(kb + 1, NT):
                            mm = nc.tensor.matmul(out[:, live(later)], s.nones[:], spl[u][:, later, live(later)],
                                                  start=False, stop=later == NT - 1, skip_group_check=True)
                        mm.then_inc(cum_done[u], 1)
                for u in range(2):
                    pe.wait_ge(w_done[u], i * NT + NT)
                    out = ps[:, 4 * u + 3, :]
                    for kb in range(NT):
                        mm = nc.tensor.matmul(out[:, live(kb)], vtok[u][:, kb, :], wgt[u][:, kb, live(kb)],
                                              start=kb == 0, stop=kb == NT - 1, skip_group_check=True)
                    mm.then_inc(o_done[u], 1)


def delta_stage(nc, s, io, mix_hi, mix_lo, spare):
    with ExitStack() as ctx:
        def one(name, shape, dt=F32):
            return ctx.enter_context(nc.sbuf_tensor(name, shape, dt))

        def sb(name, shape, dt=F32):
            return [one(f"{name}{u}", shape, dt) for u in range(2)]

        sem1 = ctx.enter_context(Semaphores(nc))

        def sem(name):
            return [sem1(f"{name}{u}") for u in range(2)]

        g = one("g", [P, HEADS, NT])
        beta = one("beta", [P, HEADS, NT])
        gcc = one("gcc", [P, HEADS, NT])
        nbe = one("nbe", [P, HEADS, NT])
        kds = one("kds", [P, HEADS, NT])
        gt = [one(f"gt{n}", [P, HEADS, NT]) for n in range(4)]
        alog = one("alog", [P, HEADS])
        dtb = one("dtb", [P, HEADS])
        ea = one("ea", [P, HEADS])
        ji = one("ji", [P, 2, P], I32)
        jx = one("jx", [P, P], I32)
        jl = one("jl", [P, LEVELS, P], I32)
        lvl = one("lvl", [P, LEVELS, P])
        raw = sb("d_raw", [P, 3, TAPS - 1 + T])
        zin = sb("d_z", [P, T])
        cv = sb("d_cv", [P, 3, T])
        sq = sb("d_sq", [P, 2, T])
        qn, kn, qg = sb("d_qn", [P, T]), sb("d_kn", [P, T]), sb("d_qg", [P, T])
        row_g, row_b = sb("d_row_g", [P, NT, P]), sb("d_row_b", [P, NT, P])
        eg = sb("d_eg", [P, T])
        dt = sb("d_dt", [P, NT, P])
        at = sb("d_at", [P, NT, P])
        qk = sb("d_qk", [P, NT, P])
        X, Y = sb("d_X", [P, NT, P]), sb("d_Y", [P, NT, P])
        blk = [spare[:].rearrange("p t d -> p (t d)")[:, u * D * NT // 2:u * D * NT // 2 + LEVELS * NT * P].rearrange(
            "p (l c t) -> p l c t", l=LEVELS, c=NT) for u in range(2)]
        Pm = sb("d_P", [P, NT, P])
        kd, vb = sb("d_kd", [P, NT, P]), sb("d_vb", [P, NT, P])
        res, vnew, state = sb("d_res", [P, P]), sb("d_vnew", [P, P]), sb("d_state", [P, P])
        names = ("tiles_in", "conv1", "conv_done", "silu_done", "sq_done", "ss_done", "dln_done", "dr_done", "qkn_done",
                 "rows_done", "row_mm", "eg_done", "diff_done", "dt_done", "dtm_done", "dtb_done", "kk_done",
                 "at_done", "atm_done", "qk_done", "L_done", "X0", "Y0a", "Y0", "blk_done", "qg_done", "ktv_done",
                 "kd_done", "vb_done", "P_mm", "P_out", "XY_mm", "X_out", "Y_out", "ks_mm", "res_done", "vn_mm",
                 "vn_done", "su_mm", "state_done", "o_done", "osq_done", "oss_done", "oln_done", "or_done",
                 "on_done", "fin_done", "mh_done", "ml_done")
        m = {n: sem("d_" + n) for n in names}
        par_in, mset, gstep, gmm, lstep, zeroed = (sem1(n) for n in ("gpar_in", "gmset", "gstep", "gmm", "lstep", "zeroed"))
        block = ctx.enter_context(nc.Block())
        ps = s.ps
        PAIRS = HEADS // 2
        LV = range(1, LEVELS)
        QC, KD, VD = 0, 1, 2

        def chunks(ap):
            return ap.rearrange("p (c t) -> p c t", c=NT)

        def half(ap, l, odd):
            return ap.rearrange("p (n two k) -> p n two k", two=2, k=2 ** l)[:, :, odd, :]

        def flat(ap):
            return ap.rearrange("p c t -> p (c t)")

        def packed(ap, l):
            return ap.rearrange("p (n k) -> p n k", k=2 ** l)

        def col(table, head, c):
            return table[:, bass.ds(head, 1), c:c + 1].rearrange("p h c -> p (h c)")

        @block.sync
        def _(sp):
            sp.dma_start(alog[:], io.a_log.broadcast_to([P, HEADS])).then_inc(par_in, 16)
            sp.dma_start(dtb[:], io.dt_bias.broadcast_to([P, HEADS])).then_inc(par_in, 16)
            sp.wait_ge(zeroed, 2)
            with sp.Fori(0, PAIRS) as i:
                for u in range(2):
                    sp.wait_ge(m["conv_done"][u], i * 3 + AHEAD)
                    sp.dma_start(raw[u][:, :, TAPS - 1:], io.proj_gdn[:, :, bass.ds(i * 2 + u, 1), :].rearrange(
                        "p g e t -> p (g e) t")).then_inc(m["tiles_in"][u], 16)
                    sp.wait_ge(m["ml_done"][u], i + AHEAD)
                    sp.dma_start(zin[u][:], io.proj_z[:, bass.ds(i * 2 + u, 1), :].rearrange(
                        "p e t -> p (e t)")).then_inc(m["tiles_in"][u], 16)

        @block.gpsimd
        def _(pool):
            pool.iota(ji[:, 0, :], [[1, P]], base=0, channel_multiplier=0).then_inc(mset, 1)
            pool.iota(ji[:, 1, :], [[0, P]], base=0, channel_multiplier=1).then_inc(mset, 1)
            for u in range(2):
                pool.memset(raw[u][:, :, 0:TAPS - 1], 0.0).then_inc(zeroed, 1)
            pool.wait_ge(gstep, 9)
            pool.wait_ge(lstep, 3)
            with pool.Fori(0, PAIRS) as i:
                for u in range(2):
                    head = i * 2 + u
                    pool.wait_ge(m["row_mm"][u], i + AHEAD)
                    for out, mat, tab in ((row_g[u], s.tri, g), (row_b[u], s.ident, beta)):
                        pool.tensor_tensor(out=out[:], in0=mat[:].unsqueeze(1).broadcast_to([P, NT, P]),
                                           in1=tab[:, bass.ds(head, 1), :].rearrange("p h c -> p (h c)").unsqueeze(
                                               2).broadcast_to([P, NT, P]), op=ALU.mult).then_inc(m["rows_done"][u], 1)
                for u in range(2):
                    pool.wait_ge(m["dt_done"][u], i + 1)
                    pool.tensor_tensor(out=dt[u][:], in0=dt[u][:], in1=s.tri[:].unsqueeze(1).broadcast_to([P, NT, P]),
                                       op=ALU.mult).then_inc(m["dtm_done"][u], 1)
                for u in range(2):
                    pool.wait_ge(m["at_done"][u], i + 1)
                    pool.tensor_tensor(out=at[u][:], in0=at[u][:], in1=s.tri_s[:].unsqueeze(1).broadcast_to([P, NT, P]),
                                       op=ALU.mult).then_inc(m["atm_done"][u], 1)
                for n, l in enumerate(range(LEVELS)):
                    for u in range(2):
                        pool.wait_ge(m["atm_done"][u], i + 1)
                        pool.tensor_tensor(out=blk[u][:, l], in0=at[u][:],
                                           in1=lvl[:, l, :].unsqueeze(1).broadcast_to([P, NT, P]),
                                           op=ALU.mult).then_inc(m["blk_done"][u], 1)
                        if l == 0:
                            pool.wait_ge(m["blk_done"][u], i * LEVELS + 1)
                            pool.tensor_tensor(out=Y[u][:], in0=s.ident[:].unsqueeze(1).broadcast_to([P, NT, P]),
                                               in1=blk[u][:, 0], op=ALU.subtract).then_inc(m["Y0"][u], 1)
                for u in range(2):
                    pool.wait_ge(m["eg_done"][u], i + 1)
                    pool.wait_ge(m["qkn_done"][u], i * 2 + 2)
                    pool.tensor_tensor(out=qg[u][:], in0=qn[u][:], in1=eg[u][:],
                                       op=ALU.mult).then_inc(m["qg_done"][u], 1)

        @block.scalar
        def _(act):
            load_exp_and_ln(nc)
            act.wait_ge(par_in, 32)
            nc.scalar.activation(ea[:], alog[:], ACT.Exp).then_inc(gstep, 1)
            act.wait_ge(mset, 4)
            nc.scalar.activation(gt[2][:], gt[2][:], ACT.Exp).then_inc(gstep, 1)
            act.wait_ge(gstep, 2)
            nc.scalar.activation(gt[2][:], gt[2][:], ACT.Ln, bias=s.one[:]).then_inc(gstep, 1)
            act.wait_ge(gstep, 3)
            nc.scalar.activation(gt[3][:], s.gates[:, :, HEADS:].rearrange("p t h -> p h t"), ACT.Exp,
                                 scale=-1.0).then_inc(gstep, 1)
            act.wait_ge(gmm, 1)
            nc.scalar.activation(nbe[:], ps[:, 0, 0:HEADS * NT].rearrange("p (h c) -> p h c", h=HEADS),
                                 ACT.Exp).then_inc(gstep, 1)
            act.wait_ge(gstep, 8)
            nc.scalar.activation(kds[:], kds[:], ACT.Exp).then_inc(gstep, 1)
            with act.Fori(0, PAIRS) as i:
                for u in range(2):
                    for n in range(3):
                        act.wait_ge(m["conv_done"][u], i * 3 + (n + 1 + AHEAD))
                        nc.scalar.activation(cv[u][:, n, :], cv[u][:, n, :], ACT.Silu).then_inc(m["silu_done"][u], 1)
                for u in range(2):
                    act.wait_ge(m["tiles_in"][u], i * 32 + 32)
                    nc.scalar.activation(zin[u][:], zin[u][:], ACT.Silu).then_inc(m["silu_done"][u], 1)
                load_exp_and_ln(nc)
                for u in range(2):
                    act.wait_ge(m["silu_done"][u], i * 4 + 2)
                    nc.scalar.activation(sq[u][:], cv[u][:, 0:2, :], ACT.Square).then_inc(m["sq_done"][u], 1)
                for u in range(2):
                    b = 4 * u
                    act.wait_ge(m["row_mm"][u], i + 1 + AHEAD)
                    nc.scalar.activation(eg[u][:], ps[:, b, :], ACT.Exp).then_inc(m["eg_done"][u], 1)
                    act.wait_ge(m["ss_done"][u], i + 1)
                    nc.scalar.activation(sq[u][:], ps[:, b + 2:b + 4, :], ACT.Ln, bias=s.eps[:]).then_inc(m["dln_done"][u], 1)
                    act.wait_ge(m["dln_done"][u], i + 1)
                    nc.scalar.activation(sq[u][:], sq[u][:], ACT.Exp, scale=-0.5).then_inc(m["dr_done"][u], 1)
                for u in range(2):
                    act.wait_ge(m["diff_done"][u], i * NT + NT)
                    nc.scalar.activation(dt[u][:], dt[u][:], ACT.Exp).then_inc(m["dt_done"][u], 1)
                for u in range(2):
                    head = i * 2 + u
                    act.wait_ge(m["ktv_done"][u], i + 1)
                    for c in range(NT):
                        nc.scalar.activation(kd[u][:, c, :], chunks(ps[:, 4 * u, :])[:, c, :], ACT.Copy,
                                             scale=col(kds, head, c)).then_inc(m["kd_done"][u], 1)
                    for c in range(NT):
                        nc.scalar.activation(vb[u][:, c, :], chunks(ps[:, 4 * u + 1, :])[:, c, :], ACT.Copy,
                                             scale=col(beta, head, c)).then_inc(m["vb_done"][u], 1)
                for n, l in enumerate(LV):
                    for u in range(2):
                        act.wait_ge(m["P_mm"][u], i * len(LV) + (n + 1))
                        nc.scalar.copy(Pm[u][:], chunks(ps[:, 4 * u + 2, :])).then_inc(m["P_out"][u], 1)
                for c in range(NT):
                    for u in range(2):
                        act.wait_ge(m["vn_mm"][u], i * NT + (c + 1))
                        nc.scalar.copy(vnew[u][:], ps[:, 4 * u + 1, 0:P]).then_inc(m["vn_done"][u], 1)
                for u in range(2):
                    act.wait_ge(m["o_done"][u], i * NT + NT)
                    nc.scalar.activation(sq[u][:, 0, :], ps[:, 4 * u + 3, :], ACT.Square).then_inc(m["osq_done"][u], 1)
                for u in range(2):
                    act.wait_ge(m["oss_done"][u], i + 1)
                    nc.scalar.activation(sq[u][:, 1, :], ps[:, 4 * u, :], ACT.Ln, scale=1.0 / P,
                                         bias=s.eps[:]).then_inc(m["oln_done"][u], 1)
                    act.wait_ge(m["oln_done"][u], i + 1)
                    nc.scalar.activation(sq[u][:, 1, :], sq[u][:, 1, :], ACT.Exp, scale=-0.5).then_inc(m["or_done"][u], 1)
                for u in range(2):
                    act.wait_ge(m["fin_done"][u], i + 1 + AHEAD)
                    nc.scalar.copy(mix_hi[:, bass.ds(i * 2 + (HEADS + u), 1), :].rearrange("p e t -> p (e t)"),
                                   zin[u][:]).then_inc(m["mh_done"][u], 1)

        @block.vector
        def _(dve):
            a_in = s.gates[:, :, 0:HEADS].rearrange("p t h -> p h t")
            dve.wait_ge(par_in, 32)
            nc.vector.tensor_tensor(gt[1][:], a_in, dtb[:].unsqueeze(2).broadcast_to([P, HEADS, NT]),
                                    ALU.add).then_inc(lstep, 1)
            dve.wait_ge(lstep, 1)
            dve.wait_ge(mset, 2)
            nc.vector.tensor_scalar(gt[0][:], gt[1][:], 0.0, None, ALU.max).then_inc(mset, 1)
            dve.wait_ge(mset, 3)
            nc.vector.scalar_tensor_tensor(out=gt[2][:], in0=gt[0][:], scalar=-2.0, in1=gt[1][:], op0=ALU.mult,
                                           op1=ALU.add).then_inc(mset, 1)
            nc.vector.tensor_tensor(jx[:], ji[:, 0, :], ji[:, 1, :], ALU.bitwise_xor).then_inc(lstep, 1)
            dve.wait_ge(gstep, 4)
            nc.vector.tensor_tensor(gt[0][:], gt[0][:], gt[2][:], ALU.add).then_inc(mset, 1)
            nc.vector.tensor_scalar(gt[3][:], gt[3][:], 1.0, None, ALU.add).then_inc(mset, 1)
            dve.wait_ge(mset, 6)
            nc.vector.scalar_tensor_tensor(out=g[:], in0=gt[0][:], scalar=-1.0,
                                           in1=ea[:].unsqueeze(2).broadcast_to([P, HEADS, NT]), op0=ALU.mult,
                                           op1=ALU.mult).then_inc(gstep, 1)
            nc.vector.reciprocal(beta[:], gt[3][:]).then_inc(gstep, 1)
            dve.wait_ge(gmm, 1)
            dve.wait_ge(gstep, 7)
            nc.vector.tensor_copy(gcc[:], ps[:, 0, 0:HEADS * NT].rearrange("p (h c) -> p h c", h=HEADS)).then_inc(mset, 1)
            dve.wait_ge(mset, 7)
            nc.vector.tensor_tensor(kds[:], ps[:, 1, 0:HEADS * NT].rearrange("p (h c) -> p h c", h=HEADS), gcc[:],
                                    ALU.subtract)
            nc.vector.scalar_tensor_tensor(out=nbe[:], in0=nbe[:], scalar=-1.0, in1=beta[:], op0=ALU.mult,
                                           op1=ALU.mult).then_inc(gstep, 1)
            dve.wait_ge(lstep, 2)
            for l in range(LEVELS):
                nc.vector.tensor_single_scalar(jl[:, l, :], jx[:], l, ALU.logical_shift_right).then_inc(mset, 1)
            dve.wait_ge(mset, 7 + LEVELS)
            nc.vector.tensor_scalar(lvl[:], jl[:], 1.0, None, ALU.is_equal).then_inc(lstep, 1)
            dve.wait_ge(lstep, 3)
            for u in range(2):
                for ahead in ("conv_done", "fin_done", "ml_done"):
                    dve.sem_inc(m[ahead][u], AHEAD)
            with dve.Fori(0, PAIRS) as i:
                for u in range(2):
                    head = i * 2 + u
                    dve.wait_ge(m["tiles_in"][u], i * 32 + 32)
                    for k in range(TAPS):
                        for n in range(3):
                            tap = s.par[:, bass.ds(head + (C_CONV + 3 * HEADS * k + HEADS * n), 1)]
                            src = raw[u][:, n, k:k + T]
                            out = cv[u][:, n, :]
                            if k == 0:
                                nc.vector.tensor_scalar(out, src, tap, None, ALU.mult).then_inc(m["conv1"][u], 1)
                            else:
                                dve.wait_ge(m["conv1"][u], i * 9 + (3 * (k - 1) + n + 1))
                                nc.vector.scalar_tensor_tensor(
                                    out=out, in0=src, scalar=tap, in1=out, op0=ALU.mult, op1=ALU.add).then_inc(
                                        m["conv_done" if k == TAPS - 1 else "conv1"][u], 1)
                for u in range(2):
                    head = i * 2 + u
                    dve.wait_ge(m["row_mm"][u], i + 1 + AHEAD)
                    dve.wait_ge(m["eg_done"][u], i + 1)
                    for c in range(NT):
                        nc.vector.tensor_scalar(dt[u][:, c, :], chunks(ps[:, 4 * u, :])[:, c, :], col(gcc, head, c),
                                                0.0, ALU.subtract, ALU.min).then_inc(m["diff_done"][u], 1)
                for u in range(2):
                    dve.wait_ge(m["dr_done"][u], i + 1)
                    nc.vector.scalar_tensor_tensor(out=qn[u][:], in0=cv[u][:, 0, :], scalar=P ** -0.5,
                                                   in1=sq[u][:, 0, :], op0=ALU.mult,
                                                   op1=ALU.mult).then_inc(m["qkn_done"][u], 1)
                    nc.vector.tensor_tensor(kn[u][:], cv[u][:, 1, :], sq[u][:, 1, :],
                                            ALU.mult).then_inc(m["qkn_done"][u], 1)
                for u in range(2):
                    b = 4 * u
                    dve.wait_ge(m["dtm_done"][u], i + 1)
                    dve.wait_ge(m["row_mm"][u], i + 1 + AHEAD)
                    nc.vector.tensor_tensor(at[u][:], dt[u][:], chunks(ps[:, b + 1, :]), ALU.mult).then_inc(m["dtb_done"][u], 1)
                    dve.wait_ge(m["kk_done"][u], i + 1)
                    dve.wait_ge(m["dtb_done"][u], i + 1)
                    nc.vector.tensor_tensor(at[u][:], at[u][:], chunks(ps[:, b + 2, :]), ALU.mult).then_inc(m["at_done"][u], 1)
                    nc.vector.tensor_tensor(qk[u][:], dt[u][:], chunks(ps[:, b + 3, :]), ALU.mult).then_inc(m["qk_done"][u], 1)
                for u in range(2):
                    dve.wait_ge(m["L_done"][u], i + 1)
                    nc.vector.scalar_tensor_tensor(out=X[u][:], in0=chunks(ps[:, 4 * u + 2, :]), scalar=-1.0,
                                                   in1=lvl[:, 0, :].unsqueeze(1).broadcast_to([P, NT, P]),
                                                   op0=ALU.mult, op1=ALU.mult).then_inc(m["X0"][u], 1)
                for u in range(2):
                    dve.wait_ge(m["X0"][u], i * 2 + 1)
                    nc.vector.tensor_tensor(X[u][:], X[u][:], s.ident[:].unsqueeze(1).broadcast_to([P, NT, P]),
                                            ALU.add).then_inc(m["X0"][u], 1)
                for n, l in enumerate(LV):
                    for u in range(2):
                        b = 4 * u
                        dve.wait_ge(m["XY_mm"][u], i * len(LV) + (n + 1))
                        if l < LEVELS - 1:
                            at_ = half(flat(X[u][:]), l, 0)
                            nc.vector.tensor_tensor(at_, at_, packed(ps[:, b + 3, 0:T // 2], l), ALU.subtract).then_inc(m["X_out"][u], 1)
                        at_ = half(flat(Y[u][:]), l, 1)
                        nc.vector.tensor_tensor(at_, at_, packed(ps[:, b + 2, 0:T // 2], l), ALU.subtract).then_inc(m["Y_out"][u], 1)
                for c in range(NT):
                    for u in range(2):
                        head = i * 2 + u
                        if c:
                            dve.wait_ge(m["ks_mm"][u], i * (NT - 1) + c)
                            dve.wait_ge(m["vb_done"][u], i * NT + NT)
                            nc.vector.scalar_tensor_tensor(out=res[u][:], in0=ps[:, 4 * u, 0:P], scalar=col(nbe, head, c),
                                                           in1=vb[u][:, c, :], op0=ALU.mult,
                                                           op1=ALU.add).then_inc(m["res_done"][u], 1)
                    for u in range(2):
                        if c < NT - 1:
                            dve.wait_ge(m["su_mm"][u], i * (NT - 1) + (c + 1))
                            if c == 0:
                                nc.vector.tensor_copy(state[u][:], ps[:, 4 * u + 2, 0:P]).then_inc(m["state_done"][u], 1)
                            else:
                                dve.wait_ge(m["state_done"][u], i * (NT - 1) + c)
                                last = (c + 1) * P - 1
                                nc.vector.scalar_tensor_tensor(out=state[u][:], in0=state[u][:],
                                                               scalar=eg[u][:, last:last + 1],
                                                               in1=ps[:, 4 * u + 2, 0:P], op0=ALU.mult,
                                                               op1=ALU.add).then_inc(m["state_done"][u], 1)
                for u in range(2):
                    dve.wait_ge(m["or_done"][u], i + 1)
                    nc.vector.scalar_tensor_tensor(out=sq[u][:, 0, :], in0=ps[:, 4 * u + 3, :], scalar=s.wn[:, 2:3],
                                                   in1=sq[u][:, 1, :], op0=ALU.mult, op1=ALU.mult).then_inc(m["on_done"][u], 1)
                for u in range(2):
                    dve.wait_ge(m["on_done"][u], i + 1)
                    nc.vector.tensor_tensor(zin[u][:], sq[u][:, 0, :], zin[u][:], ALU.mult).then_inc(m["fin_done"][u], 1)
                for u in range(2):
                    at_ = bass.ds(i * 2 + (HEADS + u), 1)
                    dve.wait_ge(m["mh_done"][u], i + 1)
                    nc.vector.tensor_tensor(mix_lo[:, at_, :].rearrange("p e t -> p (e t)"), zin[u][:],
                                            mix_hi[:, at_, :].rearrange("p e t -> p (e t)").bitcast(F32),
                                            ALU.subtract).then_inc(m["ml_done"][u], 1)

        @block.tensor
        def _(pe):
            pe.wait_ge(gstep, 6)
            nc.tensor.matmul(ps[:, 0, 0:HEADS * NT], s.tri[:], g[:].rearrange("p h c -> p (h c)"), start=True, stop=True)
            nc.tensor.matmul(ps[:, 1, 0:HEADS * NT], s.ones[:], g[:].rearrange("p h c -> p (h c)"), start=True,
                             stop=True).then_inc(gmm, 1)
            pe.wait_ge(gstep, 8)

            def cols(c):
                return slice(c * P, (c + 1) * P)

            def halves(c):
                return slice(c * P // 2, (c + 1) * P // 2)

            for u in range(2):
                pe.sem_inc(m["row_mm"][u], AHEAD)
            with pe.Fori(0, PAIRS) as i:
                for u in range(2):
                    b = 4 * u
                    pe.wait_ge(m["fin_done"][u], i + AHEAD)
                    pe.wait_ge(m["rows_done"][u], i * 2 + 2)
                    nc.tensor.matmul(ps[:, b, :], s.ones[:], row_g[u][:].rearrange("p c t -> p (c t)"), start=True, stop=True)
                    nc.tensor.matmul(ps[:, b + 1, :], s.ones[:], row_b[u][:].rearrange("p c t -> p (c t)"), start=True,
                                     stop=True).then_inc(m["row_mm"][u], 1)
                for u in range(2):
                    pe.wait_ge(m["sq_done"][u], i + 1)
                    for n in range(2):
                        mm = nc.tensor.matmul(ps[:, 4 * u + 2 + n, :], s.ones[:], sq[u][:, n, :], start=True, stop=True)
                    mm.then_inc(m["ss_done"][u], 1)
                for u in range(2):
                    b = 4 * u
                    pe.wait_ge(m["qkn_done"][u], i * 2 + 2)
                    for c in range(NT):
                        nc.tensor.matmul(ps[:, b + 2, cols(c)], kn[u][:, cols(c)], kn[u][:, cols(c)], start=True, stop=True)
                        mm = nc.tensor.matmul(ps[:, b + 3, cols(c)], kn[u][:, cols(c)], qn[u][:, cols(c)], start=True, stop=True)
                    mm.then_inc(m["kk_done"][u], 1)
                for u in range(2):
                    b = 4 * u
                    pe.wait_ge(m["diff_done"][u], i * NT + NT)
                    for c in range(NT):
                        nc.tensor.transpose(ps[:, b, cols(c)], kn[u][:, cols(c)], s.ident[:])
                    pe.wait_ge(m["dtb_done"][u], i + 1)
                    pe.wait_ge(m["silu_done"][u], i * 4 + 4)
                    for c in range(NT):
                        tp = nc.tensor.transpose(ps[:, b + 1, cols(c)], cv[u][:, 2, cols(c)], s.ident[:])
                    tp.then_inc(m["ktv_done"][u], 1)
                for u in range(2):
                    pe.wait_ge(m["atm_done"][u], i + 1)
                    for c in range(NT):
                        tp = nc.tensor.transpose(ps[:, 4 * u + 2, cols(c)], at[u][:, c, :], s.ident[:])
                    tp.then_inc(m["L_done"][u], 1)
                for n, l in enumerate(LV):
                    for u in range(2):
                        if n == 0:
                            pe.wait_ge(m["X0"][u], i * 2 + 2)
                            pe.wait_ge(m["Y0"][u], i + 1)
                            pe.wait_ge(m["qk_done"][u], i + 1)
                        else:
                            pe.wait_ge(m["X_out"][u], i * (len(LV) - 1) + n)
                            pe.wait_ge(m["Y_out"][u], i * len(LV) + n)
                        pe.wait_ge(m["blk_done"][u], i * LEVELS + (l + 1))
                        for c in range(NT):
                            mm = nc.tensor.matmul(ps[:, 4 * u + 2, cols(c)], blk[u][:, l, c, :], X[u][:, c, :], start=True, stop=True)
                        mm.then_inc(m["P_mm"][u], 1)
                    for u in range(2):
                        pe.wait_ge(m["P_out"][u], i * len(LV) + (n + 1))
                        for c in range(NT):
                            if l < LEVELS - 1:
                                nc.tensor.matmul(ps[:, 4 * u + 3, halves(c)], Y[u][:, c, :], half(Pm[u][:, c, :], l, 0),
                                                 start=True, stop=True)
                            mm = nc.tensor.matmul(ps[:, 4 * u + 2, halves(c)], Pm[u][:, c, :], half(Y[u][:, c, :], l, 1),
                                                  start=True, stop=True)
                        mm.then_inc(m["XY_mm"][u], 1)
                for c in range(NT):
                    if c:
                        for u in range(2):
                            pe.wait_ge(m["state_done"][u], i * (NT - 1) + c)
                            pe.wait_ge(m["kd_done"][u], i * NT + NT)
                            nc.tensor.matmul(ps[:, 4 * u, 0:P], kn[u][:, cols(c)], state[u][:], start=True,
                                             stop=True).then_inc(m["ks_mm"][u], 1)
                    for u in range(2):
                        if c == 0:
                            pe.wait_ge(m["Y_out"][u], i * len(LV) + len(LV))
                            pe.wait_ge(m["vb_done"][u], i * NT + NT)
                            right = vb[u][:, 0, :]
                        else:
                            pe.wait_ge(m["res_done"][u], i * (NT - 1) + c)
                            right = res[u][:]
                        nc.tensor.matmul(ps[:, 4 * u + 1, 0:P], Y[u][:, c, :], right, start=True, stop=True).then_inc(m["vn_mm"][u], 1)
                    for u in range(2):
                        pe.wait_ge(m["vn_done"][u], i * NT + (c + 1))
                        out = ps[:, 4 * u + 3, cols(c)]
                        mm = nc.tensor.matmul(out, vnew[u][:], qk[u][:, c, :], start=True, stop=c == 0)
                        if c:
                            pe.wait_ge(m["qg_done"][u], i + 1)
                            mm = nc.tensor.matmul(out, state[u][:], qg[u][:, cols(c)], start=False, stop=True)
                        mm.then_inc(m["o_done"][u], 1)
                        if c < NT - 1:
                            pe.wait_ge(m["kd_done"][u], i * NT + NT)
                            nc.tensor.matmul(ps[:, 4 * u + 2, 0:P], kd[u][:, c, :], vnew[u][:], start=True,
                                             stop=True).then_inc(m["su_mm"][u], 1)
                for u in range(2):
                    pe.wait_ge(m["osq_done"][u], i + 1)
                    nc.tensor.matmul(ps[:, 4 * u, :], s.ones[:], sq[u][:, 0, :], start=True, stop=True).then_inc(m["oss_done"][u], 1)


def out_proj_stage(nc, s, io, mix_hi, mix_lo, x2):
    with ExitStack() as ctx:
        def sb(name, shape, dt=F32):
            return ctx.enter_context(nc.sbuf_tensor(name, shape, dt))

        sem = ctx.enter_context(Semaphores(nc))
        raw = sb("o_raw", [P, RAW, KC, GRP])
        hi = sb("o_hi", [P, 2, KC, GRP], F32R)
        lo = sb("o_lo", [P, 2, KC, GRP], F32R)
        x_in = sem("ox_in")
        raw_in = [sem(f"ow_in{n}") for n in range(RAW)]
        hi_done = sem("ow_hi")
        lo_done = [sem(f"ow_lo{n}") for n in range(RAW)]
        mm_done = [sem(f"ow_mm{n}") for n in range(2)]
        added = [sem(f"o_added{n}") for n in range(2)]
        block = ctx.enter_context(nc.Block())
        ps = s.ps
        CH = KT // KC
        BODY = 2 * CH
        PAIRS = D // GRP // 2

        @block.sync
        def _(sp):
            sp.dma_start(x2[:], io.x.rearrange("(t p) d -> p t d", p=P)).then_inc(x_in, 16)
            with sp.Fori(0, PAIRS) as pair:
                for ch in range(BODY):
                    sp.wait_ge(lo_done[ch % RAW], pair * (BODY // RAW) + (ch // RAW + AHEAD))
                    sp.dma_start(raw[:, ch % RAW], io.w_o_v[:, ch % CH * KC:(ch % CH + 1) * KC, bass.ds(
                        pair * (2 * GRP) + ch // CH * GRP, GRP)]).then_inc(raw_in[ch % RAW], 16)

        @block.scalar
        def _(act):
            with act.Fori(0, PAIRS) as pair:
                for ch in range(BODY):
                    act.wait_ge(raw_in[ch % RAW], pair * (16 * BODY // RAW) + 16 * (ch // RAW + 1))
                    act.wait_ge(mm_done[ch % 2], pair * (BODY // 2) + (ch // 2 + AHEAD))
                    nc.scalar.copy(hi[:, ch % 2], raw[:, ch % RAW]).then_inc(hi_done, 1)

        @block.vector
        def _(dve):
            for ahead in (*lo_done, *added):
                dve.sem_inc(ahead, AHEAD)
            with dve.Fori(0, PAIRS) as pair:
                for ch in range(BODY):
                    dve.wait_ge(hi_done, pair * BODY + (ch + 1))
                    nc.vector.tensor_tensor(lo[:, ch % 2], raw[:, ch % RAW], hi[:, ch % 2].bitcast(F32),
                                            ALU.subtract).then_inc(lo_done[ch % RAW], 1)
                for g in range(2):
                    dve.wait_ge(mm_done[1], pair * (BODY // 2) + ((g + 1) * CH // 2 + AHEAD))
                    if g == 0:
                        dve.wait_ge(x_in, 16)
                    at = x2[:, :, bass.ds(pair * (2 * GRP) + g * GRP, GRP)]
                    nc.vector.tensor_tensor(at, ps[:, 4 * g:4 * g + 4, :], at, ALU.add).then_inc(added[g], 1)

        @block.tensor
        def _(pe):
            for ahead in mm_done:
                pe.sem_inc(ahead, AHEAD)
            with pe.Fori(0, PAIRS) as pair:
                for ch in range(BODY):
                    g, c = ch // CH, ch % CH
                    if c == 0:
                        pe.wait_ge(added[g], pair + AHEAD)
                    pe.wait_ge(lo_done[ch % RAW], pair * (BODY // RAW) + (ch // RAW + 1 + AHEAD))
                    for t in range(NT):
                        out, tok = ps[:, 4 * g + t, :], slice(t * P, (t + 1) * P)
                        for k in range(KC):
                            kt = c * KC + k
                            nc.tensor.matmul(out, mix_hi[:, kt, tok], hi[:, ch % 2, k], start=kt == 0, stop=False)
                            nc.tensor.matmul(out, mix_lo[:, kt, tok], hi[:, ch % 2, k], start=False, stop=False)
                            mm = nc.tensor.matmul(out, mix_hi[:, kt, tok], lo[:, ch % 2, k], start=False,
                                                  stop=kt == KT - 1)
                    mm.then_inc(mm_done[ch % 2], 1)


def route_stage(nc, s, io, x2, tab_pos, tab_val, items):
    NL = NG + NE
    with ExitStack() as ctx:
        def sb(name, shape, dt=F32):
            return ctx.enter_context(nc.sbuf_tensor(name, shape, dt))

        sem = ctx.enter_context(Semaphores(nc))
        xn = sb("xn", [P, NT, D])
        h2T = sb("h2T", [P, KT, T])
        wr = sb("wr", [P, KT, NL])
        bias = sb("bias", [P, NL])
        sq = sb("r_sq", [P, D])
        w2row = sb("w2row", [P, D])
        st = [sb(f"r_st{n}", [P, NT]) for n in range(4)]
        lg = sb("r_lg", [P, NT, NL])
        gmx, gsum, gg = sb("gmx", [P, NT]), sb("gsum", [P, NT]), sb("gg", [P, NT])
        gd, gsc, goh = sb("gd", [P, NT, NG]), sb("gsc", [P, NT, NG]), sb("goh", [P, NT, NG])
        picked = sb("picked", [P, NT, NG, PER])
        inl = sb("inl", [P, NT, PER])
        ex = [sb(f"r_ex{n}", [P, NT, PER]) for n in range(2)]
        esc = sb("esc", [P, NT, PER])
        eoh = [sb(f"eoh{n}", [P, NT, PER]) for n in range(2)]
        emx = [sb(f"emx{n}", [P, NT]) for n in range(2)]
        smx = sb("smx", [P, NT])
        gate = [sb(f"gate{n}", [P, NT]) for n in range(2)]
        den = sb("den", [P, NT])
        M = [sb(f"M{n}", [P, NT, NE]) for n in range(3)]
        gm = [sb(f"gm{n}", [P, NT, NE]) for n in range(2)]
        posm = sb("posm", [P, NT, NE])
        desc = sb("desc", [P, PER])
        tok = sb("tok", [P, NT])
        cnt = sb("cnt", [P, NE])
        NX = (BLKS - 1) * NE
        xcode, xexp = sb("xcode", [1, NX]), sb("xexp", [1, NX])
        kk, two = sb("kk", [1, EXTRA + 1]), sb("two", [1, NG])
        flag, rank, onesr = sb("flag", [1, NX]), sb("rank", [1, NX]), sb("onesr", [1, NX])
        fc = sb("fc", [1, 2, NX])
        hit = sb("hit", [1, EXTRA + 1, NX])
        hv = sb("hv", [1, EXTRA + 1, NX])
        xt = sb("xt", [1, 2, EXTRA + 1])
        np_ = sb("np_", [1, NG])
        npair = sb("npair", [1, 1])
        itf = sb("itf", [1, 2, N_ITEMS + 2])

        w_in, norm_in, init = sem("rw_in"), sem("r_norm_in"), sem("r_init")
        ssq, msd, recd, rstdd, xnd, stored = (sem(n) for n in ("r_ssq", "r_ms", "r_rec", "r_rstd", "r_xn", "r_stored"))
        tpd, h2d, lgm, act_exp, chain = (sem(n) for n in ("r_tp", "r_h2", "r_lgm", "r_exp", "r_chain"))
        m_done, pos_mm = sem("m_done"), sem("pos_mm")
        block = ctx.enter_context(nc.Block())
        ps = s.ps

        @block.sync
        def _(sp):
            sp.dma_start(wr[:, :, 0:NG], io.w_group.rearrange("(k p) n -> p k n", p=P)).then_inc(w_in, 16)
            sp.dma_start(wr[:, :, NG:NL], io.w_expert.rearrange("(k p) n -> p k n", p=P)).then_inc(w_in, 16)
            sp.dma_start(bias[:, 0:NG], io.b_group.broadcast_to([P, NG])).then_inc(w_in, 16)
            sp.dma_start(bias[:, NG:NL], io.b_expert.broadcast_to([P, NE])).then_inc(w_in, 16)
            sp.dma_start(w2row[:], io.norm2_row.broadcast_to([P, D])).then_inc(norm_in, 16)
            for t in range(NT):
                sp.wait_ge(xnd, t + 1)
                sp.dma_start(io.xn[t * P:(t + 1) * P, :], xn[:, t, :]).then_inc(stored, 16)
            sp.wait_ge(stored, NT * 16)

        @block.gpsimd
        def _(pool):
            fl = dict(allow_small_or_imprecise_dtypes=True)
            pool.iota(desc[:], [[-1, PER]], base=PER, channel_multiplier=0, **fl).then_inc(init, 1)
            pool.iota(tok[:], [[P, NT]], base=-int(BIG), channel_multiplier=1, **fl).then_inc(init, 1)
            pool.iota(xcode[:], [[1, NX]], base=NE - PAD_CODE, channel_multiplier=0, **fl).then_inc(init, 1)
            pool.iota(xexp[:], [[0, BLKS - 1], [1, NE]], base=0, channel_multiplier=0, **fl).then_inc(init, 1)
            pool.iota(kk[:], [[1, EXTRA + 1]], base=1, channel_multiplier=0, **fl).then_inc(init, 1)
            pool.iota(two[:], [[2, NG]], base=0, channel_multiplier=0, **fl).then_inc(init, 1)
            pool.iota(itf[:], [[0, 2], [1, N_ITEMS + 2]], base=0, channel_multiplier=0, **fl).then_inc(init, 1)
            pool.iota(s.slot[:], [[1, P]], base=0, channel_multiplier=0, **fl).then_inc(init, 1)
            pool.memset(onesr[:], 1.0).then_inc(init, 1)
            pool.memset(tab_pos[:, PAD_CODE, :], -1.0).then_inc(init, 1)
            pool.memset(tab_val[:, PAD_CODE], 0.0).then_inc(init, 1)

        @block.scalar
        def _(act):
            for t in range(NT):
                if t:
                    act.wait_ge(ssq, t)
                nc.scalar.activation(sq[:], x2[:, t, :], ACT.Square, accum_out=st[0][:, t:t + 1]).then_inc(ssq, 1)
            act.wait_ge(recd, 1)
            nc.scalar.activation(st[3][:], st[2][:], ACT.Sqrt).then_inc(rstdd, 1)
            for k in range(KT):
                act.wait_ge(tpd, k + 1)
                nc.scalar.copy(h2T[:, k, :], ps[:, 2 + k % 4, :]).then_inc(h2d, 1)
            act.wait_ge(chain, 3)
            nc.scalar.activation(gsc[:], gd[:], ACT.Exp).then_inc(act_exp, 1)
            act.wait_ge(chain, 11)
            nc.scalar.activation(ex[0][:], inl[:], ACT.Exp).then_inc(act_exp, 1)

        @block.vector
        def _(dve):
            count = [0]

            def step(ins):
                count[0] += 1
                ins.then_inc(chain, 1)
                dve.wait_ge(chain, count[0])

            def wide(ap, n):
                return ap.unsqueeze(2).broadcast_to([P, NT, n])

            def first_max(values, peak, score, onehot, n):
                step(nc.vector.tensor_reduce(peak[:], values[:], AX.X, ALU.max))
                step(nc.vector.tensor_tensor(score[:], values[:], wide(peak[:], n), ALU.is_equal))
                step(nc.vector.tensor_tensor(score[:], score[:], desc[:, PER - n:].unsqueeze(1).broadcast_to([P, NT, n]),
                                             ALU.mult))
                step(nc.vector.tensor_reduce(smx[:], score[:], AX.X, ALU.max))
                step(nc.vector.tensor_tensor(onehot[:], score[:], wide(smx[:], n), ALU.is_equal))

            dve.wait_ge(ssq, NT)
            nc.vector.tensor_scalar(st[1][:], st[0][:], 1.0 / D, EPS, ALU.mult, ALU.add).then_inc(msd, 1)
            dve.wait_ge(msd, 1)
            nc.vector.reciprocal(st[2][:], st[1][:]).then_inc(recd, 1)
            dve.wait_ge(rstdd, 1)
            dve.wait_ge(norm_in, 16)
            for t in range(NT):
                nc.vector.scalar_tensor_tensor(out=xn[:, t, :], in0=x2[:, t, :], scalar=st[3][:, t:t + 1], in1=w2row[:],
                                               op0=ALU.mult, op1=ALU.mult).then_inc(xnd, 1)
            dve.wait_ge(init, 11)
            dve.wait_ge(lgm, 1)
            step(nc.vector.tensor_tensor(lg[:], ps[:, 0, 0:NT * NL].rearrange("p (t n) -> p t n", t=NT),
                                         bias[:].unsqueeze(1).broadcast_to([P, NT, NL]), ALU.add))
            step(nc.vector.tensor_reduce(gmx[:], lg[:, :, 0:NG], AX.X, ALU.max))
            step(nc.vector.tensor_tensor(gd[:], lg[:, :, 0:NG], wide(gmx[:], NG), ALU.subtract))
            dve.wait_ge(act_exp, 1)
            step(nc.vector.tensor_reduce(gsum[:], gsc[:], AX.X, ALU.add))
            step(nc.vector.reciprocal(gg[:], gsum[:]))
            step(nc.vector.tensor_scalar(gsc[:], gd[:], 0.0, None, ALU.is_equal))
            step(nc.vector.tensor_tensor(gsc[:], gsc[:], desc[:, PER - NG:].unsqueeze(1).broadcast_to([P, NT, NG]),
                                         ALU.mult))
            step(nc.vector.tensor_reduce(smx[:], gsc[:], AX.X, ALU.max))
            step(nc.vector.tensor_tensor(goh[:], gsc[:], wide(smx[:], NG), ALU.is_equal))
            for t in range(NT):
                ins = nc.vector.tensor_tensor(picked[:, t], lg[:, t, NG:NL].rearrange("p (g e) -> p g e", g=NG),
                                              goh[:, t].unsqueeze(2).broadcast_to([P, NG, PER]), ALU.mult)
            ins.then_inc(m_done, 1)
            dve.wait_ge(m_done, 1)
            step(nc.vector.tensor_reduce(inl[:], picked[:].rearrange("p t g e -> p t e g"), AX.X, ALU.add))
            ins = nc.vector.tensor_reduce(emx[0][:], inl[:], AX.X, ALU.max)
            ins.then_inc(m_done, 1)
            dve.wait_ge(m_done, 2)
            step(nc.vector.tensor_tensor(inl[:], inl[:], wide(emx[0][:], PER), ALU.subtract))
            dve.wait_ge(act_exp, 2)
            first_max(ex[0], emx[0], esc, eoh[0], PER)
            step(nc.vector.scalar_tensor_tensor(out=ex[1][:], in0=eoh[0][:], scalar=-2.0, in1=ex[0][:], op0=ALU.mult,
                                                op1=ALU.add))
            first_max(ex[1], emx[1], esc, eoh[1], PER)
            step(nc.vector.tensor_tensor(den[:], emx[0][:], emx[1][:], ALU.add))
            step(nc.vector.reciprocal(den[:], den[:]))
            step(nc.vector.tensor_tensor(den[:], den[:], gg[:], ALU.mult))
            for n in range(2):
                step(nc.vector.tensor_tensor(gate[n][:], den[:], emx[n][:], ALU.mult))
                for t in range(NT):
                    ins = nc.vector.tensor_tensor(M[n][:, t, :].rearrange("p (g e) -> p g e", g=NG),
                                                  goh[:, t].unsqueeze(2).broadcast_to([P, NG, PER]),
                                                  eoh[n][:, t].unsqueeze(1).broadcast_to([P, NG, PER]), ALU.mult)
                step(ins)
            nc.vector.tensor_tensor(M[2][:], M[0][:], M[1][:], ALU.add).then_inc(m_done, 1)
            val = tab_val[:, 0:NE].rearrange("p e t v -> p t e v")
            for n in range(2):
                step(nc.vector.tensor_tensor(gm[n][:], M[n][:], wide(gate[n][:], NE), ALU.mult))
            nc.vector.memset(val[:, :, :, 3], 0.0)
            step(nc.vector.tensor_tensor(val[:, :, :, 2], gm[0][:], gm[1][:], ALU.add))
            step(nc.vector.tensor_copy(val[:, :, :, 0], wide(tok[:], NE)))
            step(nc.vector.scalar_tensor_tensor(out=val[:, :, :, 1], in0=M[1][:], scalar=float(T), in1=wide(tok[:], NE),
                                                op0=ALU.mult, op1=ALU.add))
            for b in range(1, BLKS):
                ins = nc.vector.tensor_copy(tab_val[:, b * NE:(b + 1) * NE], tab_val[:, 0:NE])
            step(ins)
            dve.wait_ge(pos_mm, 1)
            step(nc.vector.scalar_tensor_tensor(out=posm[:], in0=ps[:, 0, 0:NT * NE].rearrange("p (t e) -> p t e", t=NT),
                                                scalar=1.0, in1=M[2][:], op0=ALU.add, op1=ALU.mult))
            for b in range(BLKS):
                ins = nc.vector.tensor_scalar(tab_pos[:, b * NE:(b + 1) * NE, :], posm[:].rearrange("p t e -> p e t"),
                                              -1.0 - P * b, None, ALU.add)
            step(ins)
            step(nc.vector.tensor_copy(cnt[:], ps[:, 1, 0:NE]))
            for b in range(1, BLKS):
                ins = nc.vector.tensor_scalar(flag[:, (b - 1) * NE:b * NE], cnt[0:1, :], float(P * b), None, ALU.is_gt)
            step(ins)
            step(nc.vector.tensor_tensor_scan(rank[:], onesr[:], flag[:], 0.0, ALU.mult, ALU.add))
            step(nc.vector.tensor_tensor(fc[:, 0], flag[:], xcode[:], ALU.mult))
            step(nc.vector.tensor_tensor(fc[:, 1], flag[:], xexp[:], ALU.mult))
            big = [1, EXTRA + 1, NX]
            step(nc.vector.tensor_tensor(hit[:], rank[:].unsqueeze(1).broadcast_to(big), kk[:].unsqueeze(2).broadcast_to(big),
                                         ALU.is_equal))
            for n in range(2):
                step(nc.vector.tensor_tensor(hv[:], hit[:], fc[:, n].unsqueeze(1).broadcast_to(big), ALU.mult))
                step(nc.vector.tensor_reduce(xt[:, n], hv[:], AX.X, ALU.add))
            step(nc.vector.tensor_scalar(itf[:, 0, NE:NE + EXTRA + 1], xt[:, 0], float(PAD_CODE), None, ALU.add))
            nc.vector.memset(itf[:, 0, N_ITEMS:], float(PAD_CODE))
            nc.vector.memset(itf[:, 1, N_ITEMS:], 0.0)
            step(nc.vector.tensor_copy(itf[:, 1, NE:NE + EXTRA + 1], xt[:, 1]))
            step(nc.vector.tensor_tensor(np_[:], rank[:, NX - 1:NX].broadcast_to([1, NG]), two[:], ALU.is_gt))
            step(nc.vector.tensor_reduce(npair[:], np_[:], AX.X, ALU.add))
            nc.vector.tensor_scalar(items[:, 2, 0:1], npair[:], float(NE // 2), None, ALU.add)
            step(nc.vector.tensor_copy(items[:, 0:2, :], itf[:]))

        @block.tensor
        def _(pe):
            pe.wait_ge(xnd, NT)
            for k in range(KT):
                if k >= 4:
                    pe.wait_ge(h2d, k - 3)
                for t in range(NT):
                    tp = nc.tensor.transpose(ps[:, 2 + k % 4, t * P:(t + 1) * P], xn[:, t, k * P:(k + 1) * P], s.ident[:])
                tp.then_inc(tpd, 1)
            pe.wait_ge(h2d, KT)
            pe.wait_ge(w_in, 64)
            for t in range(NT):
                for k in range(KT):
                    mm = nc.tensor.matmul(ps[:, 0, t * NL:(t + 1) * NL], h2T[:, k, t * P:(t + 1) * P], wr[:, k, :],
                                          start=k == 0, stop=k == KT - 1)
            mm.then_inc(lgm, 1)
            pe.wait_ge(m_done, 3)
            for t in range(NT):
                for t2 in range(t + 1):
                    nc.tensor.matmul(ps[:, 0, t * NE:(t + 1) * NE], (s.tri_s if t2 == t else s.ones)[:], M[2][:, t2, :],
                                     start=t2 == 0, stop=t2 == t)
            for t in range(NT):
                mm = nc.tensor.matmul(ps[:, 1, 0:NE], s.ones[:], M[2][:, t, :], start=t == 0, stop=t == NT - 1)
            mm.then_inc(pos_mm, 1)


def expert_stage(nc, s, io, tab_pos, tab_val, items):
    with ExitStack() as ctx:
        def sb(name, shape, dt=F32):
            return ctx.enter_context(nc.sbuf_tensor(name, shape, dt))

        sem = ctx.enter_context(Semaphores(nc))
        SPLIT = 3
        raw = sb("e_raw", [P, RAW, KC, FE])
        hi = sb("e_hi", [P, SPLIT, KC, FE], F32R)
        lo = sb("e_lo", [P, SPLIT, KC, FE], F32R)
        sel = sb("e_sel", [P, NT, P])
        next_i = [sb(f"e_next_i{u}", [P, 2], U32) for u in range(2)]
        next_g = [sb(f"e_next_g{u}", [P, 1]) for u in range(2)]
        row_i = [sb(f"e_row_i{u}", [P, 1], U32) for u in range(2)]
        gate = [sb(f"e_gate{u}", [P, 1]) for u in range(2)]
        xg = [sb(f"e_xg{u}", [P, D]) for u in range(2)]
        xT_hi = [sb(f"e_xh{u}", [P, KT, P], F32R) for u in range(2)]
        xT_lo = [sb(f"e_xl{u}", [P, KT, P], F32R) for u in range(2)]
        act_g = sb("e_act", [P, FE])
        hid = sb("e_hid", [P, FE])
        hT_hi = sb("e_hh", [P, KC, P], F32R)
        hT_lo = sb("e_hl", [P, KC, P], F32R)
        y = [sb(f"e_y{u}", [P, D]) for u in range(2)]
        warm = sb("e_warm", [P, 1])
        raw_in = [sem(f"ew_in{n}") for n in range(RAW)]
        hi_done = sem("ew_hi")
        lo_done = [sem(f"ew_lo{n}") for n in range(RAW)]
        mm_done = [sem(f"ew_mm{n}") for n in range(SPLIT)]
        go, zero, sel_done, tab_mm, slot_done = sem("e_go"), sem("e_zero"), sem("e_sel_done"), sem("e_tab_mm"), sem("e_slot_done")
        rows_in = [sem(f"e_rows{u}") for u in range(2)]
        xt_mm, xhi_done, xlo_done = sem("e_xt_mm"), sem("e_xhi"), sem("e_xlo")
        silu_done, hid_done, ht_mm, hh_done, hl_done = (sem(n) for n in ("e_silu", "e_hid_done", "e_ht", "e_hh_done", "e_hl_done"))
        y_done, moved = sem("e_y_done"), sem("e_moved")
        scattered = [sem(f"e_scat{u}") for u in range(2)]
        y_free = [sem(f"e_y_free{u}") for u in range(2)]
        block = ctx.enter_context(nc.Block())
        ps = s.ps
        G, U, XB, HB, YB, TB = 0, 1, 2, 4, 5, 7
        XR = KT // 4
        CH = CH_PER_ITEM
        UP, GATE, DOWN = (0, 1, 2, 3), (4, 5, 10, 11), (6, 7, 8, 9)
        PRE = len(GATE)

        def slot_of(q, ring):
            return (PRE + q) % ring

        def before(k, q, ring):
            return k * (CH // ring) + (PRE + q) // ring

        def n_pairs(eng):
            return eng.value_load(items[0:1, 2, 0:1], min_val=NE // 2, max_val=N_ITEMS // 2)

        def item(eng, row, k, top):
            return eng.value_load(items[0:1, row, bass.ds(k, 1)], min_val=0, max_val=top)

        @block.sync
        def _(sp):
            def load(k, q, src):
                n = slot_of(q, RAW)
                if q >= RAW - PRE:
                    sp.wait_ge(lo_done[n], before(k, q, RAW))
                sp.dma_start(raw[:, n], src.rearrange("p e k n -> p (e k) n")).then_inc(raw_in[n], 16)

            e = item(sp, 1, 0, NE - 1)
            for c in range(PRE):
                load(0, c - PRE, io.w1_v[:, bass.ds(e, 1), c * KC:(c + 1) * KC, :])
            pairs = n_pairs(sp)
            with sp.Fori(0, pairs) as i:
                for u in range(2):
                    k = i * 2 + u
                    e, e_next = item(sp, 1, k, NE - 1), item(sp, 1, k + 1, NE - 1)
                    for q in range(CH):
                        if q in UP:
                            c = UP.index(q)
                            load(k, q, io.w3_v[:, bass.ds(e, 1), c * KC:(c + 1) * KC, :])
                        elif q in GATE:
                            c = GATE.index(q)
                            load(k, q, io.w1_v[:, bass.ds(e_next, 1), c * KC:(c + 1) * KC, :])
                        else:
                            c = DOWN.index(q)
                            load(k, q, io.w2_v[:, bass.ds(e, 1), :, c * FE:(c + 1) * FE])

        @block.gpsimd
        def _(pool):
            for u in range(2):
                pool.memset(xg[u][:], 0.0).then_inc(zero, 1)
            pool.wait_ge(zero, 2)

            def gather(k, u):
                pool.wait_ge(slot_done, k + 1)
                pool.sem_inc(go, 1)
                pool.indirect_dma_start(out=xg[u][:], out_offset=None, in_=io.xn,
                                        in_offset=bass.IndirectOffsetOnAxis(ap=next_i[u][:, 0:1], axis=0),
                                        bounds_check=T - 1, oob_is_err=False).then_inc(rows_in[u], 16)

            for u in range(2):
                pool.sem_inc(y_free[u], AHEAD)
            for u in range(2):
                gather(u, u)
            pairs = n_pairs(pool)
            with pool.Fori(0, pairs) as i:
                for u in range(2):
                    k = i * 2 + u
                    pool.wait_ge(xt_mm, k * XR + XR)
                    gather(k + 2, u)
                    pool.wait_ge(y_done, k * 4 + 4)
                    pool.sem_inc(go, 1)
                    pool.indirect_dma_start(out=io.rows, out_offset=bass.IndirectOffsetOnAxis(
                        ap=row_i[u][:, 0:1], axis=0), in_=y[u][:], in_offset=None,
                        bounds_check=2 * T - 1, oob_is_err=False).then_inc(scattered[u], 16)
                    pool.wait_ge(scattered[u], i * 16 + 16)
                    pool.sem_inc(y_free[u], 1)

        @block.scalar
        def _(act):
            def split(k, q):
                n, m = slot_of(q, RAW), slot_of(q, SPLIT)
                act.wait_ge(raw_in[n], before(k, q, RAW) * 16 + 16)
                if q >= SPLIT - PRE:
                    act.wait_ge(mm_done[m], before(k, q, SPLIT))
                nc.scalar.copy(hi[:, m], raw[:, n]).then_inc(hi_done, 1)

            def x_hi(k, u, r):
                act.wait_ge(xt_mm, k * XR + (r + 1))
                nc.scalar.copy(xT_hi[u][:, 4 * r:4 * r + 4], ps[:, XB + r % 2, :].rearrange(
                    "p (f t) -> p f t", f=4)).then_inc(xhi_done, 1)

            def y_out(k, u, c):
                if c == 0:
                    act.wait_ge(slot_done, k + 3)
                act.wait_ge(mm_done[slot_of(DOWN[c], SPLIT)], before(k, DOWN[c], SPLIT) + 1)
                nc.scalar.activation(y[u][:, c * FE:(c + 1) * FE], ps[:, YB + c % 2, :], ACT.Copy,
                                     scale=gate[u][:, 0:1]).then_inc(y_done, 1)

            nc.scalar.activation(warm[:], s.one[:], ACT.Silu)
            for u in range(2):
                for r in range(XR):
                    x_hi(u, u, r)
            for c in range(PRE):
                split(0, c - PRE)
            pairs = n_pairs(act)
            with act.Fori(0, pairs) as i:
                for u in range(2):
                    k = i * 2 + u
                    split(k, 0)
                    split(k, 1)
                    act.wait_ge(mm_done[slot_of(-1, SPLIT)], before(k, -1, SPLIT) + 1)
                    nc.scalar.activation(act_g[:], ps[:, G, :], ACT.Silu).then_inc(silu_done, 1)
                    for q in range(2, 7):
                        split(k, q)
                    act.wait_ge(ht_mm, k + 1)
                    nc.scalar.copy(hT_hi[:], ps[:, HB, :].rearrange("p (f t) -> p f t", f=KC)).then_inc(hh_done, 1)
                    split(k, 7)
                    x_hi(k + 2, u, 0)
                    x_hi(k + 2, u, 1)
                    split(k, 8)
                    y_out(k, u, 0)
                    x_hi(k + 2, u, 2)
                    split(k, 9)
                    y_out(k, u, 1)
                    x_hi(k + 2, u, 3)
                    split(k, 10)
                    y_out(k, u, 2)
                    split(k, 11)
                    y_out(k, u, 3)

        @block.vector
        def _(dve):
            def split(k, q):
                n, m = slot_of(q, RAW), slot_of(q, SPLIT)
                dve.wait_ge(hi_done, k * CH + (PRE + q + 1))
                nc.vector.tensor_tensor(lo[:, m], raw[:, n], hi[:, m].bitcast(F32), ALU.subtract).then_inc(lo_done[n], 1)

            def select(k, code):
                for t in range(NT):
                    ins = nc.vector.tensor_scalar(sel[:, t, :], s.slot[:], tab_pos[:, bass.ds(code, 1), t:t + 1].rearrange(
                        "p c t -> p (c t)"), None, ALU.is_equal)
                ins.then_inc(sel_done, 1)

            def slots(k, u):
                dve.wait_ge(tab_mm, k + 1)
                nc.vector.tensor_copy(next_g[u][:], ps[:, TB, 2:3])
                nc.vector.tensor_scalar(next_i[u][:], ps[:, TB, 0:2], BIG, None, ALU.add).then_inc(slot_done, 1)

            def x_lo(k, u, r):
                dve.wait_ge(xhi_done, k * XR + (r + 1))
                nc.vector.tensor_tensor(xT_lo[u][:, 4 * r:4 * r + 4], ps[:, XB + r % 2, :].rearrange(
                    "p (f t) -> p f t", f=4), xT_hi[u][:, 4 * r:4 * r + 4].bitcast(F32), ALU.subtract).then_inc(xlo_done, 1)

            for u in range(2):
                select(u, item(dve, 0, u, PAD_CODE))
                slots(u, u)
            for u in range(2):
                for r in range(XR):
                    x_lo(u, u, r)
            for c in range(PRE):
                split(0, c - PRE)
            pairs = n_pairs(dve)
            with dve.Fori(0, pairs) as i:
                for u in range(2):
                    k = i * 2 + u
                    split(k, 0)
                    select(k + 2, item(dve, 0, k + 2, PAD_CODE))
                    split(k, 1)
                    dve.wait_ge(y_free[u], i + AHEAD)
                    nc.vector.tensor_copy(row_i[u][:], next_i[u][:, 1:2])
                    nc.vector.tensor_copy(gate[u][:], next_g[u][:]).then_inc(moved, 1)
                    split(k, 2)
                    dve.wait_ge(moved, k + 1)
                    slots(k + 2, u)
                    split(k, 3)
                    split(k, 4)
                    dve.wait_ge(silu_done, k + 1)
                    dve.wait_ge(mm_done[slot_of(UP[3], SPLIT)], before(k, UP[3], SPLIT) + 1)
                    nc.vector.tensor_tensor(hid[:], act_g[:], ps[:, U, :], ALU.mult).then_inc(hid_done, 1)
                    split(k, 5)
                    dve.wait_ge(hh_done, k + 1)
                    nc.vector.tensor_tensor(hT_lo[:], ps[:, HB, :].rearrange("p (f t) -> p f t", f=KC),
                                            hT_hi[:].bitcast(F32), ALU.subtract).then_inc(hl_done, 1)
                    split(k, 6)
                    split(k, 7)
                    x_lo(k + 2, u, 0)
                    x_lo(k + 2, u, 1)
                    split(k, 8)
                    x_lo(k + 2, u, 2)
                    split(k, 9)
                    x_lo(k + 2, u, 3)
                    split(k, 10)
                    split(k, 11)

        @block.tensor
        def _(pe):
            def table(k, code, first):
                pe.wait_ge(sel_done, k + 1)
                if not first:
                    pe.wait_ge(slot_done, k)
                for t in range(NT):
                    mm = nc.tensor.matmul(ps[:, TB, 0:4], sel[:, t, :], tab_val[:, bass.ds(code, 1), t, :].rearrange(
                        "p c v -> p (c v)"), start=t == 0, stop=t == NT - 1)
                mm.then_inc(tab_mm, 1)

            def transpose_x(k, u, r, n_rows, fresh=False):
                if r == 0:
                    pe.wait_ge(rows_in[u], n_rows)
                if not fresh:
                    pe.wait_ge(xlo_done, k * XR + (r - 1))
                for j in range(4):
                    f = 4 * r + j
                    tp = nc.tensor.transpose(ps[:, XB + r % 2, j * P:(j + 1) * P], xg[u][:, f * P:(f + 1) * P], s.ident[:])
                tp.then_inc(xt_mm, 1)

            def three(out, a_hi, a_lo, b_hi, b_lo, first, last):
                nc.tensor.matmul(out, a_hi, b_hi, start=first, stop=False)
                nc.tensor.matmul(out, a_lo, b_hi, start=False, stop=False)
                return nc.tensor.matmul(out, a_hi, b_lo, start=False, stop=last)

            def chunk(k, q, bank, a_hi, a_lo, c, n_chunks):
                n, m = slot_of(q, RAW), slot_of(q, SPLIT)
                pe.wait_ge(lo_done[n], before(k, q, RAW) + 1)
                for j in range(KC):
                    f = c * KC + j
                    mm = three(ps[:, bank, :], a_hi[:, f, :], a_lo[:, f, :], hi[:, m, j], lo[:, m, j],
                               f == 0, f == n_chunks * KC - 1)
                mm.then_inc(mm_done[m], 1)

            for u in range(2):
                table(u, item(pe, 0, u, PAD_CODE), u == 0)
            for u in range(2):
                for r in range(XR):
                    transpose_x(u, u, r, 16, fresh=u == 0 and r < 2)
            pe.wait_ge(xlo_done, XR)
            for c in range(PRE):
                chunk(0, c - PRE, G, xT_hi[0], xT_lo[0], c, PRE)
            pairs = n_pairs(pe)
            with pe.Fori(0, pairs) as i:
                for u in range(2):
                    k = i * 2 + u
                    n_rows = i * 16 + 32
                    for q in range(CH):
                        if q in UP:
                            chunk(k, q, U, xT_hi[u], xT_lo[u], UP.index(q), 4)
                        elif q in GATE:
                            if q == GATE[0]:
                                pe.wait_ge(silu_done, k + 1)
                                pe.wait_ge(xlo_done, k * XR + 2 * XR)
                            chunk(k, q, G, xT_hi[1 - u], xT_lo[1 - u], GATE.index(q), 4)
                        else:
                            c = DOWN.index(q)
                            if c == 0:
                                pe.wait_ge(hl_done, k + 1)
                            if c >= 2:
                                pe.wait_ge(y_done, k * 4 + (c - 1))
                            chunk(k, q, YB + c % 2, hT_hi, hT_lo, 0, 1)
                        if q == 1:
                            table(k + 2, item(pe, 0, k + 2, PAD_CODE), False)
                        elif q == 4:
                            pe.wait_ge(hid_done, k + 1)
                            for j in range(KC):
                                tp = nc.tensor.transpose(ps[:, HB, j * P:(j + 1) * P], hid[:, j * P:(j + 1) * P], s.ident[:])
                            tp.then_inc(ht_mm, 1)
                        elif q == 5:
                            transpose_x(k + 2, u, 0, n_rows)
                            transpose_x(k + 2, u, 1, n_rows)
                        elif q in (6, 7):
                            transpose_x(k + 2, u, q - 4, n_rows)


def combine_stage(nc, s, io, x2):
    with ExitStack() as ctx:
        sem = ctx.enter_context(Semaphores(nc))
        r = [ctx.enter_context(nc.sbuf_tensor(f"c_row{n}", [P, NT, D], F32)) for n in range(2)]
        row_in = [[sem(f"c_in{n}_{t}") for t in range(NT)] for n in range(2)]
        first, both, stored = sem("c_first"), sem("c_both"), sem("c_stored")
        block = ctx.enter_context(nc.Block())

        @block.sync
        def _(sp):
            for t in range(NT):
                for n in range(2):
                    at = n * T + t * P
                    sp.dma_start(r[n][:, t, :], io.rows[at:at + P, :]).then_inc(row_in[n][t], 16)

        @block.vector
        def _(dve):
            for t in range(NT):
                dve.wait_ge(row_in[0][t], 16)
                nc.vector.tensor_tensor(x2[:, t, :], x2[:, t, :], r[0][:, t, :], ALU.add).then_inc(first, 1)
                dve.wait_ge(row_in[1][t], 16)
                dve.wait_ge(first, t + 1)
                nc.vector.tensor_tensor(x2[:, t, :], x2[:, t, :], r[1][:, t, :], ALU.add).then_inc(both, 1)

        @block.scalar
        def _(act):
            for t in range(NT):
                act.wait_ge(both, t + 1)
                act.dma_start(io.out[t * P:(t + 1) * P, :], x2[:, t, :]).then_inc(stored, 16)
            act.wait_ge(stored, NT * 16)


def program(nc, io):
    with ExitStack() as ctx:
        s = shared(nc, ctx)
        with ExitStack() as front:
            hT_hi = front.enter_context(nc.sbuf_tensor("hT_hi", [P, KT, T], F32R))
            hT_lo = front.enter_context(nc.sbuf_tensor("hT_lo", [P, KT, T], F32R))
            setup_stage(nc, s, io, hT_hi, hT_lo)
            project_stage(nc, s, io, hT_hi, hT_lo)
        x2 = ctx.enter_context(nc.sbuf_tensor("x2", [P, NT, D], F32))
        with ExitStack() as mixed:
            mix_hi = mixed.enter_context(nc.sbuf_tensor("mix_hi", [P, KT, T], F32R))
            mix_lo = mixed.enter_context(nc.sbuf_tensor("mix_lo", [P, KT, T], F32R))
            stick_stage(nc, s, io, mix_hi, mix_lo)
            delta_stage(nc, s, io, mix_hi, mix_lo, x2)
            out_proj_stage(nc, s, io, mix_hi, mix_lo, x2)
        with ExitStack() as back:
            tab_pos = back.enter_context(nc.sbuf_tensor("tab_pos", [P, PAD_CODE + 1, NT], F32))
            tab_val = back.enter_context(nc.sbuf_tensor("tab_val", [P, PAD_CODE + 1, NT, 4], F32))
            items = back.enter_context(nc.sbuf_tensor("items", [1, 3, N_ITEMS + 2], I32))
            route_stage(nc, s, io, x2, tab_pos, tab_val, items)
            expert_stage(nc, s, io, tab_pos, tab_val, items)
        combine_stage(nc, s, io, x2)


def views(io, a):
    io.x = a["x"].rearrange("b t d -> (b t) d")
    io.norm1_w = a["norm1_w"].rearrange("l (k p) -> (l k) p", p=P)
    io.norm2_row = a["norm2_w"]
    io.norm2_w = a["norm2_w"].rearrange("l (k p) -> (l k) p", p=P)
    io.conv_w = a["gdn_conv_w"].rearrange("l n (c p) -> (l n c) p", p=P)
    io.q_norm_w, io.k_norm_w, io.out_norm_w = a["sb_q_norm_w"], a["sb_k_norm_w"], a["gdn_out_norm_w"]
    io.a_log, io.dt_bias = a["gdn_a_log"], a["gdn_dt_bias"]
    io.w_in_v = a["w_in"].rearrange("l (k p) n -> p (l k) n", p=P)
    io.w_o_v = a["w_o"].rearrange("l (k p) n -> p (l k) n", p=P)
    io.w_group, io.w_expert = a["w_group"][0], a["w_expert"][0]
    io.b_group, io.b_expert = a["b_group"], a["b_expert"]
    io.w1_v = a["w1"][0].rearrange("e (k p) n -> p e k n", p=P)
    io.w3_v = a["w3"][0].rearrange("e (k p) n -> p e k n", p=P)
    io.w2_v = a["w2"][0].rearrange("e (k p) n -> p e k n", p=P)
    io.proj_qkv = io.proj[0:TILE_GQ].rearrange("(g e) p t -> p g e t", g=3)
    io.proj_gdn = io.proj[TILE_GQ:TILE_GZ].rearrange("(g e) p t -> p g e t", g=3)
    io.proj_z = io.proj[TILE_GZ:].rearrange("e p t -> p e t")


def build(nc, args, out):
    io = Core()
    io.proj = nc.dram_tensor("proj_scratch", (4 * N_GRP, P, T), F32, kind="Internal").ap()
    io.xn = nc.dram_tensor("xn_scratch", (T, D), F32, kind="Internal").ap()
    io.rows = nc.dram_tensor("rows_scratch", (2 * T, D), F32, kind="Internal").ap()
    io.out = out.rearrange("b t d -> (b t) d")
    views(io, args)
    program(nc, io)


INPUTS = ["x", "norm1_w", "w_in", "sb_q_norm_w", "sb_k_norm_w", "gdn_conv_w", "gdn_a_log", "gdn_dt_bias",
          "gdn_out_norm_w", "w_o", "norm2_w", "w_group", "b_group", "w_expert", "b_expert", "w1", "w3", "w2"]


def kernel(**inputs):
    import numpy as np
    from concourse import bacc
    from concourse.bass_utils import run_bass_kernel_spmd

    nc = bacc.Bacc("TRN2", target_bir_lowering=False, num_devices=1)
    arrays, args = {}, {}
    for name in INPUTS:
        a = np.ascontiguousarray(inputs[name])
        arrays[f"in_{name}"] = a
        args[name] = nc.dram_tensor(f"in_{name}", a.shape, mybir.dt.from_np(a.dtype), kind="ExternalInput").ap()
    out = nc.dram_tensor("out_0", (1, T, D), F32, kind="ExternalOutput").ap()
    build(nc, args, out)
    result = run_bass_kernel_spmd(nc, [arrays], core_ids=[0])
    return result.results[0]["out_0"]
```

```python
from contextlib import ExitStack

import concourse.bass as bass
from concourse import mybir

F32 = mybir.dt.float32
F32R = mybir.dt.float32r
I32 = mybir.dt.int32
U32 = mybir.dt.uint32
ALU = mybir.AluOpType
ACT = mybir.ActivationFunctionType
AX = mybir.AxisListType

P = 128
T = 512
NT = T // P
D = 2048
KT = D // P
HEADS = 8
GRP = 512
N_GRP = 14
IN_COLS = N_GRP * GRP + 2 * HEADS
TILE_Q, TILE_K, TILE_V = 0, 8, 16
TILE_GQ, TILE_GK, TILE_GV, TILE_GZ = 24, 32, 40, 48
TAPS = 4
CONV_ROWS = TAPS * 3 * HEADS
LEVELS = 7
KC = 4
RAW = 4
KQ = KT // 4
NG, NE = 4, 32
PER = NE // NG
FE = 512
BLKS = T // P
EXTRA = 2 * T // P - 1
N_ITEMS = NE + EXTRA + 1
PAD_CODE = BLKS * NE
EPS = 1e-6
AHEAD = 1
BIG = 4096.0
EXP_LN = 6
CH_PER_ITEM = 12


class Core:
    pass


class Semaphores:

    def __init__(self, nc):
        self.nc, self.taken = nc, []

    def __enter__(self):
        return self

    def __call__(self, name):
        self.taken.append(self.nc.alloc_semaphore(name))
        return self.taken[-1]

    def __exit__(self, *error):
        if error[0] is None:
            self.nc.clear_and_free_semaphores(self.taken)
            self.nc.all_engine_barrier()


def load_exp_and_ln(nc):
    nc.scalar.add_instruction(mybir.InstLoadActFuncSet(name=nc.get_next_instruction_name(), act_func_set_id=EXP_LN,
                                                       ins=[], outs=[]))


def shared(nc, ctx):
    s = Core()

    def sb(name, shape, dt=F32):
        return ctx.enter_context(nc.sbuf_tensor(name, shape, dt))

    s.ident = sb("ident", [P, P])
    s.ones = sb("ones", [P, P])
    s.slot = sb("slot", [P, P])
    s.tri = sb("tri", [P, P])
    s.tri_s = sb("tri_s", [P, P])
    s.ntri = sb("ntri", [P, P])
    s.nones = sb("nones", [P, P])
    s.unseen = sb("unseen", [P, P])
    s.taps = sb("taps", [P, CONV_ROWS])
    s.wn = sb("wn", [P, 4])
    s.zeros = sb("zeros", [P, P])
    s.eps = sb("eps", [P, 1])
    s.one = sb("one", [P, 1])
    s.gates = sb("gates", [P, NT, 2 * HEADS])
    s.ps = ctx.enter_context(nc.psum_tensor("ps", [P, 8, 512], F32))
    return s


def setup_stage(nc, s, io, hT_hi, hT_lo, w_raw, w_raw_in):
    with ExitStack() as ctx:
        def sb(name, shape, dt=F32):
            return ctx.enter_context(nc.sbuf_tensor(name, shape, dt))

        sem = ctx.enter_context(Semaphores(nc))

        xs = sb("xs", [P, NT, D])
        sq = sb("sq", [P, D])
        ss = sb("ss", [P, NT])
        ms = sb("ms", [P, NT])
        rec = sb("rec", [P, NT])
        rstd = sb("rstd", [P, NT])
        w1row = sb("w1row", [P, D])
        prow = sb("prow", [CONV_ROWS, P])
        wrow = sb("wrow", [3, P])
        x_in = [sem(f"x_in{t}") for t in range(NT)]
        par_in, norm_in, memset_done, consts_done = sem("par_in"), sem("norm_in"), sem("memset_done"), sem("consts_done")
        sumsq_done, ms_done, rec_done, rstd_done = sem("sumsq_done"), sem("ms_done"), sem("rec_done"), sem("rstd_done")
        xn_done, par_t = sem("xn_done"), sem("par_t")
        tp_done, hi_done, lo_done = sem("tp_done"), sem("hi_done"), sem("lo_done")
        block = ctx.enter_context(nc.Block())
        ps = s.ps

        @block.sync
        def _(sp):
            for t in range(NT):
                sp.dma_start(xs[:, t, :], io.x[t * P:(t + 1) * P, :]).then_inc(x_in[t], 16)
                if t == 0:
                    sp.dma_start(w1row[:], io.norm1_row.broadcast_to([P, D])).then_inc(norm_in, 16)
            sp.dma_start(prow[:], io.conv_w).then_inc(par_in, 16)
            sp.dma_start(wrow[0:1, :], io.q_norm_w).then_inc(par_in, 16)
            sp.dma_start(wrow[1:2, :], io.k_norm_w).then_inc(par_in, 16)
            sp.dma_start(wrow[2:3, :], io.out_norm_w).then_inc(par_in, 16)
            for ch in range(RAW):
                sp.dma_start(w_raw[:, ch], io.w_in_v[:, ch * KC:(ch + 1) * KC, 0:GRP]).then_inc(w_raw_in[ch], 16)

        @block.gpsimd
        def _(pool):
            pool.memset(s.ones[:], 1.0).then_inc(memset_done, 1)
            pool.memset(s.nones[:], -1.0).then_inc(memset_done, 1)
            pool.memset(s.eps[:], EPS).then_inc(memset_done, 1)
            pool.memset(s.one[:], 1.0).then_inc(memset_done, 1)
            pool.memset(s.zeros[:], 0.0).then_inc(memset_done, 1)
            pool.wait_ge(memset_done, 5)
            for out, src, op, base, step, mult in (
                (s.tri, s.ones, ALU.is_ge, 0, 1, -1),
                (s.tri_s, s.ones, ALU.is_gt, 0, 1, -1),
                (s.ntri, s.nones, ALU.is_ge, 0, -1, 1),
                (s.ident, s.ones, ALU.is_equal, 0, 1, -1),
                (s.unseen, s.zeros, ALU.is_gt, 0, 1, -1),
            ):
                pool.affine_select(out=out[:], in_=src[:], compare_op=op, fill=-1e30 if src is s.zeros else 0.0,
                                   base=base,
                                   pattern=[[step, P]], channel_multiplier=mult).then_inc(consts_done, 1)

        @block.scalar
        def _(act):
            def hi_tile(t):
                for q in range(KQ):
                    r = t * KQ + q
                    act.wait_ge(tp_done, r + 1)
                    nc.scalar.copy(hT_hi[:, 4 * q:4 * q + 4, t * P:(t + 1) * P], ps[:, 2 + r % 4, :].rearrange(
                        "p (k t) -> p k t", k=4)).then_inc(hi_done, 1)

            for t in range(NT):
                act.wait_ge(x_in[t], 16)
                if t:
                    act.wait_ge(sumsq_done, t)
                nc.scalar.activation(sq[:], xs[:, t, :], ACT.Square, accum_out=ss[:, t:t + 1]).then_inc(sumsq_done, 1)
                act.wait_ge(rec_done, t + 1)
                nc.scalar.activation(rstd[:, t:t + 1], rec[:, t:t + 1], ACT.Sqrt).then_inc(rstd_done, 1)
                if t:
                    hi_tile(t - 1)
            hi_tile(NT - 1)

        @block.vector
        def _(dve):
            def lo_tile(t):
                for q in range(KQ):
                    r = t * KQ + q
                    at = hT_hi[:, 4 * q:4 * q + 4, t * P:(t + 1) * P]
                    dve.wait_ge(hi_done, r + 1)
                    nc.vector.tensor_tensor(hT_lo[:, 4 * q:4 * q + 4, t * P:(t + 1) * P], ps[:, 2 + r % 4, :].rearrange(
                        "p (k t) -> p k t", k=4), at.bitcast(F32), ALU.subtract).then_inc(lo_done, 1)

            dve.wait_ge(norm_in, 16)
            for t in range(NT):
                at = slice(t, t + 1)
                dve.wait_ge(sumsq_done, t + 1)
                nc.vector.tensor_scalar(ms[:, at], ss[:, at], 1.0 / D, EPS, ALU.mult, ALU.add).then_inc(ms_done, 1)
                dve.wait_ge(ms_done, t + 1)
                nc.vector.reciprocal(rec[:, at], ms[:, at]).then_inc(rec_done, 1)
                dve.wait_ge(rstd_done, t + 1)
                nc.vector.scalar_tensor_tensor(out=xs[:, t, :], in0=xs[:, t, :], scalar=rstd[:, at], in1=w1row[:],
                                               op0=ALU.mult, op1=ALU.mult).then_inc(xn_done, 1)
                if t:
                    lo_tile(t - 1)
            lo_tile(NT - 1)
            dve.wait_ge(par_t, 2)
            nc.vector.tensor_copy(s.taps[:], ps[:, 0, 0:CONV_ROWS])
            nc.vector.tensor_scalar(s.wn[:, 0:1], ps[:, 1, 0:1], P ** -0.5, None, ALU.mult)
            nc.vector.tensor_copy(s.wn[:, 1:3], ps[:, 1, 1:3])

        @block.tensor
        def _(pe):
            pe.wait_ge(consts_done, 4)
            for r in range(NT * KQ):
                t, q = r // KQ, r % KQ
                pe.wait_ge(xn_done, t + 1)
                if r >= 4:
                    pe.wait_ge(lo_done, r - 3)
                for j in range(4):
                    k = 4 * q + j
                    tp = nc.tensor.transpose(ps[:, 2 + r % 4, j * P:(j + 1) * P], xs[:, t, k * P:(k + 1) * P], s.ident[:])
                tp.then_inc(tp_done, 1)
            pe.wait_ge(par_in, 4 * 16)
            nc.tensor.transpose(ps[:, 0, 0:CONV_ROWS], prow[:], s.ident[0:CONV_ROWS, 0:CONV_ROWS]).then_inc(par_t, 1)
            nc.tensor.transpose(ps[:, 1, 0:3], wrow[:], s.ident[0:3, 0:3]).then_inc(par_t, 1)


def project_stage(nc, s, io, hT_hi, hT_lo, raw, raw_in):
    with ExitStack() as ctx:
        def sb(name, shape, dt=F32):
            return ctx.enter_context(nc.sbuf_tensor(name, shape, dt))

        sem = ctx.enter_context(Semaphores(nc))

        hi = sb("w_hi", [P, 2, KC, GRP], F32R)
        lo = sb("w_lo", [P, 2, KC, GRP], F32R)
        stage = sb("p_stage", [P, 2, 4, T])
        ab_raw = sb("ab_raw", [P, KT, 2 * HEADS])
        ab_hi = sb("ab_hi", [P, KT, 2 * HEADS], F32R)
        ab_lo = sb("ab_lo", [P, KT, 2 * HEADS], F32R)
        gates_T = sb("gates_T", [2 * HEADS, T])
        hi_done, lo_done, mm_done = sem("pw_hi"), sem("pw_lo"), sem("pw_mm")
        staged = sem("staged")
        stored = [sem(f"p_stored{n}") for n in range(2)]
        stage_free = [sem(f"stage_free{n}") for n in range(2)]
        ab_in, ab_split, ab_mm, ab_out = sem("ab_in"), sem("ab_split"), sem("ab_mm"), sem("ab_out")
        block = ctx.enter_context(nc.Block())
        ps = s.ps
        CH = KT // KC
        BODY = 2 * CH
        PAIRS = N_GRP // 2

        @block.sync
        def _(sp):
            def load(ch, pair, col):
                return sp.dma_start(raw[:, ch % RAW, :, :], io.w_in_v[:, ch % CH * KC:(ch % CH + 1) * KC,
                                                                      bass.ds(col, GRP)])
            for ch in range(RAW, BODY):
                sp.wait_ge(lo_done, ch - RAW + 1)
                load(ch, 0, ch // CH * GRP).then_inc(raw_in[ch % RAW], 16)
            sp.dma_start(ab_raw[:], io.w_in_v[:, :, N_GRP * GRP:IN_COLS]).then_inc(ab_in, 16)
            with sp.Fori(1, PAIRS) as pair:
                for ch in range(BODY):
                    sp.wait_ge(lo_done, pair * BODY + (ch - RAW + 1))
                    load(ch, pair, pair * (2 * GRP) + ch // CH * GRP).then_inc(raw_in[ch % RAW], 16)

        @block.scalar
        def _(act):
            def split(pair, first):
                for ch in range(BODY):
                    act.wait_ge(raw_in[ch % RAW], pair * 32 + 16 * (ch // RAW + 1))
                    if ch >= 2 or not first:
                        act.wait_ge(mm_done, pair * BODY + (ch - 1))
                    nc.scalar.activation(hi[:, ch % 2], raw[:, ch % RAW], ACT.Copy).then_inc(hi_done, 1)
                    if ch % CH == 1 and (ch // CH or not first):
                        copy_out(pair, ch // CH)

            def copy_out(pair, g):
                half = 1 - g
                act.wait_ge(mm_done, pair * BODY + CH * g)
                act.wait_ge(stage_free[half], pair - half + AHEAD)
                nc.scalar.copy(stage[:, half], ps[:, 4 * half:4 * half + 4, :]).then_inc(staged, 1)

            split(0, True)
            with act.Fori(1, PAIRS) as pair:
                split(pair, False)
            act.wait_ge(ab_in, 16)
            nc.scalar.activation(ab_hi[:], ab_raw[:], ACT.Copy).then_inc(ab_split, 1)
            copy_out(PAIRS, 0)

        @block.gpsimd
        def _(pool):
            for g in range(2):
                pool.sem_inc(stage_free[g], AHEAD)
            with pool.Fori(0, PAIRS) as pair:
                for g in range(2):
                    pool.wait_ge(staged, pair * 2 + (g + 1))
                    pool.dma_start(io.proj[bass.ds(pair * 8 + 4 * g, 4)].rearrange("f p t -> p f t"),
                                   stage[:, g]).then_inc(stored[g], 16)
                    pool.wait_ge(stored[g], pair * 16 + 16)
                    pool.sem_inc(stage_free[g], 1)

        @block.vector
        def _(dve):
            with dve.Fori(0, PAIRS) as pair:
                for ch in range(BODY):
                    dve.wait_ge(hi_done, pair * BODY + (ch + 1))
                    nc.vector.tensor_tensor(lo[:, ch % 2], raw[:, ch % RAW], hi[:, ch % 2].bitcast(F32),
                                            ALU.subtract).then_inc(lo_done, 1)
            dve.wait_ge(ab_split, 1)
            nc.vector.tensor_tensor(ab_lo[:], ab_raw[:], ab_hi[:].bitcast(F32), ALU.subtract).then_inc(ab_split, 1)
            dve.wait_ge(ab_mm, 1)
            nc.vector.tensor_copy(gates_T[:], ps[0:2 * HEADS, 0, :]).then_inc(ab_out, 1)
            dve.wait_ge(ab_mm, 2)
            nc.vector.tensor_copy(s.gates[:], ps[:, 1, 0:NT * 2 * HEADS].rearrange(
                "p (t c) -> p t c", t=NT)).then_inc(ab_out, 1)

        @block.tensor
        def _(pe):
            def products(pair, first):
                for ch in range(BODY):
                    g, c = ch // CH, ch % CH
                    if c == 0 and not first:
                        pe.wait_ge(staged, pair * 2 + (g - 1))
                    pe.wait_ge(lo_done, pair * BODY + (ch + 1))
                    for f in range(4):
                        out = ps[:, 4 * g + f, :]
                        for k in range(KC):
                            kt = c * KC + k
                            w = slice(f * P, (f + 1) * P)
                            nc.tensor.matmul(out, hi[:, ch % 2, k, w], hT_hi[:, kt, :], start=kt == 0, stop=False)
                            nc.tensor.matmul(out, hi[:, ch % 2, k, w], hT_lo[:, kt, :], start=False, stop=False)
                            mm = nc.tensor.matmul(out, lo[:, ch % 2, k, w], hT_hi[:, kt, :], start=False,
                                                  stop=kt == KT - 1)
                    mm.then_inc(mm_done, 1)

            products(0, True)
            with pe.Fori(1, PAIRS) as pair:
                products(pair, False)
            pe.wait_ge(ab_split, 2)
            pe.wait_ge(staged, N_GRP - 1)
            for k in range(KT):
                out = ps[0:2 * HEADS, 0, :]
                nc.tensor.matmul(out, ab_hi[:, k, :], hT_hi[:, k, :], start=k == 0, stop=False)
                nc.tensor.matmul(out, ab_hi[:, k, :], hT_lo[:, k, :], start=False, stop=False)
                mm = nc.tensor.matmul(out, ab_lo[:, k, :], hT_hi[:, k, :], start=False, stop=k == KT - 1)
            mm.then_inc(ab_mm, 1)
            pe.wait_ge(ab_out, 1)
            for t in range(NT):
                tp = nc.tensor.transpose(ps[:, 1, t * 2 * HEADS:(t + 1) * 2 * HEADS], gates_T[:, t * P:(t + 1) * P],
                                         s.ident[0:2 * HEADS, 0:2 * HEADS])
            tp.then_inc(ab_mm, 1)


def stick_stage(nc, s, io, mix_hi, mix_lo):
    with ExitStack() as ctx:
        def sb(name, shape, dt=F32):
            return [ctx.enter_context(nc.sbuf_tensor(f"{name}{u}", shape, dt)) for u in range(2)]

        sem1 = ctx.enter_context(Semaphores(nc))

        def sem(name):
            return [sem1(f"{name}{u}") for u in range(2)]

        qkv = sb("s_qkv", [P, 3, T])
        sq = sb("s_sq", [P, 2, T])
        lnr = sb("s_ln", [P, 2, T])
        rr = sb("s_r", [P, 2, T])
        qn, kn = sb("s_qn", [P, T]), sb("s_kn", [P, T])
        vtok = sb("s_vtok", [P, NT, P])
        lg = sb("s_lg", [P, NT, T])
        spl = sb("s_spl", [P, NT, T])
        wgt = sb("s_wgt", [P, NT, T])
        qkv_in, sq_done, ss_done, ln_done, r_done = (sem(n) for n in ("qkv_in", "sq_done", "ss_done", "sln_done", "sr_done"))
        vt_done, vtok_done, qk_done, z_done = (sem(n) for n in ("vt_done", "vtok_done", "qk_done", "z_done"))
        abs_done, e_done, l_done, sp_done = (sem(n) for n in ("abs_done", "e_done", "l_done", "sp_done"))
        cum_done, w_done, o_done = (sem(n) for n in ("cum_done", "w_done", "o_done"))
        mhi_done, mlo_done, relu_done = sem("mhi_done"), sem("mlo_done"), sem("relu_done")
        block = ctx.enter_context(nc.Block())
        ps = s.ps
        PAIRS = HEADS // 2
        DOWN = list(range(NT - 1, -1, -1))

        def live(kb):
            return slice(kb * P, T)

        @block.sync
        def _(sp):
            with sp.Fori(0, PAIRS) as i:
                for u in range(2):
                    sp.wait_ge(z_done[u], i * NT + AHEAD)
                    sp.dma_start(qkv[u][:], io.proj_qkv[:, :, bass.ds(i * 2 + u, 1), :].rearrange(
                        "p g e t -> p (g e) t")).then_inc(qkv_in[u], 16)

        @block.scalar
        def _(act):
            load_exp_and_ln(nc)

            def square(i, u):
                act.wait_ge(qkv_in[u], i * 16 + 16)
                nc.scalar.activation(sq[u][:], qkv[u][:, 0:2, :], ACT.Square).then_inc(sq_done[u], 1)

            def rsqrt_sums(i, u):
                act.wait_ge(ss_done[u], i + 1)
                nc.scalar.activation(lnr[u][:], ps[:, 4 * u + 1:4 * u + 3, :], ACT.Ln, scale=1.0 / P,
                                     bias=s.eps[:]).then_inc(ln_done[u], 1)
                act.wait_ge(ln_done[u], i + 1)
                nc.scalar.activation(rr[u][:], lnr[u][:], ACT.Exp, scale=-0.5).then_inc(r_done[u], 1)

            def heads(i, more):
                for n, kb in enumerate(DOWN):
                    for u in range(2):
                        act.wait_ge(abs_done[u], i * NT + (n + 1))
                        nc.scalar.activation(lg[u][:, kb, live(kb)], lg[u][:, kb, live(kb)],
                                             ACT.Exp).then_inc(e_done[u], 1)
                    for u in range(2):
                        act.wait_ge(e_done[u], i * NT + (n + 1))
                        nc.scalar.activation(lg[u][:, kb, live(kb)], lg[u][:, kb, live(kb)], ACT.Ln,
                                             bias=s.one[:]).then_inc(l_done[u], 1)
                if more:
                    for u in range(2):
                        square(i + 1, u)
                for n, kb in enumerate(DOWN):
                    for u in range(2):
                        act.wait_ge(cum_done[u], i * NT + (n + 1))
                        nc.scalar.activation(wgt[u][:, kb, live(kb)], ps[:, 4 * u + kb, live(kb)],
                                             ACT.Exp).then_inc(w_done[u], 1)
                for u in range(2):
                    if more:
                        rsqrt_sums(i + 1, u)
                    act.wait_ge(o_done[u], i + 1)
                    nc.scalar.copy(mix_hi[:, bass.ds(i * 2 + u, 1), :].rearrange("p e t -> p (e t)"),
                                   ps[:, 4 * u + 3, :]).then_inc(mhi_done[u], 1)

            for u in range(2):
                square(0, u)
            for u in range(2):
                rsqrt_sums(0, u)
            with act.Fori(0, PAIRS - 1) as i:
                heads(i, True)
            heads(PAIRS - 1, False)

        @block.vector
        def _(dve):
            for u in range(2):
                for ahead in (vtok_done[u], mlo_done[u]):
                    dve.sem_inc(ahead, AHEAD)

            def softplus(i, n):
                kb = DOWN[n]
                for u in range(2):
                    dve.wait_ge(l_done[u], i * NT + (n + 1))
                    nc.vector.tensor_tensor(spl[u][:, kb, live(kb)], spl[u][:, kb, live(kb)], lg[u][:, kb, live(kb)],
                                            ALU.add).then_inc(sp_done[u], 1)

            with dve.Fori(0, PAIRS) as i:
                for u in range(2):
                    dve.wait_ge(r_done[u], i + 1)
                    for n, out in enumerate((qn[u], kn[u])):
                        nc.vector.scalar_tensor_tensor(out=out[:], in0=qkv[u][:, n, :], scalar=s.wn[:, n:n + 1],
                                                       in1=rr[u][:, n, :], op0=ALU.mult,
                                                       op1=ALU.mult).then_inc(qk_done[u], 1)
                for u in range(2):
                    dve.wait_ge(vt_done[u], i + 1)
                    nc.vector.tensor_copy(vtok[u][:], ps[:, 4 * u, :].rearrange(
                        "p (b d) -> p b d", b=NT)).then_inc(vtok_done[u], 1)
                for n, kb in enumerate(DOWN):
                    for u in range(2):
                        dve.wait_ge(z_done[u], i * NT + (n + 1 + AHEAD))
                        nc.vector.tensor_scalar(spl[u][:, kb, live(kb)], ps[:, 4 * u + kb, live(kb)], 0.0, None,
                                                ALU.max).then_inc(relu_done[u], 1)
                    for u in range(2):
                        dve.wait_ge(relu_done[u], i * NT + (n + 1))
                        nc.vector.scalar_tensor_tensor(out=lg[u][:, kb, live(kb)], in0=spl[u][:, kb, live(kb)],
                                                       scalar=-2.0, in1=ps[:, 4 * u + kb, live(kb)], op0=ALU.mult,
                                                       op1=ALU.add).then_inc(abs_done[u], 1)
                    if n:
                        softplus(i, n - 1)
                softplus(i, NT - 1)
                for u in range(2):
                    dve.wait_ge(mhi_done[u], i + 1)
                    nc.vector.tensor_tensor(
                        mix_lo[:, bass.ds(i * 2 + u, 1), :].rearrange("p e t -> p (e t)"), ps[:, 4 * u + 3, :],
                        mix_hi[:, bass.ds(i * 2 + u, 1), :].rearrange("p e t -> p (e t)").bitcast(F32),
                        ALU.subtract).then_inc(mlo_done[u], 1)

        @block.tensor
        def _(pe):
            for u in range(2):
                pe.sem_inc(z_done[u], AHEAD)

            def sums(i, u):
                pe.wait_ge(sq_done[u], i + 1)
                for n in range(2):
                    mm = nc.tensor.matmul(ps[:, 4 * u + 1 + n, :], s.ones[:], sq[u][:, n, :], start=True, stop=True)
                mm.then_inc(ss_done[u], 1)

            def turn_v(i, u):
                pe.wait_ge(qkv_in[u], i * 16 + 16)
                for n in range(NT):
                    tp = nc.tensor.transpose(ps[:, 4 * u, n * P:(n + 1) * P], qkv[u][:, 2, n * P:(n + 1) * P], s.ident[:])
                tp.then_inc(vt_done[u], 1)

            def heads(i, more):
                for n, kb in enumerate(DOWN):
                    for u in range(2):
                        if n == 0:
                            pe.wait_ge(mlo_done[u], i + AHEAD)
                            pe.wait_ge(qk_done[u], i * 2 + 2)
                        if kb == 0:
                            pe.wait_ge(vtok_done[u], i + 1 + AHEAD)
                        nc.tensor.matmul(ps[:, 4 * u + kb, live(kb)], kn[u][:, kb * P:(kb + 1) * P],
                                         qn[u][:, live(kb)], start=True, stop=False, skip_group_check=True)
                        nc.tensor.matmul(ps[:, 4 * u + kb, kb * P:(kb + 1) * P], s.ident[:], s.unseen[:], start=False,
                                         stop=False, skip_group_check=True).then_inc(z_done[u], 1)
                for n, kb in enumerate(DOWN):
                    for u in range(2):
                        pe.wait_ge(sp_done[u], i * NT + (n + 1))
                        out = ps[:, 4 * u + kb, :]
                        mm = nc.tensor.matmul(out[:, live(kb)], s.ntri[:], spl[u][:, kb, live(kb)], start=False,
                                              stop=kb == NT - 1, skip_group_check=True)
                        for later in range(kb + 1, NT):
                            mm = nc.tensor.matmul(out[:, live(later)], s.nones[:], spl[u][:, later, live(later)],
                                                  start=False, stop=later == NT - 1, skip_group_check=True)
                        mm.then_inc(cum_done[u], 1)
                if more:
                    for u in range(2):
                        pe.wait_ge(w_done[u], i * NT + NT)
                        sums(i + 1, u)
                for u in range(2):
                    pe.wait_ge(w_done[u], i * NT + NT)
                    out = ps[:, 4 * u + 3, :]
                    for kb in range(NT):
                        mm = nc.tensor.matmul(out[:, live(kb)], vtok[u][:, kb, :], wgt[u][:, kb, live(kb)],
                                              start=kb == 0, stop=kb == NT - 1, skip_group_check=True)
                    mm.then_inc(o_done[u], 1)
                    if more:
                        turn_v(i + 1, u)

            for u in range(2):
                turn_v(0, u)
                sums(0, u)
            with pe.Fori(0, PAIRS - 1) as i:
                heads(i, True)
            heads(PAIRS - 1, False)


def delta_stage(nc, s, io, mix_hi, mix_lo, spare):
    with ExitStack() as ctx:
        def one(name, shape, dt=F32):
            return ctx.enter_context(nc.sbuf_tensor(name, shape, dt))

        def sb(name, shape, dt=F32):
            return [one(f"{name}{u}", shape, dt) for u in range(2)]

        sem1 = ctx.enter_context(Semaphores(nc))

        def sem(name):
            return [sem1(f"{name}{u}") for u in range(2)]

        g = one("g", [P, HEADS, NT])
        beta = one("beta", [P, HEADS, NT])
        gcc = one("gcc", [P, HEADS, NT])
        nbe = one("nbe", [P, HEADS, NT])
        kds = one("kds", [P, HEADS, NT])
        gt = [one(f"gt{n}", [P, HEADS, NT]) for n in range(4)]
        alog = one("alog", [P, HEADS])
        dtb = one("dtb", [P, HEADS])
        ea = one("ea", [P, HEADS])
        lvl = one("lvl", [P, LEVELS, P])
        raw = sb("d_raw", [P, 3, TAPS - 1 + T])
        cv = sb("d_cv", [P, 3, T])
        sq = sb("d_sq", [P, 2, T])
        qn, kn, qg = sb("d_qn", [P, T]), sb("d_kn", [P, T]), sb("d_qg", [P, T])
        row_g, row_b = sb("d_row_g", [P, NT, P]), sb("d_row_b", [P, NT, P])
        eg = sb("d_eg", [P, T])
        dt = sb("d_dt", [P, NT, P])
        at = sb("d_at", [P, NT, P])
        qk = sb("d_qk", [P, NT, P])
        X, Y = sb("d_X", [P, NT, P]), sb("d_Y", [P, NT, P])
        room = spare[:].rearrange("p t d -> p (t d)")
        BLK = (LEVELS - 1) * NT * P
        blk = [room[:, u * BLK:(u + 1) * BLK].rearrange("p (l c t) -> p l c t", l=LEVELS - 1, c=NT) for u in range(2)]
        jl = room[:, 0:LEVELS * P].bitcast(I32).rearrange("p (l t) -> p l t", l=LEVELS)
        jx = room[:, LEVELS * P:(LEVELS + 1) * P].bitcast(I32)
        ji = room[:, (LEVELS + 1) * P:(LEVELS + 3) * P].bitcast(I32).rearrange("p (n t) -> p n t", n=2)
        z = [room[:, 2 * BLK:2 * BLK + HEADS // 2 * T].rearrange("p (i t) -> p i t", t=T),
             one("d_z1", [P, HEADS // 2, T])[:]]
        Pm = sb("d_P", [P, NT, P])
        kd, vb = sb("d_kd", [P, NT, P]), sb("d_vb", [P, NT, P])
        res, vnew, state = sb("d_res", [P, P]), sb("d_vnew", [P, P]), sb("d_state", [P, P])
        names = ("tiles_in", "conv1", "conv_done", "silu_done", "sq_done", "ss_done", "dln_done", "dr_done", "qkn_done",
                 "rows_done", "row_mm", "eg_done", "diff_done", "dt_done", "dtm_done", "dtb_done", "kk_done",
                 "at_done", "qk_done", "L_done", "X0", "Y0a", "Y0", "blk_done", "qg_done", "ktv_done",
                 "kd_done", "vb_done", "P_mm", "P_out", "XY_mm", "X_out", "Y_out", "ks_mm", "res_done", "vn_mm",
                 "vn_done", "su_mm", "state_done", "o_done", "osq_done", "oss_done", "oln_done", "or_done",
                 "on_done", "fin_done", "mh_done", "ml_done")
        m = {n: sem("d_" + n) for n in names}
        par_in, mset, gstep, gmm, lstep, zeroed, z_in, z_done = (sem1(n) for n in (
            "gpar_in", "gmset", "gstep", "gmm", "lstep", "zeroed", "z_in", "z_done"))
        block = ctx.enter_context(nc.Block())
        ps = s.ps
        PAIRS = HEADS // 2
        LV = range(1, LEVELS)
        CONV = [(u, k, n) for u in range(2) for k in range(TAPS) for n in range(3)]
        PER_LEVEL = 5
        SUMS_AT = (0, 1)
        QC, KD, VD = 0, 1, 2

        def chunks(ap):
            return ap.rearrange("p (c t) -> p c t", c=NT)

        def half(ap, l, odd):
            return ap.rearrange("p (n two k) -> p n two k", two=2, k=2 ** l)[:, :, odd, :]

        def flat(ap):
            return ap.rearrange("p c t -> p (c t)")

        def row(tile):
            return tile[:].rearrange("p c t -> p (c t)")

        def packed(ap, l):
            return ap.rearrange("p (n k) -> p n k", k=2 ** l)

        def col(table, head, c):
            return table[:, bass.ds(head, 1), c:c + 1].rearrange("p h c -> p (h c)")

        @block.sync
        def _(sp):
            def load(i, u):
                sp.dma_start(raw[u][:, :, TAPS - 1:], io.proj_gdn[:, :, bass.ds(i * 2 + u, 1), :].rearrange(
                    "p g e t -> p (g e) t")).then_inc(m["tiles_in"][u], 16)

            sp.wait_ge(zeroed, 2)
            sp.dma_start(alog[:], io.a_log.broadcast_to([P, HEADS])).then_inc(par_in, 16)
            sp.dma_start(dtb[:], io.dt_bias.broadcast_to([P, HEADS])).then_inc(par_in, 16)
            for u in range(2):
                load(0, u)
            for u in range(2):
                sp.dma_start(z[u], io.proj_z.rearrange("p (i u) t -> p u i t", u=2)[:, u]).then_inc(z_in, 16)
            with sp.Fori(1, PAIRS) as i:
                for u in range(2):
                    sp.wait_ge(m["conv_done"][u], i * 3 + AHEAD)
                    load(i, u)

        @block.gpsimd
        def _(pool):
            pool.iota(ji[:, 0, :], [[1, P]], base=0, channel_multiplier=0).then_inc(mset, 1)
            pool.iota(ji[:, 1, :], [[0, P]], base=0, channel_multiplier=1).then_inc(mset, 1)
            for u in range(2):
                pool.memset(raw[u][:, :, 0:TAPS - 1], 0.0).then_inc(zeroed, 1)
            pool.wait_ge(gstep, 9)
            pool.wait_ge(lstep, 3)

            def rows(i):
                for u in range(2):
                    head = i * 2 + u
                    pool.wait_ge(m["row_mm"][u], i + AHEAD)
                    for out, mat, tab in ((row_g[u], s.tri, g), (row_b[u], s.ident, beta)):
                        pool.tensor_tensor(out=out[:], in0=mat[:].unsqueeze(1).broadcast_to([P, NT, P]),
                                           in1=tab[:, bass.ds(head, 1), :].rearrange("p h c -> p (h c)").unsqueeze(
                                               2).broadcast_to([P, NT, P]), op=ALU.mult).then_inc(m["rows_done"][u], 1)

            def heads(i, more):
                for u in range(2):
                    pool.wait_ge(m["dt_done"][u], i + 1)
                    pool.tensor_tensor(out=dt[u][:], in0=dt[u][:], in1=s.tri[:].unsqueeze(1).broadcast_to([P, NT, P]),
                                       op=ALU.mult).then_inc(m["dtm_done"][u], 1)
                for l in LV:
                    for u in range(2):
                        pool.wait_ge(m["at_done"][u], i + 1)
                        pool.tensor_tensor(out=blk[u][:, l - 1], in0=at[u][:],
                                           in1=lvl[:, l, :].unsqueeze(1).broadcast_to([P, NT, P]),
                                           op=ALU.mult).then_inc(m["blk_done"][u], 1)
                for u in range(2):
                    pool.wait_ge(m["eg_done"][u], i + 1)
                    pool.wait_ge(m["qkn_done"][u], i * 2 + 2)
                    pool.tensor_tensor(out=qg[u][:], in0=qn[u][:], in1=eg[u][:],
                                       op=ALU.mult).then_inc(m["qg_done"][u], 1)
                if more:
                    rows(i + 1)
                for u in range(2):
                    at_ = bass.ds(i * 2 + (HEADS + u), 1)
                    pool.wait_ge(m["mh_done"][u], i + 1)
                    pool.tensor_tensor(out=mix_lo[:, at_, :].rearrange("p e t -> p (e t)"), in0=row(at[u]),
                                       in1=mix_hi[:, at_, :].rearrange("p e t -> p (e t)").bitcast(F32),
                                       op=ALU.subtract).then_inc(m["ml_done"][u], 1)

            for u in range(2):
                pool.sem_inc(m["ml_done"][u], AHEAD)
            rows(0)
            with pool.Fori(0, PAIRS - 1) as i:
                heads(i, True)
            heads(PAIRS - 1, False)

        @block.scalar
        def _(act):
            def silu(i, u):
                for n in range(3):
                    act.wait_ge(m["conv_done"][u], i * 3 + (n + 1 + AHEAD))
                    nc.scalar.activation(cv[u][:, n, :], cv[u][:, n, :], ACT.Silu).then_inc(m["silu_done"][u], 1)

            def square(i, u):
                act.wait_ge(m["silu_done"][u], i * 3 + 2)
                nc.scalar.activation(sq[u][:], cv[u][:, 0:2, :], ACT.Square).then_inc(m["sq_done"][u], 1)

            def rsqrt_sums(i, u):
                act.wait_ge(m["ss_done"][u], i + 1)
                nc.scalar.activation(sq[u][:], ps[:, 4 * u + 1:4 * u + 3, :], ACT.Ln, bias=s.eps[:]).then_inc(m["dln_done"][u], 1)
                act.wait_ge(m["dln_done"][u], i + 1)
                nc.scalar.activation(sq[u][:], sq[u][:], ACT.Exp, scale=-0.5).then_inc(m["dr_done"][u], 1)

            load_exp_and_ln(nc)
            act.wait_ge(par_in, 32)
            nc.scalar.activation(ea[:], alog[:], ACT.Exp).then_inc(gstep, 1)
            act.wait_ge(mset, 4)
            nc.scalar.activation(gt[2][:], gt[2][:], ACT.Exp).then_inc(gstep, 1)
            act.wait_ge(gstep, 2)
            nc.scalar.activation(gt[2][:], gt[2][:], ACT.Ln, bias=s.one[:]).then_inc(gstep, 1)
            act.wait_ge(gstep, 3)
            nc.scalar.activation(gt[3][:], s.gates[:, :, HEADS:].rearrange("p t h -> p h t"), ACT.Exp,
                                 scale=-1.0).then_inc(gstep, 1)
            act.wait_ge(gmm, 1)
            nc.scalar.activation(nbe[:], ps[:, 0, 0:HEADS * NT].rearrange("p (h c) -> p h c", h=HEADS),
                                 ACT.Exp).then_inc(gstep, 1)
            act.wait_ge(gstep, 8)
            nc.scalar.activation(kds[:], kds[:], ACT.Exp).then_inc(gstep, 1)
            for u in range(2):
                act.sem_inc(m["oln_done"][u], AHEAD)
            silu(0, 0)
            act.wait_ge(z_in, 32)
            for u in range(2):
                nc.scalar.activation(z[u], z[u], ACT.Silu).then_inc(z_done, 1)
            silu(0, 1)
            for u in range(2):
                square(0, u)
            load_exp_and_ln(nc)
            for u in range(2):
                rsqrt_sums(0, u)

            def heads(i, more):
                for u in range(2):
                    act.wait_ge(m["row_mm"][u], i + 1 + AHEAD)
                    nc.scalar.activation(eg[u][:], ps[:, 4 * u, :], ACT.Exp).then_inc(m["eg_done"][u], 1)
                for u in range(2):
                    act.wait_ge(m["diff_done"][u], i * NT + NT)
                    nc.scalar.activation(dt[u][:], dt[u][:], ACT.Exp).then_inc(m["dt_done"][u], 1)
                for u in range(2):
                    head = i * 2 + u
                    act.wait_ge(m["ktv_done"][u], i + 1)
                    for c in range(NT):
                        nc.scalar.activation(kd[u][:, c, :], chunks(ps[:, 4 * u, :])[:, c, :], ACT.Copy,
                                             scale=col(kds, head, c)).then_inc(m["kd_done"][u], 1)
                    for c in range(NT):
                        nc.scalar.activation(vb[u][:, c, :], chunks(ps[:, 4 * u + 1, :])[:, c, :], ACT.Copy,
                                             scale=col(beta, head, c)).then_inc(m["vb_done"][u], 1)
                for n, l in enumerate(LV):
                    for u in range(2):
                        act.wait_ge(m["P_mm"][u], i * len(LV) + (n + 1))
                        nc.scalar.copy(Pm[u][:], chunks(ps[:, 4 * u + 2, :])).then_inc(m["P_out"][u], 1)
                    if more and n == 3:
                        silu(i + 1, 0)
                    elif more and n == 4:
                        square(i + 1, 0)
                    elif more and n == 5:
                        silu(i + 1, 1)
                        square(i + 1, 1)
                        load_exp_and_ln(nc)
                for c in range(NT):
                    for u in range(2):
                        act.wait_ge(m["vn_mm"][u], i * NT + (c + 1))
                        nc.scalar.copy(vnew[u][:], ps[:, 4 * u, 0:P]).then_inc(m["vn_done"][u], 1)
                    if more and c - 1 in SUMS_AT:
                        rsqrt_sums(i + 1, SUMS_AT.index(c - 1))
                for u in range(2):
                    act.wait_ge(m["o_done"][u], i * NT + NT)
                    nc.scalar.activation(row(dt[u]), ps[:, 4 * u + 3, :], ACT.Square).then_inc(m["osq_done"][u], 1)
                for u in range(2):
                    act.wait_ge(m["oss_done"][u], i + 1)
                    nc.scalar.activation(row(at[u]), ps[:, 4 * u, :], ACT.Ln, scale=1.0 / P,
                                         bias=s.eps[:]).then_inc(m["oln_done"][u], 1)
                    act.wait_ge(m["oln_done"][u], i + 1 + AHEAD)
                    nc.scalar.activation(row(at[u]), row(at[u]), ACT.Exp, scale=-0.5).then_inc(m["or_done"][u], 1)
                for u in range(2):
                    act.wait_ge(m["fin_done"][u], i + 1 + AHEAD)
                    nc.scalar.copy(mix_hi[:, bass.ds(i * 2 + (HEADS + u), 1), :].rearrange("p e t -> p (e t)"),
                                   row(at[u])).then_inc(m["mh_done"][u], 1)

            with act.Fori(0, PAIRS - 1) as i:
                heads(i, True)
            heads(PAIRS - 1, False)

        @block.vector
        def _(dve):
            for u in range(2):
                for ahead in ("conv_done", "fin_done"):
                    dve.sem_inc(m[ahead][u], AHEAD)

            def conv(i, u, k, n):
                if k == 0 and n == 0:
                    dve.wait_ge(m["tiles_in"][u], i * 16 + 16)
                tap = s.taps[:, bass.ds(i * 2 + (3 * HEADS * k + HEADS * n + u), 1)]
                src = raw[u][:, n, k:k + T]
                out = cv[u][:, n, :]
                if k == 0:
                    nc.vector.tensor_scalar(out, src, tap, None, ALU.mult).then_inc(m["conv1"][u], 1)
                else:
                    dve.wait_ge(m["conv1"][u], i * 9 + (3 * (k - 1) + n + 1))
                    nc.vector.scalar_tensor_tensor(
                        out=out, in0=src, scalar=tap, in1=out, op0=ALU.mult, op1=ALU.add).then_inc(
                            m["conv_done" if k == TAPS - 1 else "conv1"][u], 1)

            for step in CONV[:len(CONV) // 2]:
                conv(0, *step)
            a_in = s.gates[:, :, 0:HEADS].rearrange("p t h -> p h t")
            dve.wait_ge(par_in, 32)
            nc.vector.tensor_tensor(gt[1][:], a_in, dtb[:].unsqueeze(2).broadcast_to([P, HEADS, NT]),
                                    ALU.add).then_inc(lstep, 1)
            dve.wait_ge(lstep, 1)
            dve.wait_ge(mset, 2)
            nc.vector.tensor_scalar(gt[0][:], gt[1][:], 0.0, None, ALU.max).then_inc(mset, 1)
            dve.wait_ge(mset, 3)
            nc.vector.scalar_tensor_tensor(out=gt[2][:], in0=gt[0][:], scalar=-2.0, in1=gt[1][:], op0=ALU.mult,
                                           op1=ALU.add).then_inc(mset, 1)
            nc.vector.tensor_tensor(jx, ji[:, 0, :], ji[:, 1, :], ALU.bitwise_xor).then_inc(lstep, 1)
            dve.wait_ge(gstep, 4)
            nc.vector.tensor_tensor(gt[0][:], gt[0][:], gt[2][:], ALU.add).then_inc(mset, 1)
            nc.vector.tensor_scalar(gt[3][:], gt[3][:], 1.0, None, ALU.add).then_inc(mset, 1)
            dve.wait_ge(mset, 6)
            nc.vector.scalar_tensor_tensor(out=g[:], in0=gt[0][:], scalar=-1.0,
                                           in1=ea[:].unsqueeze(2).broadcast_to([P, HEADS, NT]), op0=ALU.mult,
                                           op1=ALU.mult).then_inc(gstep, 1)
            nc.vector.reciprocal(beta[:], gt[3][:]).then_inc(gstep, 1)
            dve.wait_ge(gmm, 1)
            dve.wait_ge(gstep, 7)
            nc.vector.tensor_copy(gcc[:], ps[:, 0, 0:HEADS * NT].rearrange("p (h c) -> p h c", h=HEADS)).then_inc(mset, 1)
            dve.wait_ge(mset, 7)
            nc.vector.tensor_tensor(kds[:], ps[:, 1, 0:HEADS * NT].rearrange("p (h c) -> p h c", h=HEADS), gcc[:],
                                    ALU.subtract)
            nc.vector.scalar_tensor_tensor(out=nbe[:], in0=nbe[:], scalar=-1.0, in1=beta[:], op0=ALU.mult,
                                           op1=ALU.mult).then_inc(gstep, 1)
            dve.wait_ge(lstep, 2)
            for l in range(LEVELS):
                nc.vector.tensor_single_scalar(jl[:, l, :], jx, l, ALU.logical_shift_right).then_inc(mset, 1)
            dve.wait_ge(mset, 7 + LEVELS)
            nc.vector.tensor_scalar(lvl[:], jl[:], 1.0, None, ALU.is_equal).then_inc(lstep, 1)
            dve.wait_ge(lstep, 3)

            for step in CONV[len(CONV) // 2:]:
                conv(0, *step)

            def heads(i, more):
                for u in range(2):
                    head = i * 2 + u
                    dve.wait_ge(m["row_mm"][u], i + 1 + AHEAD)
                    dve.wait_ge(m["eg_done"][u], i + 1)
                    for c in range(NT):
                        nc.vector.tensor_scalar(dt[u][:, c, :], chunks(ps[:, 4 * u, :])[:, c, :], col(gcc, head, c),
                                                0.0, ALU.subtract, ALU.min).then_inc(m["diff_done"][u], 1)
                for u in range(2):
                    dve.wait_ge(m["dr_done"][u], i + 1)
                    nc.vector.scalar_tensor_tensor(out=qn[u][:], in0=cv[u][:, 0, :], scalar=P ** -0.5,
                                                   in1=sq[u][:, 0, :], op0=ALU.mult,
                                                   op1=ALU.mult).then_inc(m["qkn_done"][u], 1)
                    nc.vector.tensor_tensor(kn[u][:], cv[u][:, 1, :], sq[u][:, 1, :],
                                            ALU.mult).then_inc(m["qkn_done"][u], 1)
                for u in range(2):
                    b = 4 * u
                    dve.wait_ge(m["dtm_done"][u], i + 1)
                    dve.wait_ge(m["row_mm"][u], i + 1 + AHEAD)
                    dve.wait_ge(m["ml_done"][u], i + AHEAD)
                    nc.vector.tensor_tensor(at[u][:], dt[u][:], chunks(ps[:, b + 1, :]), ALU.mult).then_inc(m["dtb_done"][u], 1)
                    dve.wait_ge(m["kk_done"][u], i + 1)
                    dve.wait_ge(m["dtb_done"][u], i + 1)
                    nc.vector.tensor_tensor(at[u][:], at[u][:], chunks(ps[:, b + 2, :]), ALU.mult).then_inc(m["at_done"][u], 1)
                    nc.vector.tensor_tensor(qk[u][:], dt[u][:], chunks(ps[:, b + 3, :]), ALU.mult).then_inc(m["qk_done"][u], 1)
                for u in range(2):
                    dve.wait_ge(m["at_done"][u], i + 1)
                    nc.vector.scalar_tensor_tensor(out=Y[u][:], in0=at[u][:], scalar=-1.0,
                                                   in1=lvl[:, 0, :].unsqueeze(1).broadcast_to([P, NT, P]),
                                                   op0=ALU.mult, op1=ALU.mult).then_inc(m["Y0a"][u], 1)
                for u in range(2):
                    dve.wait_ge(m["Y0a"][u], i + 1)
                    nc.vector.tensor_tensor(Y[u][:], Y[u][:], s.ident[:].unsqueeze(1).broadcast_to([P, NT, P]),
                                            ALU.add).then_inc(m["Y0"][u], 1)
                for u in range(2):
                    dve.wait_ge(m["L_done"][u], i + 1)
                    nc.vector.scalar_tensor_tensor(out=X[u][:], in0=chunks(ps[:, 4 * u + 2, :]), scalar=-1.0,
                                                   in1=lvl[:, 0, :].unsqueeze(1).broadcast_to([P, NT, P]),
                                                   op0=ALU.mult, op1=ALU.mult).then_inc(m["X0"][u], 1)
                for u in range(2):
                    dve.wait_ge(m["X0"][u], i * 2 + 1)
                    nc.vector.tensor_tensor(X[u][:], X[u][:], s.ident[:].unsqueeze(1).broadcast_to([P, NT, P]),
                                            ALU.add).then_inc(m["X0"][u], 1)
                for n, l in enumerate(LV):
                    for u in range(2):
                        b = 4 * u
                        dve.wait_ge(m["XY_mm"][u], i * len(LV) + (n + 1))
                        if l < LEVELS - 1:
                            at_ = half(flat(X[u][:]), l, 0)
                            nc.vector.tensor_tensor(at_, at_, packed(ps[:, b + 3, 0:T // 2], l), ALU.subtract).then_inc(m["X_out"][u], 1)
                        at_ = half(flat(Y[u][:]), l, 1)
                        nc.vector.tensor_tensor(at_, at_, packed(ps[:, b + 2, 0:T // 2], l), ALU.subtract).then_inc(m["Y_out"][u], 1)
                    if more:
                        for step in CONV[n * PER_LEVEL:(n + 1) * PER_LEVEL]:
                            if step[1:] == (0, 0):
                                dve.wait_ge(m["ktv_done"][step[0]], i + 1)
                            conv(i + 1, *step)
                for c in range(NT):
                    for u in range(2):
                        head = i * 2 + u
                        if c:
                            dve.wait_ge(m["ks_mm"][u], i * (NT - 1) + c)
                            dve.wait_ge(m["vb_done"][u], i * NT + NT)
                            nc.vector.scalar_tensor_tensor(out=res[u][:], in0=ps[:, 4 * u, 0:P], scalar=col(nbe, head, c),
                                                           in1=vb[u][:, c, :], op0=ALU.mult,
                                                           op1=ALU.add).then_inc(m["res_done"][u], 1)
                    for u in range(2):
                        if c < NT - 1:
                            dve.wait_ge(m["su_mm"][u], i * (NT - 1) + (c + 1))
                            if c == 0:
                                nc.vector.tensor_copy(state[u][:], ps[:, 4 * u, 0:P]).then_inc(m["state_done"][u], 1)
                            else:
                                dve.wait_ge(m["state_done"][u], i * (NT - 1) + c)
                                last = (c + 1) * P - 1
                                nc.vector.scalar_tensor_tensor(out=state[u][:], in0=state[u][:],
                                                               scalar=eg[u][:, last:last + 1],
                                                               in1=ps[:, 4 * u, 0:P], op0=ALU.mult,
                                                               op1=ALU.add).then_inc(m["state_done"][u], 1)
                for u in range(2):
                    dve.wait_ge(m["or_done"][u], i + 1)
                    nc.vector.scalar_tensor_tensor(out=row(dt[u]), in0=ps[:, 4 * u + 3, :], scalar=s.wn[:, 2:3],
                                                   in1=row(at[u]), op0=ALU.mult, op1=ALU.mult).then_inc(m["on_done"][u], 1)
                for u in range(2):
                    dve.wait_ge(m["on_done"][u], i + 1)
                    dve.wait_ge(z_done, 2)
                    nc.vector.tensor_tensor(row(at[u]), row(dt[u]), z[u][:, bass.ds(i, 1), :].rearrange(
                        "p e t -> p (e t)"), ALU.mult).then_inc(m["fin_done"][u], 1)

            with dve.Fori(0, PAIRS - 1) as i:
                heads(i, True)
            heads(PAIRS - 1, False)

        @block.tensor
        def _(pe):
            pe.wait_ge(gstep, 6)
            nc.tensor.matmul(ps[:, 0, 0:HEADS * NT], s.tri[:], g[:].rearrange("p h c -> p (h c)"), start=True, stop=True)
            nc.tensor.matmul(ps[:, 1, 0:HEADS * NT], s.ones[:], g[:].rearrange("p h c -> p (h c)"), start=True,
                             stop=True).then_inc(gmm, 1)
            pe.wait_ge(gstep, 8)

            def cols(c):
                return slice(c * P, (c + 1) * P)

            def halves(c):
                return slice(c * P // 2, (c + 1) * P // 2)

            for u in range(2):
                pe.sem_inc(m["row_mm"][u], AHEAD)

            def sums(i, u):
                pe.wait_ge(m["sq_done"][u], i + 1)
                for n in range(2):
                    mm = nc.tensor.matmul(ps[:, 4 * u + 1 + n, :], s.ones[:], sq[u][:, n, :], start=True, stop=True)
                mm.then_inc(m["ss_done"][u], 1)

            for u in range(2):
                sums(0, u)

            def heads(i, more):
                for u in range(2):
                    b = 4 * u
                    pe.wait_ge(m["oln_done"][u], i + AHEAD)
                    pe.wait_ge(m["dln_done"][u], i + 1)
                    pe.wait_ge(m["rows_done"][u], i * 2 + 2)
                    nc.tensor.matmul(ps[:, b, :], s.ones[:], row_g[u][:].rearrange("p c t -> p (c t)"), start=True, stop=True)
                    nc.tensor.matmul(ps[:, b + 1, :], s.ones[:], row_b[u][:].rearrange("p c t -> p (c t)"), start=True,
                                     stop=True).then_inc(m["row_mm"][u], 1)
                for u in range(2):
                    b = 4 * u
                    pe.wait_ge(m["qkn_done"][u], i * 2 + 2)
                    pe.wait_ge(m["fin_done"][u], i + AHEAD)
                    for c in range(NT):
                        nc.tensor.matmul(ps[:, b + 2, cols(c)], kn[u][:, cols(c)], kn[u][:, cols(c)], start=True, stop=True)
                        mm = nc.tensor.matmul(ps[:, b + 3, cols(c)], kn[u][:, cols(c)], qn[u][:, cols(c)], start=True, stop=True)
                    mm.then_inc(m["kk_done"][u], 1)
                for u in range(2):
                    b = 4 * u
                    pe.wait_ge(m["diff_done"][u], i * NT + NT)
                    for c in range(NT):
                        nc.tensor.transpose(ps[:, b, cols(c)], kn[u][:, cols(c)], s.ident[:])
                    pe.wait_ge(m["dtb_done"][u], i + 1)
                    pe.wait_ge(m["silu_done"][u], i * 3 + 3)
                    for c in range(NT):
                        tp = nc.tensor.transpose(ps[:, b + 1, cols(c)], cv[u][:, 2, cols(c)], s.ident[:])
                    tp.then_inc(m["ktv_done"][u], 1)
                for u in range(2):
                    pe.wait_ge(m["at_done"][u], i + 1)
                    for c in range(NT):
                        tp = nc.tensor.transpose(ps[:, 4 * u + 2, cols(c)], at[u][:, c, :], s.ident[:])
                    tp.then_inc(m["L_done"][u], 1)
                for n, l in enumerate(LV):
                    for u in range(2):
                        if n == 0:
                            pe.wait_ge(m["X0"][u], i * 2 + 2)
                            pe.wait_ge(m["Y0"][u], i + 1)
                            pe.wait_ge(m["qk_done"][u], i + 1)
                        else:
                            pe.wait_ge(m["X_out"][u], i * (len(LV) - 1) + n)
                            pe.wait_ge(m["Y_out"][u], i * len(LV) + n)
                        pe.wait_ge(m["blk_done"][u], i * len(LV) + l)
                        for c in range(NT):
                            mm = nc.tensor.matmul(ps[:, 4 * u + 2, cols(c)], blk[u][:, l - 1, c, :], X[u][:, c, :], start=True, stop=True)
                        mm.then_inc(m["P_mm"][u], 1)
                    for u in range(2):
                        pe.wait_ge(m["P_out"][u], i * len(LV) + (n + 1))
                        for c in range(NT):
                            if l < LEVELS - 1:
                                nc.tensor.matmul(ps[:, 4 * u + 3, halves(c)], Y[u][:, c, :], half(Pm[u][:, c, :], l, 0),
                                                 start=True, stop=True)
                            mm = nc.tensor.matmul(ps[:, 4 * u + 2, halves(c)], Pm[u][:, c, :], half(Y[u][:, c, :], l, 1),
                                                  start=True, stop=True)
                        mm.then_inc(m["XY_mm"][u], 1)
                for c in range(NT):
                    if c:
                        for u in range(2):
                            pe.wait_ge(m["state_done"][u], i * (NT - 1) + c)
                            nc.tensor.matmul(ps[:, 4 * u, 0:P], kn[u][:, cols(c)], state[u][:], start=True,
                                             stop=True).then_inc(m["ks_mm"][u], 1)
                    for u in range(2):
                        if c == 0:
                            pe.wait_ge(m["Y_out"][u], i * len(LV) + len(LV))
                            pe.wait_ge(m["kd_done"][u], i * NT + NT)
                            pe.wait_ge(m["vb_done"][u], i * NT + NT)
                            right = vb[u][:, 0, :]
                        else:
                            pe.wait_ge(m["res_done"][u], i * (NT - 1) + c)
                            right = res[u][:]
                        nc.tensor.matmul(ps[:, 4 * u, 0:P], Y[u][:, c, :], right, start=True, stop=True).then_inc(m["vn_mm"][u], 1)
                    for u in range(2):
                        pe.wait_ge(m["vn_done"][u], i * NT + (c + 1))
                        out = ps[:, 4 * u + 3, cols(c)]
                        mm = nc.tensor.matmul(out, vnew[u][:], qk[u][:, c, :], start=True, stop=c == 0)
                        if c:
                            pe.wait_ge(m["qg_done"][u], i + 1)
                            mm = nc.tensor.matmul(out, state[u][:], qg[u][:, cols(c)], start=False, stop=True)
                        mm.then_inc(m["o_done"][u], 1)
                        if c < NT - 1:
                            nc.tensor.matmul(ps[:, 4 * u, 0:P], kd[u][:, c, :], vnew[u][:], start=True,
                                             stop=True).then_inc(m["su_mm"][u], 1)
                    if more and c in SUMS_AT:
                        sums(i + 1, SUMS_AT.index(c))
                for u in range(2):
                    pe.wait_ge(m["osq_done"][u], i + 1)
                    nc.tensor.matmul(ps[:, 4 * u, :], s.ones[:], row(dt[u]), start=True, stop=True).then_inc(m["oss_done"][u], 1)

            with pe.Fori(0, PAIRS - 1) as i:
                heads(i, True)
            heads(PAIRS - 1, False)


def out_proj_stage(nc, s, io, mix_hi, mix_lo, x2):
    with ExitStack() as ctx:
        def sb(name, shape, dt=F32):
            return ctx.enter_context(nc.sbuf_tensor(name, shape, dt))

        sem = ctx.enter_context(Semaphores(nc))
        raw = sb("o_raw", [P, RAW, KC, GRP])
        hi = sb("o_hi", [P, 2, KC, GRP], F32R)
        lo = sb("o_lo", [P, 2, KC, GRP], F32R)
        x_in = sem("ox_in")
        raw_in = [sem(f"ow_in{n}") for n in range(RAW)]
        hi_done = sem("ow_hi")
        lo_done = [sem(f"ow_lo{n}") for n in range(RAW)]
        mm_done = [sem(f"ow_mm{n}") for n in range(2)]
        added = [sem(f"o_added{n}") for n in range(2)]
        block = ctx.enter_context(nc.Block())
        ps = s.ps
        CH = KT // KC
        BODY = 2 * CH
        PAIRS = D // GRP // 2

        @block.sync
        def _(sp):
            with sp.Fori(0, PAIRS) as pair:
                for ch in range(BODY):
                    sp.wait_ge(lo_done[ch % RAW], pair * (BODY // RAW) + (ch // RAW + AHEAD))
                    sp.dma_start(raw[:, ch % RAW], io.w_o_v[:, ch % CH * KC:(ch % CH + 1) * KC, bass.ds(
                        pair * (2 * GRP) + ch // CH * GRP, GRP)]).then_inc(raw_in[ch % RAW], 16)

        @block.gpsimd
        def _(pool):
            pool.wait_ge(raw_in[RAW - 1], 16)
            pool.dma_start(x2[:], io.x.rearrange("(t p) d -> p t d", p=P)).then_inc(x_in, 16)

        @block.scalar
        def _(act):
            with act.Fori(0, PAIRS) as pair:
                for ch in range(BODY):
                    act.wait_ge(raw_in[ch % RAW], pair * (16 * BODY // RAW) + 16 * (ch // RAW + 1))
                    act.wait_ge(mm_done[ch % 2], pair * (BODY // 2) + (ch // 2 + AHEAD))
                    nc.scalar.copy(hi[:, ch % 2], raw[:, ch % RAW]).then_inc(hi_done, 1)

        @block.vector
        def _(dve):
            for ahead in (*lo_done, *added):
                dve.sem_inc(ahead, AHEAD)
            with dve.Fori(0, PAIRS) as pair:
                for ch in range(BODY):
                    dve.wait_ge(hi_done, pair * BODY + (ch + 1))
                    nc.vector.tensor_tensor(lo[:, ch % 2], raw[:, ch % RAW], hi[:, ch % 2].bitcast(F32),
                                            ALU.subtract).then_inc(lo_done[ch % RAW], 1)
                for g in range(2):
                    dve.wait_ge(mm_done[1], pair * (BODY // 2) + ((g + 1) * CH // 2 + AHEAD))
                    if g == 0:
                        dve.wait_ge(x_in, 16)
                    at = x2[:, :, bass.ds(pair * (2 * GRP) + g * GRP, GRP)]
                    nc.vector.tensor_tensor(at, ps[:, 4 * g:4 * g + 4, :], at, ALU.add).then_inc(added[g], 1)

        @block.tensor
        def _(pe):
            for ahead in mm_done:
                pe.sem_inc(ahead, AHEAD)
            with pe.Fori(0, PAIRS) as pair:
                for ch in range(BODY):
                    g, c = ch // CH, ch % CH
                    if c == 0:
                        pe.wait_ge(added[g], pair + AHEAD)
                    pe.wait_ge(lo_done[ch % RAW], pair * (BODY // RAW) + (ch // RAW + 1 + AHEAD))
                    for t in range(NT):
                        out, tok = ps[:, 4 * g + t, :], slice(t * P, (t + 1) * P)
                        for k in range(KC):
                            kt = c * KC + k
                            nc.tensor.matmul(out, mix_hi[:, kt, tok], hi[:, ch % 2, k], start=kt == 0, stop=False)
                            nc.tensor.matmul(out, mix_lo[:, kt, tok], hi[:, ch % 2, k], start=False, stop=False)
                            mm = nc.tensor.matmul(out, mix_hi[:, kt, tok], lo[:, ch % 2, k], start=False,
                                                  stop=kt == KT - 1)
                    mm.then_inc(mm_done[ch % 2], 1)


def route_stage(nc, s, io, x2, tab_pos, tab_val, items, e_raw, e_raw_in):
    NL = NG + NE
    with ExitStack() as ctx:
        def sb(name, shape, dt=F32):
            return ctx.enter_context(nc.sbuf_tensor(name, shape, dt))

        sem = ctx.enter_context(Semaphores(nc))
        xn = sb("xn", [P, NT, D])
        h2T = sb("h2T", [P, KT, T])
        wr = sb("wr", [P, KT, NL])
        bias = sb("bias", [P, NL])
        sq = sb("r_sq", [P, D])
        w2row = sb("w2row", [P, D])
        st = [sb(f"r_st{n}", [P, NT]) for n in range(4)]
        lgT = sb("r_lgT", [NL, T])
        lg = sb("r_lg", [P, NT, NL])
        gmx, gsum, gg = sb("gmx", [P, NT]), sb("gsum", [P, NT]), sb("gg", [P, NT])
        gd, gsc, goh = sb("gd", [P, NT, NG]), sb("gsc", [P, NT, NG]), sb("goh", [P, NT, NG])
        picked = sb("picked", [P, NT, NG, PER])
        inl = sb("inl", [P, NT, PER])
        ex = [sb(f"r_ex{n}", [P, NT, PER]) for n in range(2)]
        esc = sb("esc", [P, NT, PER])
        eoh = [sb(f"eoh{n}", [P, NT, PER]) for n in range(2)]
        emx = [sb(f"emx{n}", [P, NT]) for n in range(2)]
        smx = sb("smx", [P, NT])
        gate = [sb(f"gate{n}", [P, NT]) for n in range(2)]
        den = sb("den", [P, NT])
        M = [sb(f"M{n}", [P, NT, NE]) for n in range(3)]
        gm = [sb(f"gm{n}", [P, NT, NE]) for n in range(2)]
        posm = sb("posm", [P, NT, NE])
        desc = sb("desc", [P, PER])
        tok = sb("tok", [P, NT])
        cnt = sb("cnt", [P, NE])
        NX = (BLKS - 1) * NE
        xcode, xexp = sb("xcode", [1, NX]), sb("xexp", [1, NX])
        kk, two = sb("kk", [1, EXTRA + 1]), sb("two", [1, NG])
        flag, rank, onesr = sb("flag", [1, NX]), sb("rank", [1, NX]), sb("onesr", [1, NX])
        fc = sb("fc", [1, 2, NX])
        hit = sb("hit", [1, EXTRA + 1, NX])
        hv = sb("hv", [1, EXTRA + 1, NX])
        xt = sb("xt", [1, 2, EXTRA + 1])
        np_ = sb("np_", [1, NG])
        npair = sb("npair", [1, 1])
        itf = sb("itf", [1, 2, N_ITEMS + 2])

        w_in, norm_in, init = sem("rw_in"), sem("r_norm_in"), sem("r_init")
        ssq, msd, recd, rstdd, xnd, stored = (sem(n) for n in ("r_ssq", "r_ms", "r_rec", "r_rstd", "r_xn", "r_stored"))
        tpd, h2d, lgm, act_exp, chain = (sem(n) for n in ("r_tp", "r_h2", "r_lgm", "r_exp", "r_chain"))
        m_done, pos_mm = sem("m_done"), sem("pos_mm")
        block = ctx.enter_context(nc.Block())
        ps = s.ps

        @block.sync
        def _(sp):
            sp.dma_start(wr[:, :, 0:NG], io.w_group.rearrange("(k p) n -> p k n", p=P)).then_inc(w_in, 16)
            sp.dma_start(wr[:, :, NG:NL], io.w_expert.rearrange("(k p) n -> p k n", p=P)).then_inc(w_in, 16)
            sp.dma_start(bias[:, 0:NG], io.b_group.broadcast_to([P, NG])).then_inc(w_in, 16)
            sp.dma_start(bias[:, NG:NL], io.b_expert.broadcast_to([P, NE])).then_inc(w_in, 16)
            sp.dma_start(w2row[:], io.norm2_row.broadcast_to([P, D])).then_inc(norm_in, 16)
            for ch in range(RAW):
                sp.dma_start(e_raw[:, ch], io.w1_v[:, 0, ch * KC:(ch + 1) * KC, :]).then_inc(e_raw_in[ch], 16)
            for t in range(NT):
                sp.wait_ge(xnd, t + 1)
                sp.dma_start(io.xn[t * P:(t + 1) * P, :], xn[:, t, :]).then_inc(stored, 16)
            sp.dma_start(io.out.rearrange("(t p) d -> p t d", p=P), x2[:]).then_inc(stored, 16)
            sp.wait_ge(stored, NT * 16 + 16)

        @block.gpsimd
        def _(pool):
            fl = dict(allow_small_or_imprecise_dtypes=True)
            pool.iota(desc[:], [[-1, PER]], base=PER, channel_multiplier=0, **fl).then_inc(init, 1)
            pool.iota(tok[:], [[P, NT]], base=-int(BIG), channel_multiplier=1, **fl).then_inc(init, 1)
            pool.iota(xcode[:], [[1, NX]], base=NE - PAD_CODE, channel_multiplier=0, **fl).then_inc(init, 1)
            pool.iota(xexp[:], [[0, BLKS - 1], [1, NE]], base=0, channel_multiplier=0, **fl).then_inc(init, 1)
            pool.iota(kk[:], [[1, EXTRA + 1]], base=1, channel_multiplier=0, **fl).then_inc(init, 1)
            pool.iota(two[:], [[2, NG]], base=0, channel_multiplier=0, **fl).then_inc(init, 1)
            pool.iota(itf[:], [[0, 2], [1, N_ITEMS + 2]], base=0, channel_multiplier=0, **fl).then_inc(init, 1)
            pool.iota(s.slot[:], [[1, P]], base=0, channel_multiplier=0, **fl).then_inc(init, 1)
            pool.memset(onesr[:], 1.0).then_inc(init, 1)
            pool.memset(tab_pos[:, PAD_CODE, :], -1.0).then_inc(init, 1)
            pool.memset(tab_val[:, PAD_CODE], 0.0).then_inc(init, 1)

        @block.scalar
        def _(act):
            for t in range(NT):
                if t:
                    act.wait_ge(ssq, t)
                nc.scalar.activation(sq[:], x2[:, t, :], ACT.Square, accum_out=st[0][:, t:t + 1]).then_inc(ssq, 1)
                if t:
                    act.wait_ge(recd, t)
                    nc.scalar.activation(st[3][:, t - 1:t], st[2][:, t - 1:t], ACT.Sqrt).then_inc(rstdd, 1)
            act.wait_ge(recd, NT)
            nc.scalar.activation(st[3][:, NT - 1:], st[2][:, NT - 1:], ACT.Sqrt).then_inc(rstdd, 1)
            for r in range(NT * KQ):
                t, q = r // KQ, r % KQ
                act.wait_ge(tpd, r + 1)
                nc.scalar.copy(h2T[:, 4 * q:4 * q + 4, t * P:(t + 1) * P], ps[:, 2 + r % 4, :].rearrange(
                    "p (k t) -> p k t", k=4)).then_inc(h2d, 1)
            act.wait_ge(chain, 3)
            nc.scalar.activation(gsc[:], gd[:], ACT.Exp).then_inc(act_exp, 1)
            act.wait_ge(chain, 11)
            nc.scalar.activation(ex[0][:], inl[:], ACT.Exp).then_inc(act_exp, 1)

        @block.vector
        def _(dve):
            count = [0]

            def step(ins):
                count[0] += 1
                ins.then_inc(chain, 1)
                dve.wait_ge(chain, count[0])

            def wide(ap, n):
                return ap.unsqueeze(2).broadcast_to([P, NT, n])

            def first_max(values, peak, score, onehot, n):
                step(nc.vector.tensor_reduce(peak[:], values[:], AX.X, ALU.max))
                step(nc.vector.tensor_tensor(score[:], values[:], wide(peak[:], n), ALU.is_equal))
                step(nc.vector.tensor_tensor(score[:], score[:], desc[:, PER - n:].unsqueeze(1).broadcast_to([P, NT, n]),
                                             ALU.mult))
                step(nc.vector.tensor_reduce(smx[:], score[:], AX.X, ALU.max))
                step(nc.vector.tensor_tensor(onehot[:], score[:], wide(smx[:], n), ALU.is_equal))

            dve.wait_ge(norm_in, 16)
            for t in range(NT):
                at = slice(t, t + 1)
                dve.wait_ge(ssq, t + 1)
                nc.vector.tensor_scalar(st[1][:, at], st[0][:, at], 1.0 / D, EPS, ALU.mult, ALU.add).then_inc(msd, 1)
                dve.wait_ge(msd, t + 1)
                nc.vector.reciprocal(st[2][:, at], st[1][:, at]).then_inc(recd, 1)
                dve.wait_ge(rstdd, t + 1)
                nc.vector.scalar_tensor_tensor(out=xn[:, t, :], in0=x2[:, t, :], scalar=st[3][:, t:t + 1], in1=w2row[:],
                                               op0=ALU.mult, op1=ALU.mult).then_inc(xnd, 1)
            dve.wait_ge(init, 11)
            dve.wait_ge(lgm, 1)
            nc.vector.tensor_copy(lgT[:], ps[0:NL, 0, :]).then_inc(lgm, 1)
            dve.wait_ge(lgm, 3)
            step(nc.vector.tensor_tensor(lg[:], ps[:, 1, 0:NT * NL].rearrange("p (t n) -> p t n", t=NT),
                                         bias[:].unsqueeze(1).broadcast_to([P, NT, NL]), ALU.add))
            step(nc.vector.tensor_reduce(gmx[:], lg[:, :, 0:NG], AX.X, ALU.max))
            step(nc.vector.tensor_tensor(gd[:], lg[:, :, 0:NG], wide(gmx[:], NG), ALU.subtract))
            dve.wait_ge(act_exp, 1)
            step(nc.vector.tensor_reduce(gsum[:], gsc[:], AX.X, ALU.add))
            step(nc.vector.reciprocal(gg[:], gsum[:]))
            step(nc.vector.tensor_scalar(gsc[:], gd[:], 0.0, None, ALU.is_equal))
            step(nc.vector.tensor_tensor(gsc[:], gsc[:], desc[:, PER - NG:].unsqueeze(1).broadcast_to([P, NT, NG]),
                                         ALU.mult))
            step(nc.vector.tensor_reduce(smx[:], gsc[:], AX.X, ALU.max))
            step(nc.vector.tensor_tensor(goh[:], gsc[:], wide(smx[:], NG), ALU.is_equal))
            for t in range(NT):
                ins = nc.vector.tensor_tensor(picked[:, t], lg[:, t, NG:NL].rearrange("p (g e) -> p g e", g=NG),
                                              goh[:, t].unsqueeze(2).broadcast_to([P, NG, PER]), ALU.mult)
            ins.then_inc(m_done, 1)
            dve.wait_ge(m_done, 1)
            step(nc.vector.tensor_reduce(inl[:], picked[:].rearrange("p t g e -> p t e g"), AX.X, ALU.add))
            ins = nc.vector.tensor_reduce(emx[0][:], inl[:], AX.X, ALU.max)
            ins.then_inc(m_done, 1)
            dve.wait_ge(m_done, 2)
            step(nc.vector.tensor_tensor(inl[:], inl[:], wide(emx[0][:], PER), ALU.subtract))
            dve.wait_ge(act_exp, 2)
            first_max(ex[0], emx[0], esc, eoh[0], PER)
            step(nc.vector.scalar_tensor_tensor(out=ex[1][:], in0=eoh[0][:], scalar=-2.0, in1=ex[0][:], op0=ALU.mult,
                                                op1=ALU.add))
            first_max(ex[1], emx[1], esc, eoh[1], PER)
            step(nc.vector.tensor_tensor(den[:], emx[0][:], emx[1][:], ALU.add))
            step(nc.vector.reciprocal(den[:], den[:]))
            step(nc.vector.tensor_tensor(den[:], den[:], gg[:], ALU.mult))
            for n in range(2):
                step(nc.vector.tensor_tensor(gate[n][:], den[:], emx[n][:], ALU.mult))
                for t in range(NT):
                    ins = nc.vector.tensor_tensor(M[n][:, t, :].rearrange("p (g e) -> p g e", g=NG),
                                                  goh[:, t].unsqueeze(2).broadcast_to([P, NG, PER]),
                                                  eoh[n][:, t].unsqueeze(1).broadcast_to([P, NG, PER]), ALU.mult)
                step(ins)
            nc.vector.tensor_tensor(M[2][:], M[0][:], M[1][:], ALU.add).then_inc(m_done, 1)
            val = tab_val[:, 0:NE].rearrange("p e t v -> p t e v")
            for n in range(2):
                step(nc.vector.tensor_tensor(gm[n][:], M[n][:], wide(gate[n][:], NE), ALU.mult))
            step(nc.vector.tensor_tensor(val[:, :, :, 1], gm[0][:], gm[1][:], ALU.add))
            step(nc.vector.tensor_copy(val[:, :, :, 0], wide(tok[:], NE)))
            for b in range(1, BLKS):
                ins = nc.vector.tensor_copy(tab_val[:, b * NE:(b + 1) * NE], tab_val[:, 0:NE])
            step(ins)
            dve.wait_ge(pos_mm, 1)
            step(nc.vector.scalar_tensor_tensor(out=posm[:], in0=ps[:, 0, 0:NT * NE].rearrange("p (t e) -> p t e", t=NT),
                                                scalar=1.0, in1=M[2][:], op0=ALU.add, op1=ALU.mult))
            for b in range(BLKS):
                ins = nc.vector.tensor_scalar(tab_pos[:, b * NE:(b + 1) * NE, :], posm[:].rearrange("p t e -> p e t"),
                                              -1.0 - P * b, None, ALU.add)
            step(ins)
            step(nc.vector.tensor_copy(cnt[:], ps[:, 1, 0:NE]))
            for b in range(1, BLKS):
                ins = nc.vector.tensor_scalar(flag[:, (b - 1) * NE:b * NE], cnt[0:1, :], float(P * b), None, ALU.is_gt)
            step(ins)
            step(nc.vector.tensor_tensor_scan(rank[:], onesr[:], flag[:], 0.0, ALU.mult, ALU.add))
            step(nc.vector.tensor_tensor(fc[:, 0], flag[:], xcode[:], ALU.mult))
            step(nc.vector.tensor_tensor(fc[:, 1], flag[:], xexp[:], ALU.mult))
            big = [1, EXTRA + 1, NX]
            step(nc.vector.tensor_tensor(hit[:], rank[:].unsqueeze(1).broadcast_to(big), kk[:].unsqueeze(2).broadcast_to(big),
                                         ALU.is_equal))
            for n in range(2):
                step(nc.vector.tensor_tensor(hv[:], hit[:], fc[:, n].unsqueeze(1).broadcast_to(big), ALU.mult))
                step(nc.vector.tensor_reduce(xt[:, n], hv[:], AX.X, ALU.add))
            step(nc.vector.tensor_scalar(itf[:, 0, NE:NE + EXTRA + 1], xt[:, 0], float(PAD_CODE), None, ALU.add))
            nc.vector.memset(itf[:, 0, N_ITEMS:], float(PAD_CODE))
            nc.vector.memset(itf[:, 1, N_ITEMS:], 0.0)
            step(nc.vector.tensor_copy(itf[:, 1, NE:NE + EXTRA + 1], xt[:, 1]))
            step(nc.vector.tensor_tensor(np_[:], rank[:, NX - 1:NX].broadcast_to([1, NG]), two[:], ALU.is_gt))
            step(nc.vector.tensor_reduce(npair[:], np_[:], AX.X, ALU.add))
            nc.vector.tensor_scalar(items[:, 2, 0:1], npair[:], float(NE // 2), None, ALU.add)
            step(nc.vector.tensor_copy(items[:, 0:2, :], itf[:]))

        @block.tensor
        def _(pe):
            pe.wait_ge(w_in, 64)
            for t in range(NT):
                pe.wait_ge(xnd, t + 1)
                for q in range(KQ):
                    r = t * KQ + q
                    if r >= 4:
                        pe.wait_ge(h2d, r - 3)
                    for j in range(4):
                        k = 4 * q + j
                        tp = nc.tensor.transpose(ps[:, 2 + r % 4, j * P:(j + 1) * P], xn[:, t, k * P:(k + 1) * P], s.ident[:])
                    tp.then_inc(tpd, 1)
                for k in range(KT):
                    if k % 4 == 0:
                        pe.wait_ge(h2d, t * KQ + k // 4 + 1)
                    mm = nc.tensor.matmul(ps[0:NL, 0, t * P:(t + 1) * P], wr[:, k, :], h2T[:, k, t * P:(t + 1) * P],
                                          start=k == 0, stop=k == KT - 1)
            mm.then_inc(lgm, 1)
            pe.wait_ge(lgm, 2)
            for t in range(NT):
                tp = nc.tensor.transpose(ps[:, 1, t * NL:(t + 1) * NL], lgT[:, t * P:(t + 1) * P], s.ident[0:NL, 0:NL])
            tp.then_inc(lgm, 1)
            pe.wait_ge(m_done, 3)
            for t in range(NT):
                for t2 in range(t + 1):
                    nc.tensor.matmul(ps[:, 0, t * NE:(t + 1) * NE], (s.tri_s if t2 == t else s.ones)[:], M[2][:, t2, :],
                                     start=t2 == 0, stop=t2 == t)
            for t in range(NT):
                mm = nc.tensor.matmul(ps[:, 1, 0:NE], s.ones[:], M[2][:, t, :], start=t == 0, stop=t == NT - 1)
            mm.then_inc(pos_mm, 1)


def expert_stage(nc, s, io, tab_pos, tab_val, items, raw, raw_in):
    with ExitStack() as ctx:
        def sb(name, shape, dt=F32):
            return ctx.enter_context(nc.sbuf_tensor(name, shape, dt))

        sem = ctx.enter_context(Semaphores(nc))
        SPLIT = 3
        hi = sb("e_hi", [P, SPLIT, KC, FE], F32R)
        lo = sb("e_lo", [P, SPLIT, KC, FE], F32R)
        sel = sb("e_sel", [P, NT, P])
        next_i = [sb(f"e_next_i{u}", [P, 1], U32) for u in range(2)]
        next_g = [sb(f"e_next_g{u}", [P, 1]) for u in range(2)]
        row_i = [sb(f"e_row_i{u}", [P, 1], U32) for u in range(2)]
        gate = [sb(f"e_gate{u}", [P, 1]) for u in range(2)]
        xg = [sb(f"e_xg{u}", [P, D]) for u in range(2)]
        xT_hi = [sb(f"e_xh{u}", [P, KT, P], F32R) for u in range(2)]
        xT_lo = [sb(f"e_xl{u}", [P, KT, P], F32R) for u in range(2)]
        act_g = sb("e_act", [P, FE])
        hid = sb("e_hid", [P, FE])
        hT_hi = sb("e_hh", [P, KC, P], F32R)
        hT_lo = sb("e_hl", [P, KC, P], F32R)
        y = [sb(f"e_y{u}", [P, D]) for u in range(2)]
        warm = sb("e_warm", [P, 1])
        hi_done = sem("ew_hi")
        lo_done = [sem(f"ew_lo{n}") for n in range(RAW)]
        mm_done = [sem(f"ew_mm{n}") for n in range(SPLIT)]
        go, zero, sel_done, tab_mm, slot_done = sem("e_go"), sem("e_zero"), sem("e_sel_done"), sem("e_tab_mm"), sem("e_slot_done")
        rows_in = [sem(f"e_rows{u}") for u in range(2)]
        xt_mm, xhi_done, xlo_done = sem("e_xt_mm"), sem("e_xhi"), sem("e_xlo")
        silu_done, hid_done, ht_mm, hh_done, hl_done = (sem(n) for n in ("e_silu", "e_hid_done", "e_ht", "e_hh_done", "e_hl_done"))
        y_done, moved = sem("e_y_done"), sem("e_moved")
        scattered = [sem(f"e_scat{u}") for u in range(2)]
        y_free = [sem(f"e_y_free{u}") for u in range(2)]
        block = ctx.enter_context(nc.Block())
        ps = s.ps
        G, U, XB, HB, YB, TB = 0, 1, 2, 4, 5, 7
        XR = KT // 4
        CH = CH_PER_ITEM
        UP, GATE, DOWN = (0, 1, 2, 3), (4, 5, 10, 11), (6, 7, 8, 9)
        PRE = len(GATE)

        def slot_of(q, ring):
            return (PRE + q) % ring

        def before(k, q, ring):
            return k * (CH // ring) + (PRE + q) // ring

        def n_pairs(eng):
            return eng.value_load(items[0:1, 2, 0:1], min_val=NE // 2, max_val=N_ITEMS // 2)

        def item(eng, row, k, top):
            return eng.value_load(items[0:1, row, bass.ds(k, 1)], min_val=0, max_val=top)

        @block.sync
        def _(sp):
            def load(k, q, src):
                n = slot_of(q, RAW)
                sp.wait_ge(lo_done[n], before(k, q, RAW))
                sp.dma_start(raw[:, n], src.rearrange("p e k n -> p (e k) n")).then_inc(raw_in[n], 16)

            pairs = n_pairs(sp)
            with sp.Fori(0, pairs) as i:
                for u in range(2):
                    k = i * 2 + u
                    e, e_next = item(sp, 1, k, NE - 1), item(sp, 1, k + 1, NE - 1)
                    for q in range(CH):
                        if q in UP:
                            c = UP.index(q)
                            load(k, q, io.w3_v[:, bass.ds(e, 1), c * KC:(c + 1) * KC, :])
                        elif q in GATE:
                            c = GATE.index(q)
                            load(k, q, io.w1_v[:, bass.ds(e_next, 1), c * KC:(c + 1) * KC, :])
                        else:
                            c = DOWN.index(q)
                            load(k, q, io.w2_v[:, bass.ds(e, 1), :, c * FE:(c + 1) * FE])

        @block.gpsimd
        def _(pool):
            for u in range(2):
                pool.memset(xg[u][:], 0.0).then_inc(zero, 1)
            pool.wait_ge(zero, 2)

            def gather(k, u):
                pool.wait_ge(slot_done, k + 1)
                pool.sem_inc(go, 1)
                pool.indirect_dma_start(out=xg[u][:], out_offset=None, in_=io.xn,
                                        in_offset=bass.IndirectOffsetOnAxis(ap=next_i[u][:, 0:1], axis=0),
                                        bounds_check=T - 1, oob_is_err=False).then_inc(rows_in[u], 16)

            for u in range(2):
                pool.sem_inc(y_free[u], AHEAD)
            for u in range(2):
                gather(u, u)
            pairs = n_pairs(pool)
            with pool.Fori(0, pairs) as i:
                for u in range(2):
                    k = i * 2 + u
                    pool.wait_ge(xt_mm, k * XR + XR)
                    gather(k + 2, u)
                    pool.wait_ge(y_done, k * 4 + 4)
                    pool.sem_inc(go, 1)
                    pool.indirect_dma_start(out=io.out, out_offset=bass.IndirectOffsetOnAxis(
                        ap=row_i[u][:, 0:1], axis=0), in_=y[u][:], in_offset=None, bounds_check=T - 1,
                        oob_is_err=False, compute_op=ALU.add).then_inc(scattered[u], 16)
                    pool.wait_ge(scattered[u], i * 16 + 16)
                    pool.sem_inc(y_free[u], 1)

        @block.scalar
        def _(act):
            def split(k, q):
                n, m = slot_of(q, RAW), slot_of(q, SPLIT)
                act.wait_ge(raw_in[n], before(k, q, RAW) * 16 + 16)
                if q >= SPLIT - PRE:
                    act.wait_ge(mm_done[m], before(k, q, SPLIT))
                nc.scalar.copy(hi[:, m], raw[:, n]).then_inc(hi_done, 1)

            def x_hi(k, u, r):
                act.wait_ge(xt_mm, k * XR + (r + 1))
                nc.scalar.copy(xT_hi[u][:, 4 * r:4 * r + 4], ps[:, XB + r % 2, :].rearrange(
                    "p (f t) -> p f t", f=4)).then_inc(xhi_done, 1)

            def y_out(k, u, c):
                if c == 0:
                    act.wait_ge(slot_done, k + 3)
                act.wait_ge(mm_done[slot_of(DOWN[c], SPLIT)], before(k, DOWN[c], SPLIT) + 1)
                nc.scalar.activation(y[u][:, c * FE:(c + 1) * FE], ps[:, YB + c % 2, :], ACT.Copy,
                                     scale=gate[u][:, 0:1]).then_inc(y_done, 1)

            nc.scalar.activation(warm[:], s.one[:], ACT.Silu)
            split(0, -4)
            split(0, -3)
            for r in range(XR):
                x_hi(0, 0, r)
            split(0, -2)
            split(0, -1)
            for r in range(XR):
                x_hi(1, 1, r)
            pairs = n_pairs(act)
            with act.Fori(0, pairs) as i:
                for u in range(2):
                    k = i * 2 + u
                    split(k, 0)
                    split(k, 1)
                    act.wait_ge(mm_done[slot_of(-1, SPLIT)], before(k, -1, SPLIT) + 1)
                    nc.scalar.activation(act_g[:], ps[:, G, :], ACT.Silu).then_inc(silu_done, 1)
                    for q in range(2, 7):
                        split(k, q)
                    act.wait_ge(ht_mm, k + 1)
                    nc.scalar.copy(hT_hi[:], ps[:, HB, :].rearrange("p (f t) -> p f t", f=KC)).then_inc(hh_done, 1)
                    split(k, 7)
                    x_hi(k + 2, u, 0)
                    x_hi(k + 2, u, 1)
                    split(k, 8)
                    y_out(k, u, 0)
                    x_hi(k + 2, u, 2)
                    split(k, 9)
                    y_out(k, u, 1)
                    x_hi(k + 2, u, 3)
                    split(k, 10)
                    y_out(k, u, 2)
                    split(k, 11)
                    y_out(k, u, 3)

        @block.vector
        def _(dve):
            def split(k, q):
                n, m = slot_of(q, RAW), slot_of(q, SPLIT)
                dve.wait_ge(hi_done, k * CH + (PRE + q + 1))
                nc.vector.tensor_tensor(lo[:, m], raw[:, n], hi[:, m].bitcast(F32), ALU.subtract).then_inc(lo_done[n], 1)

            def select(k, code):
                for t in range(NT):
                    ins = nc.vector.tensor_scalar(sel[:, t, :], s.slot[:], tab_pos[:, bass.ds(code, 1), t:t + 1].rearrange(
                        "p c t -> p (c t)"), None, ALU.is_equal)
                ins.then_inc(sel_done, 1)

            def slots(k, u):
                dve.wait_ge(tab_mm, k + 1)
                nc.vector.tensor_copy(next_g[u][:], ps[:, TB, 1:2])
                nc.vector.tensor_scalar(next_i[u][:], ps[:, TB, 0:1], BIG, None, ALU.add).then_inc(slot_done, 1)

            def x_lo(k, u, r):
                dve.wait_ge(xhi_done, k * XR + (r + 1))
                nc.vector.tensor_tensor(xT_lo[u][:, 4 * r:4 * r + 4], ps[:, XB + r % 2, :].rearrange(
                    "p (f t) -> p f t", f=4), xT_hi[u][:, 4 * r:4 * r + 4].bitcast(F32), ALU.subtract).then_inc(xlo_done, 1)

            for u in range(2):
                select(u, item(dve, 0, u, PAD_CODE))
                slots(u, u)
            split(0, -4)
            for r in range(XR):
                x_lo(0, 0, r)
            for q in (-3, -2, -1):
                split(0, q)
            for r in range(XR):
                x_lo(1, 1, r)
            pairs = n_pairs(dve)
            with dve.Fori(0, pairs) as i:
                for u in range(2):
                    k = i * 2 + u
                    split(k, 0)
                    select(k + 2, item(dve, 0, k + 2, PAD_CODE))
                    split(k, 1)
                    dve.wait_ge(y_free[u], i + AHEAD)
                    nc.vector.tensor_copy(row_i[u][:], next_i[u][:])
                    nc.vector.tensor_copy(gate[u][:], next_g[u][:]).then_inc(moved, 1)
                    split(k, 2)
                    dve.wait_ge(moved, k + 1)
                    slots(k + 2, u)
                    split(k, 3)
                    split(k, 4)
                    dve.wait_ge(silu_done, k + 1)
                    dve.wait_ge(mm_done[slot_of(UP[3], SPLIT)], before(k, UP[3], SPLIT) + 1)
                    nc.vector.tensor_tensor(hid[:], act_g[:], ps[:, U, :], ALU.mult).then_inc(hid_done, 1)
                    split(k, 5)
                    dve.wait_ge(hh_done, k + 1)
                    nc.vector.tensor_tensor(hT_lo[:], ps[:, HB, :].rearrange("p (f t) -> p f t", f=KC),
                                            hT_hi[:].bitcast(F32), ALU.subtract).then_inc(hl_done, 1)
                    split(k, 6)
                    split(k, 7)
                    x_lo(k + 2, u, 0)
                    x_lo(k + 2, u, 1)
                    split(k, 8)
                    x_lo(k + 2, u, 2)
                    split(k, 9)
                    x_lo(k + 2, u, 3)
                    split(k, 10)
                    split(k, 11)

        @block.tensor
        def _(pe):
            def table(k, code, first):
                pe.wait_ge(sel_done, k + 1)
                if not first:
                    pe.wait_ge(slot_done, k)
                for t in range(NT):
                    mm = nc.tensor.matmul(ps[:, TB, 0:2], sel[:, t, :], tab_val[:, bass.ds(code, 1), t, :].rearrange(
                        "p c v -> p (c v)"), start=t == 0, stop=t == NT - 1)
                mm.then_inc(tab_mm, 1)

            def transpose_x(k, u, r, n_rows, fresh=False):
                if r == 0:
                    pe.wait_ge(rows_in[u], n_rows)
                if not fresh:
                    pe.wait_ge(xlo_done, k * XR + (r - 1))
                for j in range(4):
                    f = 4 * r + j
                    tp = nc.tensor.transpose(ps[:, XB + r % 2, j * P:(j + 1) * P], xg[u][:, f * P:(f + 1) * P], s.ident[:])
                tp.then_inc(xt_mm, 1)

            def three(out, a_hi, a_lo, b_hi, b_lo, first, last):
                nc.tensor.matmul(out, a_hi, b_hi, start=first, stop=False)
                nc.tensor.matmul(out, a_lo, b_hi, start=False, stop=False)
                return nc.tensor.matmul(out, a_hi, b_lo, start=False, stop=last)

            def chunk(k, q, bank, a_hi, a_lo, c, n_chunks):
                n, m = slot_of(q, RAW), slot_of(q, SPLIT)
                pe.wait_ge(lo_done[n], before(k, q, RAW) + 1)
                for j in range(KC):
                    f = c * KC + j
                    mm = three(ps[:, bank, :], a_hi[:, f, :], a_lo[:, f, :], hi[:, m, j], lo[:, m, j],
                               f == 0, f == n_chunks * KC - 1)
                mm.then_inc(mm_done[m], 1)

            for u in range(2):
                table(u, item(pe, 0, u, PAD_CODE), u == 0)
            for r in range(XR):
                transpose_x(0, 0, r, 16, fresh=r < 2)
            pe.wait_ge(xlo_done, XR)
            for c in range(PRE):
                chunk(0, c - PRE, G, xT_hi[0], xT_lo[0], c, PRE)
            for r in range(XR):
                transpose_x(1, 1, r, 16)
            pairs = n_pairs(pe)
            with pe.Fori(0, pairs) as i:
                for u in range(2):
                    k = i * 2 + u
                    n_rows = i * 16 + 32
                    for q in range(CH):
                        if q in UP:
                            chunk(k, q, U, xT_hi[u], xT_lo[u], UP.index(q), 4)
                        elif q in GATE:
                            if q == GATE[0]:
                                pe.wait_ge(silu_done, k + 1)
                                pe.wait_ge(xlo_done, k * XR + 2 * XR)
                            chunk(k, q, G, xT_hi[1 - u], xT_lo[1 - u], GATE.index(q), 4)
                        else:
                            c = DOWN.index(q)
                            if c == 0:
                                pe.wait_ge(hl_done, k + 1)
                            if c >= 2:
                                pe.wait_ge(y_done, k * 4 + (c - 1))
                            chunk(k, q, YB + c % 2, hT_hi, hT_lo, 0, 1)
                        if q == 1:
                            table(k + 2, item(pe, 0, k + 2, PAD_CODE), False)
                        elif q == 4:
                            pe.wait_ge(hid_done, k + 1)
                            for j in range(KC):
                                tp = nc.tensor.transpose(ps[:, HB, j * P:(j + 1) * P], hid[:, j * P:(j + 1) * P], s.ident[:])
                            tp.then_inc(ht_mm, 1)
                        elif q == 5:
                            transpose_x(k + 2, u, 0, n_rows)
                            transpose_x(k + 2, u, 1, n_rows)
                        elif q in (6, 7):
                            transpose_x(k + 2, u, q - 4, n_rows)


def program(nc, io):
    with ExitStack() as ctx:
        s = shared(nc, ctx)
        with ExitStack() as front:
            hT_hi = front.enter_context(nc.sbuf_tensor("hT_hi", [P, KT, T], F32R))
            hT_lo = front.enter_context(nc.sbuf_tensor("hT_lo", [P, KT, T], F32R))
            sem = front.enter_context(Semaphores(nc))
            w_raw = front.enter_context(nc.sbuf_tensor("w_raw", [P, RAW, KC, GRP], F32))
            w_raw_in = [sem(f"pw_in{n}") for n in range(RAW)]
            setup_stage(nc, s, io, hT_hi, hT_lo, w_raw, w_raw_in)
            project_stage(nc, s, io, hT_hi, hT_lo, w_raw, w_raw_in)
        x2 = ctx.enter_context(nc.sbuf_tensor("x2", [P, NT, D], F32))
        with ExitStack() as mixed:
            mix_hi = mixed.enter_context(nc.sbuf_tensor("mix_hi", [P, KT, T], F32R))
            mix_lo = mixed.enter_context(nc.sbuf_tensor("mix_lo", [P, KT, T], F32R))
            stick_stage(nc, s, io, mix_hi, mix_lo)
            delta_stage(nc, s, io, mix_hi, mix_lo, x2)
            out_proj_stage(nc, s, io, mix_hi, mix_lo, x2)
        with ExitStack() as back:
            tab_pos = back.enter_context(nc.sbuf_tensor("tab_pos", [P, PAD_CODE + 1, NT], F32))
            tab_val = back.enter_context(nc.sbuf_tensor("tab_val", [P, PAD_CODE + 1, NT, 2], F32))
            items = back.enter_context(nc.sbuf_tensor("items", [1, 3, N_ITEMS + 2], I32))
            sem = back.enter_context(Semaphores(nc))
            e_raw = back.enter_context(nc.sbuf_tensor("e_raw", [P, RAW, KC, FE], F32))
            e_raw_in = [sem(f"ew_in{n}") for n in range(RAW)]
            route_stage(nc, s, io, x2, tab_pos, tab_val, items, e_raw, e_raw_in)
            expert_stage(nc, s, io, tab_pos, tab_val, items, e_raw, e_raw_in)


def views(io, a):
    io.x = a["x"].rearrange("b t d -> (b t) d")
    io.norm1_row = a["norm1_w"]
    io.norm2_row = a["norm2_w"]
    io.conv_w = a["gdn_conv_w"].rearrange("l n (c p) -> (l n c) p", p=P)
    io.q_norm_w, io.k_norm_w, io.out_norm_w = a["sb_q_norm_w"], a["sb_k_norm_w"], a["gdn_out_norm_w"]
    io.a_log, io.dt_bias = a["gdn_a_log"], a["gdn_dt_bias"]
    io.w_in_v = a["w_in"].rearrange("l (k p) n -> p (l k) n", p=P)
    io.w_o_v = a["w_o"].rearrange("l (k p) n -> p (l k) n", p=P)
    io.w_group, io.w_expert = a["w_group"][0], a["w_expert"][0]
    io.b_group, io.b_expert = a["b_group"], a["b_expert"]
    io.w1_v = a["w1"][0].rearrange("e (k p) n -> p e k n", p=P)
    io.w3_v = a["w3"][0].rearrange("e (k p) n -> p e k n", p=P)
    io.w2_v = a["w2"][0].rearrange("e (k p) n -> p e k n", p=P)
    io.proj_qkv = io.proj[0:TILE_GQ].rearrange("(g e) p t -> p g e t", g=3)
    io.proj_gdn = io.proj[TILE_GQ:TILE_GZ].rearrange("(g e) p t -> p g e t", g=3)
    io.proj_z = io.proj[TILE_GZ:].rearrange("e p t -> p e t")


def build(nc, args, out):
    io = Core()
    io.proj = nc.dram_tensor("proj_scratch", (4 * N_GRP, P, T), F32, kind="Internal").ap()
    io.xn = nc.dram_tensor("xn_scratch", (T, D), F32, kind="Internal").ap()
    io.out = out.rearrange("b t d -> (b t) d")
    views(io, args)
    program(nc, io)


INPUTS = ["x", "norm1_w", "w_in", "sb_q_norm_w", "sb_k_norm_w", "gdn_conv_w", "gdn_a_log", "gdn_dt_bias",
          "gdn_out_norm_w", "w_o", "norm2_w", "w_group", "b_group", "w_expert", "b_expert", "w1", "w3", "w2"]


def kernel(**inputs):
    import numpy as np
    from concourse import bacc
    from concourse.bass_utils import run_bass_kernel_spmd

    nc = bacc.Bacc("TRN2", target_bir_lowering=False, num_devices=1)
    arrays, args = {}, {}
    for name in INPUTS:
        a = np.ascontiguousarray(inputs[name])
        arrays[f"in_{name}"] = a
        args[name] = nc.dram_tensor(f"in_{name}", a.shape, mybir.dt.from_np(a.dtype), kind="ExternalInput").ap()
    out = nc.dram_tensor("out_0", (1, T, D), F32, kind="ExternalOutput").ap()
    build(nc, args, out)
    result = run_bass_kernel_spmd(nc, [arrays], core_ids=[0])
    return result.results[0]["out_0"]
```
